# Optimizing a Trainium2 kernel written in Bass

```python
import jax, jax.numpy as jnp
from jax import lax
import numpy as np

D_MODEL = 1024
BATCH = 1
SEQ = 256
DEPTH = 2

GRID_W = 64
CTX_LEN = 256
N_HEADS = 8
N_KV_HEADS = 2
HEAD_DIM = 64
GROUP = N_HEADS // N_KV_HEADS
WINDOW = 128
BLOCK = 128
ROPE_BASE = 10000.0
ROPE_FREQS = HEAD_DIM // 4
CONF_W = 256
CONF_K = 31
SC_W = 256
SC_K = 3
FN_W = 256
FN_GROUPS = 4
FN_GROUP_W = FN_W // FN_GROUPS
N_BRANCH = 4
Q_W = N_HEADS * HEAD_DIM
KV_W = N_KV_HEADS * HEAD_DIM
IN_SIZES = (Q_W, KV_W, KV_W, 2 * CONF_W, SC_W, SC_W, SC_W, FN_W, N_BRANCH * D_MODEL)
IN_W = Q_W + 2 * KV_W + 2 * CONF_W + 3 * SC_W + FN_W + N_BRANCH * D_MODEL
D_FF = 2816
FFN_K = 3
EPS = 1e-6
NEG_INF = -1e30

kernel_name = "hybrid_parallel_mixer_dit_block"

def split_cols(p, sizes):
    idx = []
    acc = 0
    for n in sizes[:-1]:
        acc += n
        idx.append(acc)
    return jnp.split(p, idx, axis=-1)

def rms_norm(x, g):
    xf = x.astype(jnp.float32)
    y = xf * lax.rsqrt(jnp.mean(xf * xf, axis=-1, keepdims=True) + EPS)
    return (y * g.astype(jnp.float32)).astype(x.dtype)

def layer_norm(x, g, b):
    xf = x.astype(jnp.float32)
    mu = jnp.mean(xf, axis=-1, keepdims=True)
    xc = xf - mu
    var = jnp.mean(xc * xc, axis=-1, keepdims=True)
    y = xc * lax.rsqrt(var + EPS) * g.astype(jnp.float32) + b.astype(jnp.float32)
    return y.astype(x.dtype)

def adaln(cvec, w, b):
    m = jax.nn.silu(cvec) @ w + b
    return [t[..., None, :] for t in jnp.split(m, 6, axis=-1)]

def modulate(h, shift, scale):
    return h * (1 + scale) + shift

def dwconv(x, w, b=None):
    k, ch = w.shape
    pad = (k - 1) // 2
    y = lax.conv_general_dilated(
        x, w[:, None, :].astype(x.dtype), window_strides=(1,), padding=[(pad, pad)],
        dimension_numbers=("NWC", "WIO", "NWC"), feature_group_count=ch)
    if b is not None:
        y = y + b.astype(x.dtype)
    return y

def axial_rope_tables(n_tokens):
    rows = n_tokens // GRID_W
    r = jnp.repeat(jnp.arange(rows), GRID_W)
    col = jnp.tile(jnp.arange(GRID_W), rows)
    inv = ROPE_BASE ** (-jnp.arange(ROPE_FREQS, dtype=jnp.float32) / ROPE_FREQS)
    ang = jnp.stack([r, col], axis=-1).astype(jnp.float32)[:, :, None] * inv
    return jnp.cos(ang)[:, None, :, None, :], jnp.sin(ang)[:, None, :, None, :]

def apply_rope(x, cos, sin):
    b, s, h, _ = x.shape
    xs = x.astype(jnp.float32).reshape(b, s, h, 2, 2, ROPE_FREQS)
    rot = jnp.stack([-xs[..., 1, :], xs[..., 0, :]], axis=-2)
    return (xs * cos + rot * sin).reshape(b, s, h, HEAD_DIM).astype(x.dtype)

def attend_with_sink(q, k, v, sink, mask):
    s = jnp.einsum("bqhgd,bkhd->bhgqk", q, k, preferred_element_type=jnp.float32) * (HEAD_DIM ** -0.5)
    if mask is not None:
        s = jnp.where(mask, s, NEG_INF)
    sk = sink.astype(jnp.float32)[None, :, :, None, None]
    m = jnp.maximum(jnp.max(s, axis=-1, keepdims=True), sk)
    p = jnp.exp(s - m)
    denom = jnp.sum(p, axis=-1, keepdims=True) + jnp.exp(sk - m)
    return jnp.einsum("bhgqk,bkhd->bqhgd", (p / denom).astype(v.dtype), v)

def windowed_latent_attention(q, k, v, kc, vc, sink):
    b, s = q.shape[:2]
    nb = s // BLOCK
    band = BLOCK + 2 * WINDOW

    def bands(t):
        tp = jnp.pad(t, ((0, 0), (WINDOW, WINDOW), (0, 0), (0, 0)))
        tb = tp.reshape(b, nb + 2, BLOCK, N_KV_HEADS, HEAD_DIM)
        tb = jnp.concatenate([tb[:, :-2], tb[:, 1:-1], tb[:, 2:]], axis=2)
        return jnp.moveaxis(tb, 1, 0)

    qb = jnp.moveaxis(q.reshape(b, nb, BLOCK, N_KV_HEADS, GROUP, HEAD_DIM), 1, 0)
    rel = jnp.arange(band)[None, :] - WINDOW - jnp.arange(BLOCK)[:, None]
    in_win = jnp.abs(rel) <= WINDOW
    kpos = jnp.arange(nb)[:, None] * BLOCK - WINDOW + jnp.arange(band)[None, :]
    valid = in_win[None] & ((kpos >= 0) & (kpos < s))[:, None, :]
    ctx_ok = jnp.ones((BLOCK, kc.shape[1]), dtype=bool)

    def one_block(args):
        qi, ki, vi, mi = args
        kk = jnp.concatenate([ki, kc], axis=1)
        vv = jnp.concatenate([vi, vc], axis=1)
        mm = jnp.concatenate([mi, ctx_ok], axis=1)
        return attend_with_sink(qi, kk, vv, sink, mm)

    out = lax.map(one_block, (qb, bands(k), bands(v), valid))
    return jnp.moveaxis(out, 0, 1).reshape(b, s, Q_W)

def local_branches(p_conf, p_b, p_c, p_x, p_fn, conf_dw_w, conf_dw_b, conf_ln_g, conf_ln_b, sc_w):
    a, g = jnp.split(p_conf, 2, axis=-1)
    u = dwconv(a * jax.nn.sigmoid(g), conf_dw_w, conf_dw_b)
    y_conf = jax.nn.silu(layer_norm(u, conf_ln_g, conf_ln_b))
    y_sc = p_b * dwconv(p_c * p_x, sc_w)
    bsz, n = p_fn.shape[:2]
    f = p_fn.astype(jnp.float32).reshape(bsz, n, FN_GROUPS, FN_GROUP_W)
    y_fn = jnp.fft.fft2(f, axes=(1, 3), norm="ortho").real.astype(p_fn.dtype).reshape(bsz, n, FN_W)
    return y_conf, y_sc, y_fn

def merge_branches(ys, p_gate, w_brs, w_out):
    gates = jnp.split(jax.nn.sigmoid(p_gate), N_BRANCH, axis=-1)
    m = gates[0] * (ys[0] @ w_brs[0])
    for g, y, w in zip(gates[1:], ys[1:], w_brs[1:]):
        m = m + g * (y @ w)
    return m @ w_out

def mixer_output(p, y_attn, conf_dw_w, conf_dw_b, conf_ln_g, conf_ln_b, sc_w, w_brs, w_out):
    y_conf, y_sc, y_fn = local_branches(p[3], p[4], p[5], p[6], p[7],
                                        conf_dw_w, conf_dw_b, conf_ln_g, conf_ln_b, sc_w)
    return merge_branches((y_attn, y_conf, y_sc, y_fn), p[8], w_brs, w_out)

def conv_ffn(h, w_up, dw_w, dw_b, w_down):
    a, b = jnp.split(h @ w_up, 2, axis=-1)
    return (jax.nn.silu(dwconv(a, dw_w, dw_b)) * b) @ w_down

def setup_inputs(seed: int = 0) -> dict:
    key = jax.random.key(seed)
    ks = jax.random.split(key, 25)
    D = D_MODEL

    def nrm(k, shape, s):
        return jax.random.normal(k, shape, jnp.float32) * s

    return {
        "x": nrm(ks[0], (BATCH, SEQ, D), 1.0),
        "c": nrm(ks[1], (BATCH, D), 1.0),
        "ctx": nrm(ks[2], (BATCH, CTX_LEN, D), 1.0),
        "c_ctx": nrm(ks[3], (D,), 1.0),
        "w_ada": nrm(ks[4], (DEPTH, D, 6 * D), 0.5 * D ** -0.5),
        "b_ada": nrm(ks[5], (DEPTH, 6 * D), 0.02),
        "g_mix": 1.0 + nrm(ks[6], (DEPTH, D), 0.02),
        "w_in": nrm(ks[7], (DEPTH, D, IN_W), D ** -0.5),
        "attn_sink": nrm(ks[8], (DEPTH, N_HEADS), 1.0),
        "conf_dw_w": nrm(ks[9], (DEPTH, CONF_K, CONF_W), CONF_K ** -0.5),
        "conf_dw_b": nrm(ks[10], (DEPTH, CONF_W), 0.02),
        "conf_ln_g": 1.0 + nrm(ks[11], (DEPTH, CONF_W), 0.02),
        "conf_ln_b": nrm(ks[12], (DEPTH, CONF_W), 0.02),
        "sc_w": nrm(ks[13], (DEPTH, SC_K, SC_W), SC_K ** -0.5),
        "w_br_attn": nrm(ks[14], (DEPTH, Q_W, D), Q_W ** -0.5),
        "w_br_conf": nrm(ks[15], (DEPTH, CONF_W, D), CONF_W ** -0.5),
        "w_br_sconv": nrm(ks[16], (DEPTH, SC_W, D), SC_W ** -0.5),
        "w_br_fourier": nrm(ks[17], (DEPTH, FN_W, D), FN_W ** -0.5),
        "w_out": nrm(ks[18], (DEPTH, D, D), D ** -0.5),
        "g_ffn": 1.0 + nrm(ks[19], (DEPTH, D), 0.02),
        "w_up": nrm(ks[20], (DEPTH, D, 2 * D_FF), D ** -0.5),
        "ffn_dw_w": nrm(ks[21], (DEPTH, FFN_K, D_FF), FFN_K ** -0.5),
        "ffn_dw_b": nrm(ks[22], (DEPTH, D_FF), 0.02),
        "w_down": nrm(ks[23], (DEPTH, D_FF, D), D_FF ** -0.5),
        "g_final": 1.0 + nrm(ks[24], (D,), 0.02),
    }

def reference(x, c, ctx, c_ctx, w_ada, b_ada, g_mix, w_in, attn_sink, conf_dw_w, conf_dw_b,
              conf_ln_g, conf_ln_b, sc_w, w_br_attn, w_br_conf, w_br_sconv, w_br_fourier, w_out,
              g_ffn, w_up, ffn_dw_w, ffn_dw_b, w_down, g_final):
    b, s = x.shape[:2]
    lc = ctx.shape[1]
    cos, sin = axial_rope_tables(s)
    for l in range(DEPTH):
        last = l == DEPTH - 1
        sh1, sc1, gt1, sh2, sc2, gt2 = adaln(c, w_ada[l], b_ada[l])
        csh1, csc1, cgt1, csh2, csc2, cgt2 = adaln(c_ctx, w_ada[l], b_ada[l])
        sink = attn_sink[l].reshape(N_KV_HEADS, GROUP)
        w_brs = (w_br_attn[l], w_br_conf[l], w_br_sconv[l], w_br_fourier[l])

        hx = modulate(rms_norm(x, g_mix[l]), sh1, sc1)
        hc = modulate(rms_norm(ctx, g_mix[l]), csh1, csc1)
        px = split_cols(hx @ w_in[l], IN_SIZES)
        q = apply_rope(px[0].reshape(b, s, N_HEADS, HEAD_DIM), cos, sin)
        k = apply_rope(px[1].reshape(b, s, N_KV_HEADS, HEAD_DIM), cos, sin)
        v = px[2].reshape(b, s, N_KV_HEADS, HEAD_DIM)
        if last:
            kc, vc = jnp.split(hc @ w_in[l][:, Q_W:Q_W + 2 * KV_W], 2, axis=-1)
        else:
            pc = split_cols(hc @ w_in[l], IN_SIZES)
            kc, vc = pc[1], pc[2]
        kc = kc.reshape(b, lc, N_KV_HEADS, HEAD_DIM)
        vc = vc.reshape(b, lc, N_KV_HEADS, HEAD_DIM)

        y_attn = windowed_latent_attention(q, k, v, kc, vc, sink)
        x = x + gt1 * mixer_output(px, y_attn, conf_dw_w[l], conf_dw_b[l], conf_ln_g[l],
                                   conf_ln_b[l], sc_w[l], w_brs, w_out[l])
        if not last:
            qc = pc[0].reshape(b, lc, N_KV_HEADS, GROUP, HEAD_DIM)
            yc_attn = attend_with_sink(qc, kc, vc, sink, None).reshape(b, lc, Q_W)
            ctx = ctx + cgt1 * mixer_output(pc, yc_attn, conf_dw_w[l], conf_dw_b[l], conf_ln_g[l],
                                            conf_ln_b[l], sc_w[l], w_brs, w_out[l])

        x = x + gt2 * conv_ffn(modulate(rms_norm(x, g_ffn[l]), sh2, sc2),
                               w_up[l], ffn_dw_w[l], ffn_dw_b[l], w_down[l])
        if not last:
            ctx = ctx + cgt2 * conv_ffn(modulate(rms_norm(ctx, g_ffn[l]), csh2, csc2),
                                        w_up[l], ffn_dw_w[l], ffn_dw_b[l], w_down[l])
    return rms_norm(x, g_final)


_drawn_inputs = setup_inputs


def setup_inputs(seed=0):
    import zlib

    import numpy as np

    out = dict(_drawn_inputs(seed))
    spreads = {}
    factors = {'ctx': 3.307,
     'g_mix': 4.827,
     'attn_sink': 8.0,
     'conf_dw_b': 64.0,
     'conf_ln_g': 200.0,
     'conf_ln_b': 200.0,
     'g_ffn': 20.199,
     'ffn_dw_b': 29.533,
     'g_final': 23.077}
    for name, (base, spread) in spreads.items():
        noise = np.random.default_rng([zlib.crc32(name.encode()), seed]).standard_normal(out[name].shape)
        drawn = base * np.exp(spread * noise) if base else spread * noise
        out[name] = __import__('jax').numpy.asarray(drawn.astype(out[name].dtype))
    for name, factor in factors.items():
        out[name] = (out[name] * factor).astype(out[name].dtype)
    return out
```

```python
from contextlib import ExitStack

import concourse.bass as bass
from concourse import mybir

F32 = mybir.dt.float32
F32R = mybir.dt.float32r
ALU = mybir.AluOpType
ACT = mybir.ActivationFunctionType
AX = mybir.AxisListType

P = 128
D = 1024
DEPTH = 2
SEQ = 256
CTX = 256
KD = D // P
N_HEADS = 8
HEAD = 64
Q_W, KV_W = 512, 128
CONF_W, CONF_K = 256, 31
SC_W, SC_K = 256, 3
FN_W = 256
D_FF = 2816
HALF_FF = D_FF // 2 // P
EPS = 1e-6
NT = SEQ + CTX
PAD = (CONF_K - 1) // 2
SLOTS = 4
AHEAD = 3
TAPS = 2 * CONF_K
ADA_A, ADA_B = 16, 32
ADA_L = ADA_A + ADA_B

PHASES = [("in", 18, 8), ("fn", 8, 10), ("sc", 8, 10), ("at", 12, 8), ("cf", 8, 10), ("out", 8, 8),
          ("up0", 22, 8), ("dn0", 8, HALF_FF), ("up1", 22, 8), ("dn1", 8, HALF_FF)]
START, SIZE, LEN = {}, [], {}
for _name, _count, _tiles in PHASES:
    START[_name] = len(SIZE)
    LEN[_name] = _count
    SIZE += [_tiles] * _count
PER_LAYER = len(SIZE)
TOTAL = DEPTH * PER_LAYER

VEC, _at = {}, 0
for _name, _n in [("cc", 2 * KD), ("b_ada", DEPTH * ADA_L), ("g_mix", DEPTH * KD), ("g_ffn", DEPTH * KD),
                  ("g_final", KD), ("sink", DEPTH * N_HEADS), ("conf_w", DEPTH * TAPS), ("conf_b", DEPTH * 2),
                  ("ln_g", DEPTH * 2), ("ln_b", DEPTH * 2), ("sc_w", DEPTH * 2 * SC_K),
                  ("ffn_w", DEPTH * 2 * HALF_FF * 3), ("ffn_b", DEPTH * 2 * HALF_FF), ("eps", 1)]:
    VEC[_name] = _at
    _at += _n
NVEC = _at
MAT, _at = {}, 0
for _name, _n in [("ident", 128), ("mean", 128), ("rot", 128), ("mask0", 128), ("mask1", 128),
                  ("chan", 256), ("pos", 1024), ("cos", 256), ("sin", 256)]:
    MAT[_name] = _at
    _at += _n
NMAT = _at


class Step:

    def __init__(self, n, idx, i=None):
        self.n, self.idx, self.i = n, idx, i
        self.slot = n % SLOTS

    def up(self, base, per=4):
        return base if self.i is None else base + per * self.i

    def turn(self, ahead=0):
        return self.up((self.n + ahead) // SLOTS + 1, 1)


def walk(eng, layer, name, step, keep=0):
    first, count = layer * PER_LAYER + START[name], LEN[name]
    groups = (count - keep) // SLOTS
    if groups >= 2:
        with eng.Fori(0, groups) as i:
            for j in range(SLOTS):
                step(Step(first + j, j, i))
    else:
        groups = 0
    for idx in range(groups * SLOTS, count):
        step(Step(first + idx, idx))


def program(nc, io):
    ctx = ExitStack()
    with ctx:
        base = -(-nc.sbuf_base // 32) * 32
        top = [base]

        def at(name, shape, dt, offset):
            return nc.alloc_sbuf_tensor_at(name, [P] + shape, dt, offset=offset)

        def place(name, shape, dt=F32):
            size = 4
            for s in shape:
                size *= s
            offset = top[0]
            top[0] += -(-size // 32) * 32
            return at(name, shape, dt, offset)

        SLOT = HALF_FF * P
        raw = place("raw", [SLOTS, SLOT])
        w_hi = place("w_hi", [SLOTS, SLOT], F32R)
        w_lo = place("w_lo", [SLOTS, SLOT], F32R)
        ada_raw = place("ada_raw", [2, KD * P])
        X = place("X", [KD, NT])
        h_off = top[0]
        h_hi = place("h_hi", [KD, NT], F32R)
        h_lo = place("h_lo", [KD, NT], F32R)
        y_off = top[0]
        y_hi = place("y_hi", [8, NT], F32R)
        y_lo = place("y_lo", [8, NT], F32R)
        yc_hi = place("yc_hi", [2, NT], F32R)
        yc_lo = place("yc_lo", [2, NT], F32R)
        q_off = top[0]
        q = place("q", [4, NT])
        k = place("k", [NT])
        v = place("v", [NT // P, KV_W])
        glu = place("glu", [2, 2, SEQ + 2 * PAD])
        acc = place("acc", [2, NT])
        t_off = top[0]
        prob = place("prob", [2, NT])
        probT = place("probT", [2, NT])
        sqb = place("sqb", [NT])
        sqa = place("sqa", [NT])
        mat = place("mat", [NMAT])
        vec = place("vec", [NVEC])
        csil = place("csil", [KD, 2])
        mod = place("mod", [2, ADA_L, 2])
        gsc = place("gsc", [2, 2, KD])
        nsink = place("nsink", [DEPTH * N_HEADS])
        small = place("small", [2, 6])
        assert top[0] <= nc.sbuf_usable_end, (top[0], nc.sbuf_usable_end)
        mg_hi = at("mg_hi", [KD, NT], F32R, y_off)
        mg_lo = at("mg_lo", [KD, NT], F32R, y_off + 4 * KD * NT)
        assert y_off + 4 * NT * 2 * HALF_FF <= t_off
        hid_hi = at("hid_hi", [HALF_FF, NT], F32R, y_off)
        hid_lo = at("hid_lo", [HALF_FF, NT], F32R, y_off + 4 * HALF_FF * NT)
        x_in = at("x_in", [KD, NT], F32, q_off)
        ya_off = y_off + 4 * 4 * NT
        cx = at("cx", [2, 2, SEQ + 2], F32, ya_off)
        pb = at("pb", [2, NT], F32, y_off + 4 * 8 * NT + 4 * 4 * NT)
        pc = at("pc", [2, NT], F32, y_off + 4 * 8 * NT + 4 * 6 * NT)
        assert 4 * 2 * 2 * (SEQ + 2) <= 4 * 4 * NT
        tmp = [at(f"tmp{b}", [NT], F32, t_off + 4 * NT * b) for b in range(2)]
        sig = [at(f"sig{b}", [NT], F32, t_off + 4 * NT * (2 + b)) for b in range(2)]
        y_out = at("y_out", [KD, SEQ], F32, h_off)

        psA = [ctx.enter_context(nc.psum_tensor(f"psA{b}", [P, 512], F32)) for b in range(4)]
        psB = [ctx.enter_context(nc.psum_tensor(f"psB{b}", [P, 512], F32)) for b in range(4)]

        def sem(name):
            return ctx.enter_context(nc.semaphore(name))

        raw_full = [sem(f"raw_full{s}") for s in range(SLOTS)]
        ada_full = [sem(f"ada_full{s}") for s in range(2)]
        mats_in, vecs_in, x_full, x_again, stored = map(sem, ("mats_in", "vecs_in", "x_full", "x_again", "stored"))
        head_done, rest_done = sem("head_done"), sem("rest_done")
        chunk_done, ada_done = sem("chunk_done"), sem("ada_done")
        evac = sem("evac")
        csil_done, nsink_done, mod_done, gsc_done = map(sem, ("csil_done", "nsink_done", "mod_done", "gsc_done"))
        sq_done, sq_sum, stat, root, inv, ht, h_head, h_rest = map(sem, (
            "sq_done", "sq_sum", "stat", "root", "inv", "ht", "h_head", "h_rest"))
        pads, rot, rope, fc_mm, fc, fn_mm, fn_head, fn_rest = map(sem, (
            "pads", "rot", "rope", "fc_mm", "fc", "fn_mm", "fn_head", "fn_rest"))
        sc_step, sc_head, sc_rest, sigd = map(sem, ("sc_step", "sc_head", "sc_rest", "sigd"))
        s_mm, negm, expd, den, pn, t_mm, pt, o_mm, o_head, o_rest = map(sem, (
            "s_mm", "negm", "expd", "den", "pn", "t_mm", "pt", "o_mm", "o_head", "o_rest"))
        tap, ln_mean, ln_xc, ln_sq, ln_var, ln_root, ln_inv, ln_n, ln_silu, ln_head, ln_rest = map(sem, (
            "tap", "ln_mean", "ln_xc", "ln_sq", "ln_var", "ln_root", "ln_inv", "ln_n", "ln_silu", "ln_head",
            "ln_rest"))
        prod, m_sum, m_head, m_rest = map(sem, ("prod", "m_sum", "m_head", "m_rest"))
        cv, silu, hid_head, hid_rest, x_part, fin = map(sem, ("cv", "silu", "hid_head", "hid_rest", "x_part", "fin"))

        def M(name, n=128, off=0):
            return mat[:, MAT[name] + off:MAT[name] + off + n]

        def V(name, i):
            return vec[:, VEC[name] + i:VEC[name] + i + 1]

        def Vd(name, i):
            return vec[:, bass.ds(VEC[name] + i, 1)]

        def streams(layer):
            return 2 if layer == 0 else 1

        def both(ap, T):
            return ap.rearrange("p (s t) -> p s t", s=T // SEQ)

        def branch_sum(layer, o):
            return X[:, o, 0:NT] if layer == 0 else X[:, o, SEQ:NT]

        def f_in(layer, c):
            return X[:, c, 0:NT] if layer == 0 else X[:, c, SEQ:NT]

        def f_mid(layer, tb):
            if layer == 0:
                return X[:, 2 + tb, :].rearrange("p (c n) -> p c n", c=2)
            return X[:, 2 + 2 * tb:4 + 2 * tb, SEQ:NT]

        def units(layer):
            return [(s, qi, t, half) for s in range(streams(layer)) for qi in range(2) for t in range(4)
                    for half in range(2)]

        NU = [len(units(0)), len(units(1))]
        U0 = [0, NU[0]]

        block = ctx.enter_context(nc.Block())

        @block.sync
        def _(sp):
            sp.dma_start(vec[:, :], io["vec"]).then_inc(vecs_in, 16)
            for kk in range(4):
                sp.dma_start(X[:, 2 * kk:2 * kk + 2, :], io["x"][:, 2 * kk:2 * kk + 2, :]).then_inc(x_full, 16)
            sp.dma_start(mat[:, :], io["mat"]).then_inc(mats_in, 16)

            for layer in range(DEPTH):
                for name, _, tiles in PHASES:
                    src = io[f"w_{name}{layer}"]

                    def load(st):
                        if st.n >= SLOTS:
                            sp.wait_ge(rest_done, st.up(st.n - SLOTS + 1))
                        dst = raw[:, st.slot, 0:tiles * P]
                        if st.i is None:
                            sp.dma_start(dst, src[st.idx]).then_inc(raw_full[st.slot], 16)
                        else:
                            sp.dma_start(dst, src[bass.ds(st.up(st.idx), 1)].rearrange("a p n -> p (a n)"))\
                                .then_inc(raw_full[st.slot], 16)
                    if layer == 0 and name == "in":
                        for idx in range(LEN[name]):
                            load(Step(idx, idx))
                    else:
                        walk(sp, layer, name, load)
                    if layer == 0 and name == "cf":
                        sp.wait_ge(chunk_done, START["fn"] + 1)
                        sp.wait_ge(tap, TAPS)
                        sp.dma_start(x_in[:, :, :], io["x"]).then_inc(x_again, 16)
            for kk in range(KD):
                sp.wait_ge(fin, kk + 1)
                sp.dma_start(io["out"][:, kk, :], y_out[:, kk, :]).then_inc(stored, 16)
            sp.wait_ge(stored, 16 * KD)

        @block.gpsimd
        def _(pool):
            def load_ada(a):
                if a >= 2:
                    pool.wait_ge(ada_done, a - 1)
                pool.dma_start(ada_raw[:, a % 2, :], io["w_ada"][a]).then_inc(ada_full[a % 2], 16)
            pool.memset(glu[:, :, :, :], 0.0).then_inc(pads, 1)
            pool.memset(cx[:, :, :, :], 0.0).then_inc(pads, 1)
            for a in range(2):
                load_ada(a)
            with pool.Fori(0, DEPTH * ADA_L // 2 - 1) as i:
                for b in range(2):
                    pool.wait_ge(ada_done, 2 * i + b + 1)
                    pool.dma_start(ada_raw[:, b, :], io["w_ada"][bass.ds(2 * i + (2 + b), 1)]
                                   .rearrange("a p n -> p (a n)")).then_inc(ada_full[b], 16)

        @block.tensor
        def _(pe):
            def product(out, st, tile, hi, lo, first, last):
                w0 = w_hi[:, st.slot, tile * P:(tile + 1) * P]
                w1 = w_lo[:, st.slot, tile * P:(tile + 1) * P]
                pe.matmul(out, w0, hi, start=first, stop=False)
                pe.matmul(out, w0, lo, start=False, stop=False)
                return pe.matmul(out, w1, hi, start=False, stop=last)

            def begin(st):
                pe.wait_ge(rest_done, st.up(st.n + 1))
                if st.n >= SLOTS:
                    pe.wait_ge(evac, st.up(st.n - SLOTS + 1))

            def from_h(st, T, out, waits=None):
                for kk in range(KD):
                    if waits is not None:
                        pe.wait_ge(h_rest, waits + kk + 1)
                    mm = product(out, st, kk, h_hi[:, kk, 0:T], h_lo[:, kk, 0:T], kk == 0, kk == KD - 1)
                return mm

            def ada(a, i=None):
                pe.wait_ge(ada_full[a % 2], 16 * (a // 2 + 1) + (0 if i is None else 32 * i))
                col = a % ADA_L
                col = 2 * (col if col < ADA_A else col - ADA_A)
                for kk in range(KD):
                    out = psB[3][:, col:col + 2] if i is None else psB[3][:, bass.ds(col + 8 * i, 2)]
                    mm = pe.matmul(out, ada_raw[:, a % 2, kk * P:(kk + 1) * P],
                                   csil[:, kk, :], start=(kk == 0), stop=(kk == KD - 1))
                mm.then_inc(ada_done, 1)

            def norm_stat(layer, which, T):
                pe.wait_ge(sq_sum, 7 * (2 * layer + which + 1))
                pe.matmul(psB[0][:, 0:T], M("mean"), sqa[:, 0:T], start=True, stop=True).then_inc(stat, 1)

            pe.wait_ge(csil_done, 1)
            pe.wait_ge(mats_in, 16)
            norm_stat(0, 0, NT)
            for a in range(ADA_A):
                ada(a)

            for layer in range(DEPTH):
                n0 = layer * PER_LAYER
                T = SEQ * streams(layer)
                if layer:
                    norm_stat(layer, 0, NT)
                for idx in range(LEN["in"]):
                    st = Step(n0 + idx, idx)
                    begin(st)
                    waits = 8 * 2 * layer if idx == 0 else None
                    if idx == 5:
                        for tb in range(NT // P):
                            for kk in range(KD):
                                tok = slice(tb * P, (tb + 1) * P)
                                wt = slice(kk * P, (kk + 1) * P)
                                out = psA[st.slot][:, tb * P:(tb + 1) * P]
                                pe.matmul(out, h_hi[:, kk, tok], w_hi[:, st.slot, wt], start=(kk == 0), stop=False)
                                pe.matmul(out, h_hi[:, kk, tok], w_lo[:, st.slot, wt], start=False, stop=False)
                                mm = pe.matmul(out, h_lo[:, kk, tok], w_hi[:, st.slot, wt], start=False,
                                               stop=(kk == KD - 1))
                    else:
                        cols = NT if idx == 4 else T
                        mm = from_h(st, cols, psA[st.slot][:, 0:cols], waits)
                    mm.then_inc(chunk_done, 1)
                for j in range(5):
                    pe.wait_ge(evac, n0 + j + 1)
                    if j >= 2:
                        pe.wait_ge(rope, 15 * layer + 3 * (j - 2) + 1)
                    else:
                        pe.wait_ge(evac, n0 + 5)
                    src = q[:, j, 0:SEQ] if j < 4 else k[:, 0:SEQ]
                    pe.matmul(psB[j % 2][:, 0:SEQ], M("rot"), src, start=True, stop=True).then_inc(rot, 1)
                pe.wait_ge(evac, n0 + LEN["in"])
                for tb in range(T // P):
                    for c in range(2):
                        mm = pe.matmul(psA[tb][:, c * 256:(c + 1) * 256], f_in(layer, c)[:, tb * P:(tb + 1) * P],
                                       M("chan", 256), start=True, stop=True)
                    mm.then_inc(fc_mm, 1)
                fc0 = 4 * layer
                pe.wait_ge(fc, fc0 + T // P)
                for s in range(streams(layer)):
                    for c in range(2):
                        out = psA[2 * s + c][:, 0:SEQ]
                        for h in range(2):
                            mid = f_mid(layer, 2 * s + h)
                            for part in range(2):
                                mm = pe.matmul(out, mid[:, c, part * P:(part + 1) * P],
                                               M("pos", SEQ, 512 * h + 256 * part),
                                               start=(h == 0 and part == 0), stop=(h == 1 and part == 1))
                        mm.then_inc(fn_mm, 1)

                un, u0 = units(layer), U0[layer]
                per = ADA_B // len(un)
                pe.wait_ge(rope, 15 * (layer + 1))
                pe.wait_ge(fn_rest, fc0 + 2 * streams(layer))
                for j in range(len(un) + 2):
                    if j < len(un):
                        s, qi, t, half = un[j]
                        k0, nk = (0, 4) if s == 0 else (2, 2)
                        ps = psA[j % 2]
                        if j >= 2:
                            pe.wait_ge(expd, 2 * (u0 + j - 1))
                        rows = slice(64 * half, 64 * half + 64)
                        q0 = SEQ * s + P * qi
                        mm = pe.matmul(ps[:, 0:nk * P], q[rows, t, q0:q0 + P], k[rows, k0 * P:(k0 + nk) * P],
                                       start=True, stop=True)
                        if s == 0:
                            mm = pe.matmul(ps[:, (1 - qi) * P:(2 - qi) * P], M("ident"), M(f"mask{qi}"),
                                           start=False, stop=True, skip_group_check=True)
                        mm.then_inc(s_mm, 1)
                    if j >= 2:
                        s, qi, t, half = un[j - 2]
                        k0, nk = (0, 4) if s == 0 else (2, 2)
                        pair = (j - 2) // 2
                        pe.wait_ge(pt, u0 + j - 1)
                        if half == 0 and pair >= 2:
                            pe.wait_ge(o_rest, u0 // 2 + pair - 1)
                        for b in range(nk):
                            mm = pe.matmul(psB[pair % 2][64 * half:64 * half + 64, 0:P],
                                           v[:, k0 + b, 64 * half:64 * half + 64],
                                           probT[:, j % 2, b * P:(b + 1) * P], start=(b == 0), stop=(b == nk - 1))
                        mm.then_inc(o_mm, 1)
                    if j < len(un):
                        for a in range(per):
                            ada(layer * ADA_L + ADA_A + per * j + a)
                    if 1 <= j <= len(un):
                        s = un[j - 1][0]
                        nk = 4 if s == 0 else 2
                        pe.wait_ge(pn, u0 + j)
                        if j >= 3:
                            pe.wait_ge(pt, u0 + j - 2)
                        for b in range(nk):
                            mm = pe.transpose(psA[2 + (j - 1) % 2][:, b * P:(b + 1) * P],
                                              prob[:, (j - 1) % 2, b * P:(b + 1) * P], M("ident"))
                        mm.then_inc(t_mm, 1)

                pe.wait_ge(mod_done, 4 * layer + 4)
                pe.wait_ge(o_rest, (u0 + len(un)) // 2)

                def merge(st, hi, lo, tiles, wait):
                    begin(st)
                    from_h(st, T, psA[st.slot][:, 0:T])
                    if wait is not None:
                        pe.wait_ge(*wait)
                    for c in range(tiles):
                        mm = product(psB[st.slot][:, 0:T], st, KD + c, hi[:, c, 0:T], lo[:, c, 0:T],
                                     c == 0, c == tiles - 1)
                    mm.then_inc(chunk_done, 1)

                walk(pe, layer, "fn", lambda st: merge(st, y_hi[:, 0:2, :], y_lo[:, 0:2, :], 2, None))
                walk(pe, layer, "sc", lambda st: merge(st, y_hi[:, 2:4, :], y_lo[:, 2:4, :], 2,
                                                       (sc_rest, 2 * layer + 2)))
                m0 = n0 + START["at"]
                pe.wait_ge(evac, m0 - 3)
                pe.wait_ge(tap, TAPS * (layer + 1))
                for c in range(2):
                    mm = pe.matmul(psB[m0 % 4][:, 0:T], M("mean"), acc[:, c, 0:T], start=(c == 0), stop=(c == 1))
                mm.then_inc(ln_mean, 1)
                for idx in range(LEN["at"]):
                    st = Step(m0 + idx, idx)
                    begin(st)
                    if idx % 3 < 2:
                        mm = from_h(st, T, psA[st.slot][:, 0:T])
                    else:
                        if idx == 8:
                            pe.wait_ge(ln_xc, 2 * layer + 2)
                        if idx == 11:
                            pe.wait_ge(ln_root, layer + 1)
                        for half, ps in enumerate((psA, psB)):
                            for c in range(4):
                                mm = product(ps[st.slot][:, 0:T], st, 4 * half + c, y_hi[:, 4 + c, 0:T],
                                             y_lo[:, 4 + c, 0:T], c == 0, c == 3)
                    mm.then_inc(chunk_done, 1)
                    if idx == 6:
                        pe.wait_ge(ln_sq, 2 * layer + 2)
                        pe.wait_ge(evac, m0)
                        for c, sq in enumerate((sqb, sqa)):
                            mm = pe.matmul(psB[(m0 + 3) % 4][:, 0:T], M("mean"), sq[:, 0:T],
                                           start=(c == 0), stop=(c == 1))
                        mm.then_inc(ln_var, 1)
                walk(pe, layer, "cf", lambda st: merge(st, yc_hi, yc_lo, 2, (ln_rest, 2 * layer + 2)))

                def project(st):
                    begin(st)
                    for kk in range(KD):
                        if st.i is None and st.idx == 0:
                            pe.wait_ge(m_rest, 8 * layer + kk + 1)
                        mm = product(psA[st.slot][:, 0:T], st, kk, mg_hi[:, kk, 0:T], mg_lo[:, kk, 0:T],
                                     kk == 0, kk == KD - 1)
                    mm.then_inc(chunk_done, 1)
                pe.wait_ge(m_rest, 8 * layer + 8)
                walk(pe, layer, "out", project)
                norm_stat(layer, 1, T)

                for f in range(2):
                    if f == 0:
                        pe.wait_ge(h_rest, 8 * (2 * layer + 2))

                    def lift(st):
                        begin(st)
                        from_h(st, T, psA[st.slot][:, 0:T]).then_inc(chunk_done, 1)
                    walk(pe, layer, f"up{f}", lift)

                    def lower(st):
                        begin(st)
                        for c in range(HALF_FF):
                            mm = product(psA[st.slot][:, 0:T], st, c, hid_hi[:, c, 0:T], hid_lo[:, c, 0:T],
                                         c == 0, c == HALF_FF - 1)
                        mm.then_inc(chunk_done, 1)
                        if layer == 0:
                            ada(ADA_L + 8 * f + st.idx, st.i and 2 * st.i)
                    pe.wait_ge(hid_rest, HALF_FF * (2 * layer + f + 1))
                    if layer == 0:
                        for idx in range(LEN[f"dn{f}"]):
                            lower(Step(n0 + START[f"dn{f}"] + idx, idx))
                    else:
                        walk(pe, layer, f"dn{f}", lower)
            pe.wait_ge(sq_sum, 7 * (2 * DEPTH + 1))
            pe.matmul(psB[0][:, 0:SEQ], M("mean"), sqa[:, 0:SEQ], start=True, stop=True).then_inc(stat, 1)

        @block.scalar
        def _(act):
            def head(st, tiles):
                if st.i is None and st.n + AHEAD >= TOTAL:
                    return
                act.wait_ge(raw_full[(st.n + AHEAD) % SLOTS], 16 * st.turn(AHEAD))
                if st.n >= 1:
                    act.wait_ge(chunk_done, st.up(st.n))
                s = (st.n + AHEAD) % SLOTS
                act.activation(w_hi[:, s, 0:tiles * P], raw[:, s, 0:tiles * P], ACT.Copy).then_inc(head_done, 1)

            def size(st, layer, name):
                return SIZE[START[name]] if st.i is not None else SIZE[(st.n + AHEAD) % PER_LAYER]

            def square(count, o, T, direct, before):
                if before is not None:
                    act.wait_ge(*before)
                if count % 8 >= 2:
                    act.wait_ge(sq_sum, 7 * (count // 8) + count % 8 - 1)
                src = X[:, o, 0:T] if isinstance(o, int) else X[:, bass.ds(o, 1), 0:T].rearrange("p a t -> p (a t)")
                act.activation((sqa if direct else sqb)[:, 0:T], src, ACT.Square).then_inc(sq_done, 1)

            def norm(layer, which, T):
                r = 2 * layer + which
                act.wait_ge(stat, r + 1)
                act.wait_ge(sq_sum, 7 * (r + 1))
                act.activation(sqb[:, 0:T], psB[0][:, 0:T], ACT.Sqrt, bias=V("eps", 0)).then_inc(root, 1)
                for kk in range(KD):
                    act.wait_ge(ht, 8 * r + kk + 1)
                    for s in range(T // SEQ):
                        cols = slice(s * SEQ, (s + 1) * SEQ)
                        op = act.activation(h_hi[:, kk, cols], tmp[kk % 2][:, cols], ACT.Identity,
                                            bias=mod[:, layer, 24 * which + kk, s:s + 1])
                    op.then_inc(h_head, 1)

            act.wait_ge(vecs_in, 16)
            act.activation(csil[:, :, :].rearrange("p k c -> p (k c)"), vec[:, VEC["cc"]:VEC["cc"] + 2 * KD],
                           ACT.Silu).then_inc(csil_done, 1)
            act.wait_ge(x_full, 64)
            for kk in range(KD):
                square(kk, kk, NT, kk == 0, None)
            for ahead in range(AHEAD):
                head(Step(ahead - AHEAD, 0), 8)

            for layer in range(DEPTH):
                n0 = layer * PER_LAYER
                T = SEQ * streams(layer)
                norm(layer, 0, NT)
                for idx in range(LEN["in"]):
                    st = Step(n0 + idx, idx)
                    head(st, size(st, layer, "in"))
                    if idx in (14, 16):
                        act.wait_ge(chunk_done, st.n + 1)
                        act.activation(sig[(idx - 14) // 2][:, 0:T], psA[st.slot][:, 0:T], ACT.Sigmoid)\
                            .then_inc(sigd, 1)
                fc0 = 4 * layer
                for tb in range(T // P):
                    act.wait_ge(fc_mm, fc0 + tb + 1)
                    act.activation(f_mid(layer, tb), psA[tb][:, :].rearrange("p (c n) -> p c n", c=2), ACT.Copy)\
                        .then_inc(fc, 1)
                for j in range(2 * streams(layer)):
                    s, c = divmod(j, 2)
                    act.wait_ge(fn_mm, fc0 + j + 1)
                    act.activation(y_hi[:, c, s * SEQ:(s + 1) * SEQ], psA[j][:, 0:SEQ], ACT.Copy)\
                        .then_inc(fn_head, 1)
                for c in range(2):
                    act.wait_ge(sc_step, 8 * layer + 7 + c)
                    act.activation(y_hi[:, 2 + c, 0:T], pc[:, c, 0:T], ACT.Copy).then_inc(sc_head, 1)

                un, u0 = units(layer), U0[layer]
                act.wait_ge(nsink_done, 1)
                for j in range(len(un) + 3):
                    if j < len(un):
                        s, qi, t, half = un[j]
                        width = (4 if s == 0 else 2) * P
                        h = layer * N_HEADS + t + 4 * half
                        act.wait_ge(negm, 2 * (u0 + j + 1))
                        if j >= 2:
                            act.wait_ge(t_mm, u0 + j - 1)
                        act.activation(prob[:, j % 2, 0:width], psA[j % 2][:, 0:width], ACT.Exp,
                                       bias=small[:, j % 2, 1:2], scale=HEAD ** -0.5,
                                       accum_out=small[:, j % 2, 2:3]).then_inc(expd, 1)
                        act.activation(small[:, j % 2, 3:4], nsink[:, h:h + 1], ACT.Exp,
                                       bias=small[:, j % 2, 1:2], scale=-1.0).then_inc(expd, 1)
                    if 1 <= j <= len(un):
                        width = (4 if un[j - 1][0] == 0 else 2) * P
                        act.wait_ge(t_mm, u0 + j)
                        if j >= 3:
                            act.wait_ge(o_mm, u0 + j - 2)
                        act.activation(probT[:, (j - 1) % 2, 0:width], psA[2 + (j - 1) % 2][:, 0:width], ACT.Copy)\
                            .then_inc(pt, 1)
                    if j >= 3 and j % 2 == 1:
                        pair = (j - 3) // 2
                        s, qi, t, _ = un[2 * pair]
                        c0 = SEQ * s + P * qi
                        act.wait_ge(o_mm, u0 + 2 * pair + 2)
                        if pair == 0:
                            act.wait_ge(sc_rest, 2 * layer + 2)
                        act.activation(y_hi[:, 4 + t, c0:c0 + P], psB[pair % 2][:, 0:P], ACT.Copy)\
                            .then_inc(o_head, 1)

                s0 = 34 * layer + 2

                def gate(name, b):
                    def step(st):
                        head(st, size(st, layer, name))
                        act.wait_ge(chunk_done, st.up(st.n + 1))
                        act.wait_ge(evac, st.up(st.n - (st.idx > 0)))
                        act.activation(sig[st.n % 2][:, 0:T], psA[st.slot][:, 0:T], ACT.Sigmoid).then_inc(sigd, 1)
                        if name == "cf" and st.i is None and st.idx > 0:
                            merged_head(st.idx - 1)
                    return step

                def merged_head(o):
                    act.wait_ge(m_sum, 24 * layer + 16 + o + 1)
                    act.activation(mg_hi[:, o, 0:T], branch_sum(layer, o), ACT.Copy).then_inc(m_head, 1)

                walk(act, layer, "fn", gate("fn", 0), keep=AHEAD)
                walk(act, layer, "sc", gate("sc", 1), keep=AHEAD)
                m0 = n0 + START["at"]
                for idx in range(LEN["at"]):
                    st = Step(m0 + idx, idx)
                    head(st, size(st, layer, "at"))
                    if idx % 3 < 2:
                        o = idx // 3 * 2 + idx % 3
                        act.wait_ge(chunk_done, st.n + 1)
                        act.wait_ge(evac, m0 if o < 2 else m0 + o // 2 * 3)
                        act.activation(sig[o % 2][:, 0:T], psA[st.slot][:, 0:T], ACT.Sigmoid).then_inc(sigd, 1)
                    if idx == 2:
                        for c, sq in enumerate((sqb, sqa)):
                            act.wait_ge(ln_xc, 2 * layer + c + 1)
                            act.activation(sq[:, 0:T], acc[:, c, 0:T], ACT.Square).then_inc(ln_sq, 1)
                    if idx == 7:
                        act.wait_ge(ln_var, layer + 1)
                        act.activation(sqb[:, 0:T], psB[(m0 + 3) % 4][:, 0:T], ACT.Sqrt, bias=V("eps", 0),
                                       scale=float(D // CONF_W)).then_inc(ln_root, 1)
                    if idx == 9:
                        for c in range(2):
                            act.wait_ge(ln_n, 2 * layer + c + 1)
                            act.activation(acc[:, c, 0:T], acc[:, c, 0:T], ACT.Silu, bias=V("ln_b", 2 * layer + c),
                                           scale=V("ln_g", 2 * layer + c)).then_inc(ln_silu, 1)
                        for c in range(2):
                            act.wait_ge(ln_silu, 2 * layer + c + 1)
                            act.activation(yc_hi[:, c, 0:T], acc[:, c, 0:T], ACT.Copy).then_inc(ln_head, 1)
                for idx in range(LEN["cf"]):
                    gate("cf", 3)(Step(n0 + START["cf"] + idx, idx))
                merged_head(KD - 1)

                def squares(name, r):
                    def step(st):
                        head(st, size(st, layer, name))
                        o = st.up(st.idx)
                        square(8 * r + st.idx, o, T, st.idx == 0, (evac, st.up(st.n + 1)))
                    return step
                for idx in range(LEN["out"]):
                    squares("out", 2 * layer + 1)(Step(n0 + START["out"] + idx, idx))
                norm(layer, 1, T)

                for f in range(2):
                    p0 = HALF_FF * (2 * layer + f)

                    def lift(st):
                        head(st, size(st, layer, f"up{f}"))
                        pair = st.up(st.idx // 2, 2)
                        b = (st.idx // 2) % 2
                        if st.idx % 2 == 0:
                            act.wait_ge(evac, st.up(st.n + 1))
                            act.activation(tmp[b][:, 0:T], tmp[b][:, 0:T], ACT.Silu,
                                           bias=Vd("ffn_b", p0 + pair)).then_inc(silu, 1)
                        else:
                            act.wait_ge(evac, st.up(st.n + 1))
                            act.activation(hid_hi[:, bass.ds(pair, 1), 0:T].rearrange("p a t -> p (a t)"),
                                           sig[b][:, 0:T], ACT.Copy).then_inc(hid_head, 1)
                    walk(act, layer, f"up{f}", lift, keep=AHEAD)
                    if f == 0:
                        walk(act, layer, "dn0", lambda st: head(st, size(st, layer, "dn0")), keep=AHEAD)
                    else:
                        for idx in range(LEN["dn1"]):
                            squares("dn1", 2 * layer + 2)(Step(n0 + START["dn1"] + idx, idx))
            act.wait_ge(stat, 2 * DEPTH + 1)
            act.wait_ge(sq_sum, 7 * (2 * DEPTH + 1))
            act.activation(sqb[:, 0:SEQ], psB[0][:, 0:SEQ], ACT.Sqrt, bias=V("eps", 0)).then_inc(root, 1)

        @block.vector
        def _(dve):
            def rest(st, tiles):
                if st.i is None and st.n + AHEAD >= TOTAL:
                    return
                s = (st.n + AHEAD) % SLOTS
                dve.wait_ge(head_done, st.up(st.n + AHEAD + 1))
                dve.tensor_tensor(w_lo[:, s, 0:tiles * P], raw[:, s, 0:tiles * P],
                                  w_hi[:, s, 0:tiles * P].bitcast(F32), ALU.subtract).then_inc(rest_done, 1)

            def size(st, name):
                return SIZE[START[name]] if st.i is not None else SIZE[(st.n + AHEAD) % PER_LAYER]

            def read_mod(group, layer, c0, count, ready):
                dve.wait_ge(ada_done, ready)
                bank = psB[3][:, 0:2 * count].rearrange("p (c v) -> p c v", v=2)
                for vv in range(2):
                    dve.tensor_tensor(mod[:, layer, c0:c0 + count, vv], bank[:, :, vv],
                                      vec[:, VEC["b_ada"] + ADA_L * layer + c0:VEC["b_ada"] + ADA_L * layer + c0 + count],
                                      ALU.add).then_inc(mod_done, 1)
                dve.wait_ge(mod_done, 2 * group + 2)
                which = group % 2
                g = VEC["g_mix" if which == 0 else "g_ffn"] + KD * layer
                for vv in range(2):
                    dve.scalar_tensor_tensor(gsc[:, which, vv, :], mod[:, layer, 24 * which + 8:24 * which + 16, vv],
                                             1.0, vec[:, g:g + KD], ALU.add, ALU.mult).then_inc(gsc_done, 1)

            def add_square(count, T):
                r, o = divmod(count, 8)
                if o:
                    dve.wait_ge(sq_done, count + 1)
                    if o > 1:
                        dve.wait_ge(sq_sum, 7 * r + o - 1)
                    dve.tensor_tensor(sqa[:, 0:T], sqa[:, 0:T], sqb[:, 0:T], ALU.add).then_inc(sq_sum, 1)

            def norm(layer, which, T):
                r = 2 * layer + which
                dve.wait_ge(root, r + 1)
                dve.reciprocal(sqb[:, 0:T], sqb[:, 0:T]).then_inc(inv, 1)
                dve.wait_ge(inv, r + 1)
                dve.wait_ge(gsc_done, 2 * r + 2)
                for kk in range(KD + 1):
                    if kk < KD:
                        if kk >= 2:
                            dve.wait_ge(h_rest, 8 * r + kk - 1)
                        for s in range(T // SEQ):
                            cols = slice(s * SEQ, (s + 1) * SEQ)
                            op = dve.scalar_tensor_tensor(tmp[kk % 2][:, cols], X[:, kk, cols],
                                                          gsc[:, which, s, kk:kk + 1], sqb[:, cols],
                                                          ALU.mult, ALU.mult)
                        op.then_inc(ht, 1)
                    if kk >= 1:
                        c = kk - 1
                        dve.wait_ge(h_head, 8 * r + c + 1)
                        for s in range(T // SEQ):
                            cols = slice(s * SEQ, (s + 1) * SEQ)
                            op = dve.scalar_tensor_tensor(h_lo[:, c, cols], tmp[c % 2][:, cols],
                                                          mod[:, layer, 24 * which + c, s:s + 1],
                                                          h_hi[:, c, cols].bitcast(F32), ALU.add, ALU.subtract)
                        op.then_inc(h_rest, 1)

            dve.wait_ge(vecs_in, 16)
            dve.tensor_scalar(nsink[:, :], vec[:, VEC["sink"]:VEC["sink"] + DEPTH * N_HEADS], -1.0, None, ALU.mult)\
                .then_inc(nsink_done, 1)
            for kk in range(KD):
                add_square(kk, NT)
            for ahead in range(AHEAD):
                rest(Step(ahead - AHEAD, 0), 8)
            read_mod(0, 0, 0, ADA_A, ADA_A)

            for layer in range(DEPTH):
                n0 = layer * PER_LAYER
                S = streams(layer)
                T = SEQ * S
                if layer:
                    read_mod(2, 1, 0, ADA_A, ADA_L + ADA_A)
                norm(layer, 0, NT)
                dve.wait_ge(pads, 2)
                if layer:
                    dve.memset(cx[:, :, :, :], 0.0).then_inc(pads, 1)
                    dve.memset(glu[:, :, :, :], 0.0).then_inc(pads, 1)
                    dve.wait_ge(pads, 4)
                for idx in range(LEN["in"]):
                    st = Step(n0 + idx, idx)
                    rest(st, size(st, "in"))
                    ps = psA[st.slot]
                    if idx in (14, 16):
                        continue
                    dve.wait_ge(chunk_done, st.n + 1)
                    if idx < 4:
                        dve.tensor_copy(q[:, idx, 0:T], ps[:, 0:T]).then_inc(evac, 1)
                    elif idx == 4:
                        dve.tensor_copy(k[:, :], ps[:, :]).then_inc(evac, 1)
                    elif idx == 5:
                        dve.tensor_copy(v[:, :, :].rearrange("p b n -> p (b n)"), ps[:, :]).then_inc(evac, 1)
                    elif idx < 8:
                        dve.tensor_copy(f_in(layer, idx - 6), ps[:, 0:T]).then_inc(evac, 1)
                    elif idx in (8, 10):
                        dve.tensor_copy(pc[:, (idx - 8) // 2, 0:T], ps[:, 0:T]).then_inc(evac, 1)
                    elif idx in (9, 11):
                        c = (idx - 9) // 2
                        dve.wait_ge(evac, st.n)
                        dve.tensor_tensor(cx[:, c, 0:S, 1:1 + SEQ], both(ps[:, 0:T], T), both(pc[:, c, 0:T], T),
                                          ALU.mult).then_inc(evac, 1)
                    elif idx in (12, 13):
                        dve.tensor_copy(pb[:, idx - 12, 0:T], ps[:, 0:T]).then_inc(evac, 1)
                    else:
                        c = (idx - 15) // 2
                        dve.wait_ge(sigd, 34 * layer + c + 1)
                        dve.tensor_tensor(glu[:, c, 0:S, PAD:PAD + SEQ], both(ps[:, 0:T], T),
                                          both(sig[c][:, 0:T], T), ALU.mult).then_inc(evac, 2)
                for j in range(5):
                    dst = q[:, j, 0:SEQ] if j < 4 else k[:, 0:SEQ]
                    r = 15 * layer + 3 * j
                    dve.wait_ge(rot, 5 * layer + j + 1)
                    if j >= 2:
                        dve.wait_ge(rope, r - 3)
                    dve.tensor_tensor(tmp[j % 2][:, 0:SEQ], psB[j % 2][:, 0:SEQ], M("sin", SEQ), ALU.mult)\
                        .then_inc(rope, 1)
                    dve.tensor_tensor(dst, dst, M("cos", SEQ), ALU.mult).then_inc(rope, 1)
                    dve.wait_ge(rope, r + 2)
                    dve.tensor_tensor(dst, dst, tmp[j % 2][:, 0:SEQ], ALU.add).then_inc(rope, 1)
                fc0 = 4 * layer
                for step in range(4):
                    for c in range(2):
                        w = 3 * (2 * layer + c)
                        u = both(pc[:, c, 0:T], T)
                        if step:
                            dve.wait_ge(sc_step, 8 * layer + 2 * step - 1 + c)
                        if step == 0:
                            op = dve.tensor_scalar(u, cx[:, c, 0:S, 0:SEQ], V("sc_w", w), None, ALU.mult)
                        elif step < 3:
                            op = dve.scalar_tensor_tensor(u, cx[:, c, 0:S, step:step + SEQ], V("sc_w", w + step), u,
                                                          ALU.mult, ALU.add)
                        else:
                            op = dve.tensor_tensor(u, u, both(pb[:, c, 0:T], T), ALU.mult)
                        op.then_inc(sc_step, 1)
                for j in range(2 * S):
                    s, c = divmod(j, 2)
                    dve.wait_ge(fn_head, fc0 + j + 1)
                    dve.tensor_tensor(y_lo[:, c, s * SEQ:(s + 1) * SEQ], psA[j][:, 0:SEQ],
                                      y_hi[:, c, s * SEQ:(s + 1) * SEQ].bitcast(F32), ALU.subtract)\
                        .then_inc(fn_rest, 1)
                for c in range(2):
                    dve.wait_ge(sc_head, 2 * layer + c + 1)
                    dve.tensor_tensor(y_lo[:, 2 + c, 0:T], pc[:, c, 0:T], y_hi[:, 2 + c, 0:T].bitcast(F32),
                                      ALU.subtract).then_inc(sc_rest, 1)

                def conv_tap(i):
                    j, c = divmod(i, 2)
                    w = V("conf_w", TAPS * layer + CONF_K * c + j)
                    src, dst = glu[:, c, 0:S, j:j + SEQ], both(acc[:, c, 0:T], T)
                    if j == 0:
                        op = dve.tensor_scalar(dst, src, w, V("conf_b", 2 * layer + c), ALU.mult, ALU.add)
                    else:
                        dve.wait_ge(tap, TAPS * layer + i - 1)
                        op = dve.scalar_tensor_tensor(dst, src, w, dst, ALU.mult, ALU.add)
                    op.then_inc(tap, 1)

                un, u0 = units(layer), U0[layer]
                per = -(-TAPS // len(un))
                todo = 0
                for j in range(len(un) + 4):
                    if j < len(un):
                        s, qi, t, half = un[j]
                        width = (4 if s == 0 else 2) * P
                        h = layer * N_HEADS + t + 4 * half
                        dve.wait_ge(s_mm, u0 + j + 1)
                        dve.tensor_reduce(small[:, j % 2, 0:1], psA[j % 2][:, 0:width], AX.X, ALU.max)\
                            .then_inc(negm, 1)
                        dve.wait_ge(negm, 2 * (u0 + j) + 1)
                        dve.tensor_scalar(small[:, j % 2, 1:2], small[:, j % 2, 0:1], -HEAD ** -0.5,
                                          nsink[:, h:h + 1], ALU.mult, ALU.min).then_inc(negm, 1)
                    if 1 <= j <= len(un):
                        b = (j - 1) % 2
                        width = (4 if un[j - 1][0] == 0 else 2) * P
                        dve.wait_ge(expd, 2 * (u0 + j))
                        dve.tensor_tensor(small[:, b, 4:5], small[:, b, 2:3], small[:, b, 3:4], ALU.add)\
                            .then_inc(den, 1)
                        dve.wait_ge(den, 2 * (u0 + j - 1) + 1)
                        dve.reciprocal(small[:, b, 4:5], small[:, b, 4:5]).then_inc(den, 1)
                        dve.wait_ge(den, 2 * (u0 + j))
                        dve.tensor_scalar(prob[:, b, 0:width], prob[:, b, 0:width], small[:, b, 4:5], None,
                                          ALU.mult).then_inc(pn, 1)
                    for _ in range(per):
                        if todo < TAPS:
                            conv_tap(todo)
                            todo += 1
                    if j >= 4 and j % 2 == 0:
                        pair = (j - 4) // 2
                        s, qi, t, _ = un[2 * pair]
                        c0 = SEQ * s + P * qi
                        dve.wait_ge(o_head, u0 // 2 + pair + 1)
                        dve.tensor_tensor(y_lo[:, 4 + t, c0:c0 + P], psB[pair % 2][:, 0:P],
                                          y_hi[:, 4 + t, c0:c0 + P].bitcast(F32), ALU.subtract).then_inc(o_rest, 1)
                read_mod(2 * layer + 1, layer, ADA_A, ADA_B, ADA_L * (layer + 1))

                def dyn_sum(st_o):
                    c0 = 0 if layer == 0 else SEQ
                    if isinstance(st_o, int):
                        return X[:, st_o, c0:c0 + T]
                    return X[:, bass.ds(st_o, 1), c0:c0 + T].rearrange("p a t -> p (a t)")

                def branch(name, b):
                    def step(st):
                        rest(st, size(st, name))
                        if name == "cf" and st.idx > 0:
                            merged_rest(st.idx - 1)
                        o = st.up(st.idx)
                        dve.wait_ge(sigd, st.up(34 * layer + 2 + 8 * b + st.idx + 1))
                        dve.wait_ge(chunk_done, st.up(st.n + 1))
                        ps, sg = psB[st.slot][:, 0:T], sig[st.n % 2][:, 0:T]
                        if b == 0:
                            dve.tensor_tensor(dyn_sum(o), ps, sg, ALU.mult).then_inc(evac, 1)
                        else:
                            g = 8 * (b - 1) + st.idx
                            if g >= 2:
                                dve.wait_ge(m_sum, st.up(24 * layer + g - (st.idx > 0)))
                            t = tmp[st.n % 2][:, 0:T]
                            dve.tensor_tensor(t, ps, sg, ALU.mult).then_inc(evac, 1)
                            dve.wait_ge(evac, st.up(st.n + 1))
                            dve.tensor_tensor(dyn_sum(o), dyn_sum(o), t, ALU.add).then_inc(m_sum, 1)
                    return step

                def merged_rest(o):
                    dve.wait_ge(m_head, 8 * layer + o + 1)
                    dve.tensor_tensor(mg_lo[:, o, 0:T], branch_sum(layer, o), mg_hi[:, o, 0:T].bitcast(F32),
                                      ALU.subtract).then_inc(m_rest, 1)

                walk(dve, layer, "fn", branch("fn", 0), keep=AHEAD)
                walk(dve, layer, "sc", branch("sc", 1), keep=AHEAD)
                m0 = n0 + START["at"]
                for idx in range(LEN["at"]):
                    st = Step(m0 + idx, idx)
                    rest(st, size(st, "at"))
                    if idx == 1:
                        dve.wait_ge(ln_mean, layer + 1)
                        for c in range(2):
                            dve.scalar_tensor_tensor(acc[:, c, 0:T], psB[m0 % 4][:, 0:T], -float(D // CONF_W),
                                                     acc[:, c, 0:T], ALU.mult, ALU.add).then_inc(ln_xc, 1)
                    if idx % 3 == 2:
                        for half, ps in enumerate((psA, psB)):
                            o = idx // 3 * 2 + half
                            if half == 0:
                                dve.wait_ge(sigd, 34 * layer + 2 + 16 + o + 2)
                                dve.wait_ge(chunk_done, st.n + 1)
                                dve.wait_ge(m_sum, 24 * layer + 8 + o)
                            t = tmp[half][:, 0:T]
                            dve.tensor_tensor(t, ps[st.slot][:, 0:T], sig[half][:, 0:T], ALU.mult)\
                                .then_inc(*((evac, 3) if half else (prod, 1)))
                        for half in range(2):
                            o = idx // 3 * 2 + half
                            if half == 0:
                                dve.wait_ge(prod, 4 * layer + idx // 3 + 1)
                            else:
                                dve.wait_ge(evac, st.n + 1)
                            dve.tensor_tensor(dyn_sum(o), dyn_sum(o), tmp[half][:, 0:T], ALU.add).then_inc(m_sum, 1)
                    if idx == 8:
                        dve.wait_ge(ln_root, layer + 1)
                        dve.reciprocal(sqb[:, 0:T], sqb[:, 0:T]).then_inc(ln_inv, 1)
                        dve.wait_ge(ln_inv, layer + 1)
                        for c in range(2):
                            dve.tensor_tensor(acc[:, c, 0:T], acc[:, c, 0:T], sqb[:, 0:T], ALU.mult)\
                                .then_inc(ln_n, 1)
                    if idx == 10:
                        for c in range(2):
                            dve.wait_ge(ln_head, 2 * layer + c + 1)
                            dve.tensor_tensor(yc_lo[:, c, 0:T], acc[:, c, 0:T], yc_hi[:, c, 0:T].bitcast(F32),
                                              ALU.subtract).then_inc(ln_rest, 1)
                for idx in range(LEN["cf"]):
                    branch("cf", 3)(Step(n0 + START["cf"] + idx, idx))
                merged_rest(KD - 1)

                def residual(name, which, r, ada_col):
                    def step(st):
                        rest(st, size(st, name))
                        if r is not None and st.idx > 0:
                            add_square(8 * r + st.idx - 1, T)
                        dve.wait_ge(chunk_done, st.up(st.n + 1))
                        o = st.up(st.idx)
                        for s in range(S):
                            cols = slice(s * SEQ, (s + 1) * SEQ)
                            old = x_in if layer == 0 and name == "out" else X
                            if st.i is None:
                                dst, src = X[:, st.idx, cols], old[:, st.idx, cols]
                                g = mod[:, layer, ada_col + st.idx, s:s + 1]
                            else:
                                dst = X[:, bass.ds(o, 1), cols].rearrange("p a t -> p (a t)")
                                src = dst
                                g = mod[:, layer, bass.ds(o + ada_col, 1), s:s + 1].rearrange("p a b -> p (a b)")
                            op = dve.scalar_tensor_tensor(dst, psA[st.slot][:, cols], g, src, ALU.mult, ALU.add)
                        op.then_inc(evac, 1)
                    return step

                if layer == 0:
                    dve.wait_ge(x_again, 16)
                for idx in range(LEN["out"]):
                    residual("out", 1, 2 * layer + 1, 16)(Step(n0 + START["out"] + idx, idx))
                add_square(8 * (2 * layer + 1) + 7, T)
                norm(layer, 1, T)

                for f in range(2):
                    p0 = HALF_FF * (2 * layer + f)

                    def hidden_rest(st, pair, b):
                        dve.wait_ge(hid_head, st.up(p0 + pair + 1, 2))
                        dst = hid_lo[:, bass.ds(st.up(pair, 2), 1), 0:T].rearrange("p a t -> p (a t)")
                        src = hid_hi[:, bass.ds(st.up(pair, 2), 1), 0:T].rearrange("p a t -> p (a t)")
                        dve.tensor_tensor(dst, sig[b][:, 0:T], src.bitcast(F32), ALU.subtract).then_inc(hid_rest, 1)

                    def lift(st):
                        rest(st, size(st, f"up{f}"))
                        pair, b = st.idx // 2, (st.idx // 2) % 2
                        ps = psA[st.slot][:, 0:T]
                        dve.wait_ge(chunk_done, st.up(st.n + 1))
                        if st.idx % 2 == 0:
                            w = 3 * p0 + 3 * pair
                            c0 = 2 * p0 + 2 * pair
                            t3, p3 = both(tmp[b][:, 0:T], T), both(ps, T)
                            dve.tensor_scalar(t3, p3, Vd("ffn_w", st.up(w + 1, 6)), None, ALU.mult).then_inc(cv, 1)
                            dve.wait_ge(cv, st.up(c0 + 1, 4))
                            dve.scalar_tensor_tensor(t3[:, :, 1:SEQ], p3[:, :, 0:SEQ - 1], Vd("ffn_w", st.up(w, 6)),
                                                     t3[:, :, 1:SEQ], ALU.mult, ALU.add).then_inc(cv, 1)
                            dve.wait_ge(cv, st.up(c0 + 2, 4))
                            dve.scalar_tensor_tensor(t3[:, :, 0:SEQ - 1], p3[:, :, 1:SEQ],
                                                     Vd("ffn_w", st.up(w + 2, 6)), t3[:, :, 0:SEQ - 1],
                                                     ALU.mult, ALU.add).then_inc(evac, 1)
                        else:
                            dve.wait_ge(silu, st.up(p0 + pair + 1, 2))
                            dve.tensor_tensor(sig[b][:, 0:T], ps, tmp[b][:, 0:T], ALU.mult).then_inc(evac, 1)
                            hidden_rest(st, pair, b)
                    walk(dve, layer, f"up{f}", lift, keep=AHEAD)
                    name = f"dn{f}"
                    if f == 0:
                        walk(dve, layer, name, residual(name, 1, None, 40), keep=AHEAD)
                    else:
                        for idx in range(LEN[name]):
                            residual(name, 1, 2 * layer + 2, 40)(Step(n0 + START[name] + idx, idx))
                        add_square(8 * (2 * layer + 2) + 7, T)
            dve.wait_ge(root, 2 * DEPTH + 1)
            dve.reciprocal(sqb[:, 0:SEQ], sqb[:, 0:SEQ]).then_inc(inv, 1)
            dve.wait_ge(inv, 2 * DEPTH + 1)
            for kk in range(KD):
                dve.scalar_tensor_tensor(y_out[:, kk, :], X[:, kk, 0:SEQ], V("g_final", kk), sqb[:, 0:SEQ],
                                         ALU.mult, ALU.mult).then_inc(fin, 1)


def constants():
    import numpy as np
    m = np.zeros((P, NMAT), np.float64)

    def put(name, a, off=0):
        m[:a.shape[0], MAT[name] + off:MAT[name] + off + a.shape[1]] = a
    put("ident", np.eye(P))
    put("mean", np.full((P, P), 1.0 / D))
    r = np.zeros((P, P))
    for g in range(P // 32):
        for j in range(16):
            a, b = 32 * g + j, 32 * g + 16 + j
            r[b, a] = -1.0
            r[a, b] = 1.0
    put("rot", r)
    i = np.arange(P)
    put("mask0", np.where(i[None, :] <= i[:, None], 0.0, -1e30))
    put("mask1", np.where(i[None, :] >= i[:, None], 0.0, -1e30))
    c = np.arange(64)
    ang = 2 * np.pi * np.outer(c, c) / 64
    put("chan", np.kron(np.eye(2), np.cos(ang)))
    put("chan", np.kron(np.eye(2), np.sin(ang)), 128)
    n = np.arange(SEQ)
    ang = 2 * np.pi * (np.outer(n, n) % SEQ) / SEQ
    scale = 1.0 / np.sqrt(SEQ * 64)
    for h in range(2):
        put("pos", np.cos(ang)[h * P:(h + 1) * P] * scale, 512 * h)
        put("pos", -np.sin(ang)[h * P:(h + 1) * P] * scale, 512 * h + 256)
    m = m.astype(np.float32)
    inv = np.float32(10000.0) ** (-np.arange(16, dtype=np.float32) / np.float32(16))
    pos = np.stack([n // 64, n % 64]).astype(np.float32)
    a = np.zeros((64, SEQ), np.float32)
    for axis in range(2):
        for half in range(2):
            a[axis * 32 + half * 16:axis * 32 + half * 16 + 16] = pos[axis][None, :] * inv[:, None]
    m[:, MAT["cos"]:MAT["cos"] + SEQ] = np.tile(np.cos(a), (2, 1))
    m[:, MAT["sin"]:MAT["sin"] + SEQ] = np.tile(np.sin(a), (2, 1))
    return m


def kernel(**inputs):
    import numpy as np
    import concourse.bacc as bacc
    from concourse.bass_utils import run_bass_kernel_spmd as run

    a = {name: np.asarray(x) for name, x in inputs.items()}

    def tiles(w):
        kk, mm = w.shape
        return w.reshape(kk // P, P, mm // P, P).transpose(2, 0, 1, 3)

    def chunks(t):
        n, c = t.shape[:2]
        return np.ascontiguousarray(t.transpose(0, 2, 1, 3).reshape(n, P, c * P))

    def channels(x):
        return x.T.reshape(-1, P, x.shape[0]).transpose(1, 0, 2)

    arrays = {"mat": constants()}
    heads = np.concatenate([np.arange(HEAD) + HEAD * h for t in range(4) for h in (t, t + 4)])
    arrays["x"] = np.ascontiguousarray(np.concatenate([channels(a["x"][0]), channels(a["ctx"][0])], axis=2))
    vec = np.zeros((P, NVEC), np.float32)

    def put(name, cols, off=0):
        vec[:, VEC[name] + off:VEC[name] + off + cols.shape[1]] = cols
    put("cc", np.stack([a["c"][0].reshape(KD, P), a["c_ctx"].reshape(KD, P)], 2).transpose(1, 0, 2).reshape(P, -1))
    put("b_ada", a["b_ada"].reshape(-1, P).T)
    put("g_mix", a["g_mix"].reshape(-1, P).T)
    put("g_ffn", a["g_ffn"].reshape(-1, P).T)
    put("g_final", a["g_final"].reshape(-1, P).T)
    put("sink", np.broadcast_to(a["attn_sink"].reshape(1, -1), (P, DEPTH * N_HEADS)))
    put("conf_w", a["conf_dw_w"].reshape(DEPTH, CONF_K, 2, P).transpose(3, 0, 2, 1).reshape(P, -1))
    put("conf_b", a["conf_dw_b"].reshape(-1, P).T)
    put("ln_g", a["conf_ln_g"].reshape(-1, P).T)
    put("ln_b", a["conf_ln_b"].reshape(-1, P).T)
    put("sc_w", a["sc_w"].reshape(DEPTH, SC_K, 2, P).transpose(3, 0, 2, 1).reshape(P, -1))
    put("ffn_w", a["ffn_dw_w"].reshape(DEPTH, 3, 2 * HALF_FF, P).transpose(3, 0, 2, 1).reshape(P, -1))
    put("ffn_b", a["ffn_dw_b"].reshape(-1, P).T)
    vec[:, VEC["eps"]] = EPS
    arrays["vec"] = vec
    arrays["w_ada"] = np.concatenate([chunks(tiles(w)) for w in a["w_ada"]])
    for layer in range(DEPTH):
        w = a["w_in"][layer]
        at = np.cumsum([0, Q_W, KV_W, KV_W, 2 * CONF_W, SC_W, SC_W, SC_W, FN_W])
        wq, wk, wv, wcf, wb, wc, wx, wf = (tiles(w[:, s:e]) for s, e in zip(at[:-1], at[1:]))
        wq = tiles(w[:, heads])
        gates = tiles(w[:, at[-1]:]).reshape(4, KD, KD, P, P)
        arrays[f"w_in{layer}"] = chunks(np.concatenate(
            [wq, wk, wv, wf, wc[0:1], wx[0:1], wc[1:2], wx[1:2], wb, wcf[2:3], wcf[0:1], wcf[3:4], wcf[1:2]]))
        br = [tiles(a["w_br_attn"][layer][heads]), tiles(a["w_br_conf"][layer]), tiles(a["w_br_sconv"][layer]),
              tiles(a["w_br_fourier"][layer])]
        for name, b in (("fn", 3), ("sc", 2), ("cf", 1)):
            arrays[f"w_{name}{layer}"] = chunks(np.concatenate([gates[b], br[b]], axis=1))
        at_chunks = []
        for o in range(0, KD, 2):
            at_chunks += [gates[0][o], gates[0][o + 1], np.concatenate([br[0][o], br[0][o + 1]])]
        arrays[f"w_at{layer}"] = chunks(np.stack(at_chunks))
        arrays[f"w_out{layer}"] = chunks(tiles(a["w_out"][layer]))
        up = tiles(a["w_up"][layer]).reshape(2, 2, HALF_FF, KD, P, P)
        down = tiles(a["w_down"][layer])
        for f in range(2):
            arrays[f"w_up{f}{layer}"] = chunks(up[:, f].transpose(1, 0, 2, 3, 4).reshape(2 * HALF_FF, KD, P, P))
            arrays[f"w_dn{f}{layer}"] = chunks(down[:, f * HALF_FF:(f + 1) * HALF_FF])

    nc = bacc.Bacc("TRN2", target_bir_lowering=False, num_devices=1)
    io = {name: nc.dram_tensor(name, x.shape, F32, kind="ExternalInput").ap() for name, x in arrays.items()}
    io["out"] = nc.dram_tensor("out", (P, KD, SEQ), F32, kind="ExternalOutput").ap()
    program(nc, io)
    r = run(nc, [arrays], core_ids=[0])
    return np.ascontiguousarray(r.results[0]["out"].transpose(2, 1, 0).reshape(1, SEQ, D))
```

```python
from contextlib import ExitStack

import concourse.bass as bass
from concourse import mybir

F32 = mybir.dt.float32
F32R = mybir.dt.float32r
ALU = mybir.AluOpType
ACT = mybir.ActivationFunctionType
AX = mybir.AxisListType

P = 128
D = 1024
DEPTH = 2
SEQ = 256
CTX = 256
KD = D // P
N_HEADS = 8
HEAD = 64
Q_W, KV_W = 512, 128
CONF_W, CONF_K = 256, 31
SC_W, SC_K = 256, 3
FN_W = 256
D_FF = 2816
HALF_FF = D_FF // 2 // P
EPS = 1e-6
NT = SEQ + CTX
PAD = (CONF_K - 1) // 2
SLOTS = 4
AHEAD = 3
TAPS = 2 * CONF_K
ADA_A, ADA_B = 16, 32
ADA_L = ADA_A + ADA_B

PHASES = [("in", 18, 8), ("fn", 8, 10), ("sc", 8, 10), ("at", 12, 8), ("cf", 8, 10), ("out", 8, 8),
          ("up0", 22, 8), ("dn0", 8, HALF_FF), ("up1", 22, 8), ("dn1", 8, HALF_FF)]
START, SIZE, LEN = {}, [], {}
for _name, _count, _tiles in PHASES:
    START[_name] = len(SIZE)
    LEN[_name] = _count
    SIZE += [_tiles] * _count
PER_LAYER = len(SIZE)
TOTAL = DEPTH * PER_LAYER

ADA_START = {2: START["in"] + 2, 3: START["fn"], 4: START["sc"] + 1, 5: START["at"] + 3, 6: START["cf"] + 1,
             8: START["up0"], 9: START["up0"] + 10, 7: START["up0"] + 21, 10: START["up1"] + 1,
             11: START["up1"] + 10}
ORDER = [0, 1] + sorted(ADA_START, key=ADA_START.get)
POS = {_g: _p for _p, _g in enumerate(ORDER)}
REDUCE = {ADA_START[_g] + 10 - (_g == 3): _g for _g in ADA_START}
ADA_AT = {ADA_START[_g] + _k: 8 * _g + _k for _g in ADA_START for _k in range(8)}
assert len(ADA_AT) == DEPTH * ADA_L - ADA_A and max(REDUCE) < START["dn1"]
FILLS = []
for _n in range(TOTAL):
    FILLS.append(("w", _n))
    if _n - AHEAD in ADA_AT:
        FILLS.append(("ada", ADA_AT[_n - AHEAD]))
PLACE = {_f: _p for _p, _f in enumerate(FILLS)}


def ada_vectors(a):
    return 2 if a < ADA_L or a % ADA_L < 16 else 1


ADA_STEPS, _s = {}, 0
for _kind, _a in FILLS:
    if _kind == "ada":
        _s += ada_vectors(_a)
        ADA_STEPS[_a] = _s


VEC, _at = {}, 0
for _name, _n in [("cc", 2 * KD), ("b_ada", DEPTH * ADA_L), ("g_mix", DEPTH * KD), ("g_ffn", DEPTH * KD),
                  ("g_final", KD), ("sink", DEPTH * N_HEADS), ("conf_w", DEPTH * TAPS), ("conf_b", DEPTH * 2),
                  ("ln_g", DEPTH * 2), ("ln_b", DEPTH * 2), ("sc_w", DEPTH * 2 * SC_K),
                  ("ffn_w", DEPTH * 2 * HALF_FF * 3), ("ffn_b", DEPTH * 2 * HALF_FF), ("eps", 1), ("one", 1)]:
    VEC[_name] = _at
    _at += _n
NVEC = _at
MAT, _at = {}, 0
for _name, _n in [("ident", 128), ("mean", 128), ("rot", 128), ("mask0", 128), ("mask1", 128),
                  ("chan", 256), ("pos", 1024), ("cos", 256), ("sin", 256)]:
    MAT[_name] = _at
    _at += _n
NMAT = _at


class Step:

    def __init__(self, n, idx, i=None):
        self.n, self.idx, self.i = n, idx, i
        self.slot = n % SLOTS

    def up(self, base, per=4):
        return base if self.i is None else base + per * self.i

    def filled(self, item, ahead=0):
        p = PLACE[(item, self.n + ahead)]
        per = 0 if self.i is None else (PLACE[(item, self.n + ahead + SLOTS)] - p) * 16 // SLOTS
        return p % SLOTS, self.up(16 * (p // SLOTS + 1), per)


def walk(eng, layer, name, step, lead=0, skip=0, keep=0):
    first, count = layer * PER_LAYER + START[name], LEN[name]
    if lead:
        skip = max(skip, -(-lead // SLOTS))
    groups = (count - keep) // SLOTS
    if groups - skip < 2:
        skip = groups = 0
    for idx in range(lead, min(skip * SLOTS, count)):
        step(Step(first + idx, idx))
    if groups:
        with eng.Fori(skip, groups) as i:
            for j in range(SLOTS):
                step(Step(first + j, j, i))
        lead = 0
    for idx in range(max(lead, groups * SLOTS), count):
        step(Step(first + idx, idx))


def program(nc, io):
    ctx = ExitStack()
    with ctx:
        base = -(-nc.sbuf_base // 32) * 32
        top = [base]

        def at(name, shape, dt, offset):
            return nc.alloc_sbuf_tensor_at(name, [P] + shape, dt, offset=offset)

        def place(name, shape, dt=F32):
            size = 4
            for s in shape:
                size *= s
            offset = top[0]
            top[0] += -(-size // 32) * 32
            return at(name, shape, dt, offset)

        SLOT = HALF_FF * P
        raw = place("raw", [SLOTS, SLOT])
        w_hi = place("w_hi", [SLOTS, SLOT], F32R)
        w_lo = place("w_lo", [SLOTS, SLOT], F32R)
        ada_first = at("ada_first", [ADA_A, KD * P], F32, base)
        assert ADA_A * KD * P <= 3 * SLOTS * SLOT
        ada_sum = place("ada_sum", [2, KD * P])
        X = place("X", [KD, NT])
        h_off = top[0]
        h_hi = place("h_hi", [KD, NT], F32R)
        h_lo = place("h_lo", [KD, NT], F32R)
        y_off = top[0]
        y_hi = place("y_hi", [8, NT], F32R)
        y_lo = place("y_lo", [8, NT], F32R)
        yc_hi = place("yc_hi", [2, NT], F32R)
        yc_lo = place("yc_lo", [2, NT], F32R)
        q_off = top[0]
        q = place("q", [4, NT])
        k = place("k", [NT])
        v = place("v", [NT // P, KV_W])
        glu = place("glu", [2, 2, SEQ + 2 * PAD])
        acc = place("acc", [2, NT])
        t_off = top[0]
        prob = place("prob", [2, NT])
        probT = place("probT", [2, NT])
        sqb = place("sqb", [NT])
        sqa = place("sqa", [NT])
        mat = place("mat", [NMAT])
        vec = place("vec", [NVEC])
        csil = place("csil", [KD, 2])
        mod = place("mod", [2, ADA_L, 2])
        gsc = place("gsc", [2, 2, KD])
        nsink = place("nsink", [DEPTH * N_HEADS])
        small = place("small", [2, 6])
        assert top[0] <= nc.sbuf_usable_end, (top[0], nc.sbuf_usable_end)
        mg_hi = at("mg_hi", [KD, NT], F32R, y_off)
        mg_lo = at("mg_lo", [KD, NT], F32R, y_off + 4 * KD * NT)
        assert y_off + 4 * NT * 2 * HALF_FF <= t_off
        hid_hi = at("hid_hi", [HALF_FF, NT], F32R, y_off)
        hid_lo = at("hid_lo", [HALF_FF, NT], F32R, y_off + 4 * HALF_FF * NT)
        x_in = at("x_in", [KD, NT], F32, q_off)
        ya_off = y_off + 4 * 4 * NT
        cx = at("cx", [2, 2, SEQ + 2], F32, ya_off)
        pb = at("pb", [2, NT], F32, y_off + 4 * 8 * NT + 4 * 4 * NT)
        pc = at("pc", [2, NT], F32, y_off + 4 * 8 * NT + 4 * 6 * NT)
        assert 4 * 2 * 2 * (SEQ + 2) <= 4 * 4 * NT
        tmp = [at(f"tmp{b}", [NT], F32, t_off + 4 * NT * b) for b in range(2)]
        sig = [at(f"sig{b}", [NT], F32, t_off + 4 * NT * (2 + b)) for b in range(2)]
        y_out = at("y_out", [KD, SEQ], F32, h_off)

        psA = [ctx.enter_context(nc.psum_tensor(f"psA{b}", [P, 512], F32)) for b in range(4)]
        psB = [ctx.enter_context(nc.psum_tensor(f"psB{b}", [P, 512], F32)) for b in range(4)]

        def sem(name):
            return ctx.enter_context(nc.semaphore(name))

        raw_full = [sem(f"raw_full{s}") for s in range(SLOTS)]
        ada_in = [sem(f"ada_in{j}") for j in range(ADA_A // 2)]
        mats_in, vecs_in, x_full, x_again, stored = map(sem, ("mats_in", "vecs_in", "x_full", "x_again", "stored"))
        head_done, rest_done = sem("head_done"), sem("rest_done")
        chunk_done = sem("chunk_done")
        evac = sem("evac")
        ada_pe, ada_row, ada_acc, reduced = sem("ada_pe"), sem("ada_row"), sem("ada_acc"), sem("ada_reduced")
        tap_pool = sem("tap_pool")
        csil_done, nsink_done, mod_done, gsc_done = map(sem, ("csil_done", "nsink_done", "mod_done", "gsc_done"))
        sq_done, sq_sum, stat, root, inv, ht, h_head, h_rest = map(sem, (
            "sq_done", "sq_sum", "stat", "root", "inv", "ht", "h_head", "h_rest"))
        pads, rot, rope, fc_mm, fc, fn_mm, fn_head, fn_rest = map(sem, (
            "pads", "rot", "rope", "fc_mm", "fc", "fn_mm", "fn_head", "fn_rest"))
        sc_step, sc_head, sc_rest, sigd = map(sem, ("sc_step", "sc_head", "sc_rest", "sigd"))
        s_mm, negm, expd, den, pn, t_mm, pt, o_mm, o_head, o_rest = map(sem, (
            "s_mm", "negm", "expd", "den", "pn", "t_mm", "pt", "o_mm", "o_head", "o_rest"))
        tap, ln_mean, ln_xc, ln_sq, ln_var, ln_root, ln_inv, ln_n, ln_silu, ln_head, ln_rest = map(sem, (
            "tap", "ln_mean", "ln_xc", "ln_sq", "ln_var", "ln_root", "ln_inv", "ln_n", "ln_silu", "ln_head",
            "ln_rest"))
        m_sum, m_head, m_rest = map(sem, ("m_sum", "m_head", "m_rest"))
        cv, silu, hid_head, hid_rest, x_part, fin = map(sem, ("cv", "silu", "hid_head", "hid_rest", "x_part", "fin"))

        def M(name, n=128, off=0):
            return mat[:, MAT[name] + off:MAT[name] + off + n]

        def V(name, i):
            return vec[:, VEC[name] + i:VEC[name] + i + 1]

        def Vd(name, i):
            return vec[:, bass.ds(VEC[name] + i, 1)]

        def streams(layer):
            return 2 if layer == 0 else 1

        def both(ap, T):
            return ap.rearrange("p (s t) -> p s t", s=T // SEQ)

        def branch_sum(layer, o):
            return X[:, o, 0:NT] if layer == 0 else X[:, o, SEQ:NT]

        def f_in(layer, c):
            return X[:, c, 0:NT] if layer == 0 else X[:, c, SEQ:NT]

        def f_mid(layer, tb):
            if layer == 0:
                return X[:, 2 + tb, :].rearrange("p (c n) -> p c n", c=2)
            return X[:, 2 + 2 * tb:4 + 2 * tb, SEQ:NT]

        def units(layer):
            return [(s, qi, t, half) for s in range(streams(layer)) for qi in range(2) for t in range(4)
                    for half in range(2)]

        NU = [len(units(0)), len(units(1))]
        U0 = [0, NU[0]]

        block = ctx.enter_context(nc.Block())

        @block.sync
        def _(sp):
            sp.dma_start(vec[:, :], io["vec"]).then_inc(vecs_in, 16)

            def slot_free(p, shift=0):
                if p >= SLOTS:
                    item, m = FILLS[p - SLOTS]
                    if item == "w":
                        sp.wait_ge(rest_done, m + 1 + shift)
                    else:
                        sp.wait_ge(ada_acc, ADA_STEPS[m])

            def load_ada(a):
                p = PLACE[("ada", a)]
                slot_free(p)
                sp.dma_start(raw[:, p % SLOTS, 0:KD * P], io["w_ada"][a]).then_inc(raw_full[p % SLOTS], 16)

            for j in range(ADA_A // 2):
                sp.dma_start(ada_first[:, 2 * j:2 * j + 2, :], io["w_ada"][2 * j:2 * j + 2].rearrange("a p n -> p a n"))\
                    .then_inc(ada_in[j], 16)
            sp.wait_ge(ada_pe, -(-SLOTS * SLOT // (KD * P)))
            for layer in range(DEPTH):
                for name, _, tiles in PHASES:
                    src = io[f"w_{name}{layer}"]

                    def load(st):
                        p = PLACE[("w", st.n)]
                        slot_free(p, 0 if st.i is None else SLOTS * st.i)
                        dst = raw[:, p % SLOTS, 0:tiles * P]
                        if st.i is None:
                            sp.dma_start(dst, src[st.idx]).then_inc(raw_full[p % SLOTS], 16)
                            if st.n - AHEAD in ADA_AT:
                                load_ada(ADA_AT[st.n - AHEAD])
                        else:
                            sp.dma_start(dst, src[bass.ds(st.up(st.idx), 1)].rearrange("a p n -> p (a n)"))\
                                .then_inc(raw_full[p % SLOTS], 16)

                    walk(sp, layer, name, load, skip=LEN[name] if layer == 0 or name == "in" else 0)
                    if layer == 0 and name == "cf":
                        sp.wait_ge(chunk_done, START["fn"] + 1)
                        sp.wait_ge(tap, CONF_K)
                        sp.wait_ge(tap_pool, 2 * CONF_K)
                        sp.dma_start(x_in[:, :, :], io["x"]).then_inc(x_again, 16)
            for kk in range(KD):
                sp.wait_ge(fin, kk + 1)
                sp.dma_start(io["out"][:, kk, :], y_out[:, kk, :]).then_inc(stored, 16)
            sp.wait_ge(stored, 16 * KD)

        @block.gpsimd
        def _(pool):
            pool.memset(glu[:, :, :, :], 0.0).then_inc(pads, 1)
            pool.memset(cx[:, :, :, :], 0.0).then_inc(pads, 1)
            for layer in range(DEPTH):
                if layer:
                    pool.wait_ge(chunk_done, PER_LAYER)
                    pool.memset(cx[:, :, :, :], 0.0).then_inc(pads, 1)
                    pool.memset(glu[:, :, :, :], 0.0).then_inc(pads, 1)
                S = streams(layer)
                part, dst = both(sqb[:, 0:SEQ * S], SEQ * S), both(acc[:, 1, 0:SEQ * S], SEQ * S)
                c0 = 2 * CONF_K * layer
                pool.wait_ge(evac, layer * PER_LAYER + LEN["in"])
                for j in range(CONF_K):
                    w = V("conf_w", TAPS * layer + CONF_K + j)
                    src = glu[:, 1, 0:S, j:j + SEQ]
                    if j == 0:
                        pool.tensor_scalar(dst, src, w, V("conf_b", 2 * layer + 1), ALU.mult, ALU.add)\
                            .then_inc(tap_pool, 2)
                        continue
                    pool.wait_ge(tap_pool, c0 + 2 * j)
                    pool.tensor_scalar(part, src, w, 0.0, ALU.mult, ALU.add).then_inc(tap_pool, 1)
                    pool.wait_ge(tap_pool, c0 + 2 * j + 1)
                    pool.tensor_tensor(dst, dst, part, ALU.add).then_inc(tap_pool, 1)

                T = SEQ * S
                n0 = layer * PER_LAYER

                def add(n, idx, o, b):
                    pool.wait_ge(evac, n + idx + 1)
                    dst = branch_sum(layer, o)
                    pool.tensor_tensor(dst, dst, tmp[b][:, 0:T], ALU.add).then_inc(m_sum, 1)
                for idx in range(LEN["sc"]):
                    add(n0 + START["sc"], idx, idx, idx % 2)
                for idx in range(2, LEN["at"], 3):
                    for half in range(2):
                        add(n0 + START["at"], idx, idx // 3 * 2 + half, half)
                for idx in range(LEN["cf"]):
                    add(n0 + START["cf"], idx, idx, idx % 2)

                for f in range(2):
                    p0 = HALF_FF * (2 * layer + f)

                    def hidden_rest(st):
                        if st.idx % 2:
                            pair, b = st.idx // 2, (st.idx // 2) % 2
                            pool.wait_ge(hid_head, st.up(p0 + pair + 1, 2))
                            dst = hid_lo[:, bass.ds(st.up(pair, 2), 1), 0:T].rearrange("p a t -> p (a t)")
                            src = hid_hi[:, bass.ds(st.up(pair, 2), 1), 0:T].rearrange("p a t -> p (a t)")
                            pool.tensor_tensor(dst, sig[b][:, 0:T], src.bitcast(F32), ALU.subtract)\
                                .then_inc(hid_rest, 1)
                    walk(pool, layer, f"up{f}", hidden_rest)

        @block.tensor
        def _(pe):
            def product(out, st, tile, hi, lo, first, last):
                w0 = w_hi[:, st.slot, tile * P:(tile + 1) * P]
                w1 = w_lo[:, st.slot, tile * P:(tile + 1) * P]
                pe.matmul(out, w0, hi, start=first, stop=False)
                pe.matmul(out, w0, lo, start=False, stop=False)
                return pe.matmul(out, w1, hi, start=False, stop=last)

            def begin(st):
                pe.wait_ge(rest_done, st.up(st.n + 1))
                if st.n >= SLOTS:
                    pe.wait_ge(evac, st.up(st.n - SLOTS + 1))

            def from_h(st, T, out):
                for kk in range(KD):
                    mm = product(out, st, kk, h_hi[:, kk, 0:T], h_lo[:, kk, 0:T], kk == 0, kk == KD - 1)
                return mm

            def ada_product(a):
                g, kk = divmod(a, 8)
                if a % 2 == 0:
                    pe.wait_ge(ada_in[a // 2], 16)
                for half in range(2):
                    mm = pe.matmul(psA[2 * g + half][0:2, :], csil[:, kk, :],
                                   ada_first[:, a, half * 512:(half + 1) * 512], start=(kk == 0), stop=(kk == KD - 1))
                mm.then_inc(ada_pe, 1)

            def turn_group(g):
                pe.wait_ge(ada_row, 2 * (g + 1))
                for c in range(KD):
                    mm = pe.matmul(psB[1 + g][:, 2 * c:2 * c + 2], ada_sum[0:2, g, c * P:(c + 1) * P],
                                   mat[0:2, MAT["ident"]:MAT["ident"] + 2], start=True, stop=True)
                mm.then_inc(reduced, 1)

            def reduce_group(g, bank):
                pe.wait_ge(ada_acc, ADA_STEPS[8 * g + 7])
                for c in range(KD):
                    for vv in range(ada_vectors(8 * g)):
                        mm = pe.matmul(bank[:, 2 * c + vv:2 * c + vv + 1], ada_sum[:, vv, c * P:(c + 1) * P],
                                       V("one", 0), start=True, stop=True)
                mm.then_inc(reduced, 1)

            def reduce_in_front(st):
                if st.i is None and st.n in REDUCE:
                    pe.wait_ge(evac, st.n - SLOTS + 1)
                    reduce_group(REDUCE[st.n], psB[st.slot])

            def reduction_read(st, late=0):
                if st.i is None and st.n - late in REDUCE:
                    pe.wait_ge(mod_done, POS[REDUCE[st.n - late]] + 1)

            def lead(layer, name, T, count, hi, lo, ready):
                first = layer * PER_LAYER + START[name]
                sts = [Step(first + j, j) for j in range(AHEAD)]
                for st in sts:
                    begin(st)
                for kk in range(count):
                    pe.wait_ge(ready[0], ready[1] + kk + 1)
                    for st in sts:
                        mm = product(psA[st.slot][:, 0:T], st, kk, hi[:, kk, 0:T], lo[:, kk, 0:T],
                                     kk == 0, kk == count - 1)
                        if kk == count - 1:
                            mm.then_inc(chunk_done, 1)

            def norm_stat(layer, which, T):
                pe.wait_ge(sq_sum, 7 * (2 * layer + which + 1))
                pe.matmul(psB[0][:, 0:T], M("mean"), sqa[:, 0:T], start=True, stop=True).then_inc(stat, 1)

            pe.wait_ge(csil_done, 1)
            for a in range(8):
                ada_product(a)
            pe.wait_ge(mats_in, 16)
            norm_stat(0, 0, NT)
            for a in range(8, ADA_A):
                ada_product(a)
                if a == 11:
                    turn_group(0)
            turn_group(1)

            for layer in range(DEPTH):
                n0 = layer * PER_LAYER
                T = SEQ * streams(layer)
                if layer:
                    norm_stat(layer, 0, NT)
                lead(layer, "in", T, KD, h_hi, h_lo, (h_rest, 16 * layer))
                for idx in range(AHEAD, LEN["in"]):
                    st = Step(n0 + idx, idx)
                    reduce_in_front(st)
                    begin(st)
                    if idx == 5:
                        for tb in range(NT // P):
                            for kk in range(KD):
                                tok = slice(tb * P, (tb + 1) * P)
                                wt = slice(kk * P, (kk + 1) * P)
                                out = psA[st.slot][:, tb * P:(tb + 1) * P]
                                pe.matmul(out, h_hi[:, kk, tok], w_hi[:, st.slot, wt], start=(kk == 0), stop=False)
                                pe.matmul(out, h_hi[:, kk, tok], w_lo[:, st.slot, wt], start=False, stop=False)
                                mm = pe.matmul(out, h_lo[:, kk, tok], w_hi[:, st.slot, wt], start=False,
                                               stop=(kk == KD - 1))
                    else:
                        cols = NT if idx == 4 else T
                        mm = from_h(st, cols, psA[st.slot][:, 0:cols])
                    mm.then_inc(chunk_done, 1)
                    reduction_read(st, 1)
                for j in range(5):
                    pe.wait_ge(evac, n0 + j + 1)
                    if j >= 2:
                        pe.wait_ge(rope, 15 * layer + 3 * (j - 2) + 1)
                    else:
                        pe.wait_ge(evac, n0 + 5)
                    src = q[:, j, 0:SEQ] if j < 4 else k[:, 0:SEQ]
                    pe.matmul(psB[j % 2][:, 0:SEQ], M("rot"), src, start=True, stop=True).then_inc(rot, 1)
                pe.wait_ge(evac, n0 + LEN["in"])
                for tb in range(T // P):
                    for c in range(2):
                        mm = pe.matmul(psA[tb][:, c * 256:(c + 1) * 256], f_in(layer, c)[:, tb * P:(tb + 1) * P],
                                       M("chan", 256), start=True, stop=True)
                    mm.then_inc(fc_mm, 1)
                fc0 = 4 * layer
                pe.wait_ge(fc, fc0 + T // P)
                for s in range(streams(layer)):
                    for c in range(2):
                        out = psA[2 * s + c][:, 0:SEQ]
                        for h in range(2):
                            mid = f_mid(layer, 2 * s + h)
                            for part in range(2):
                                mm = pe.matmul(out, mid[:, c, part * P:(part + 1) * P],
                                               M("pos", SEQ, 512 * h + 256 * part),
                                               start=(h == 0 and part == 0), stop=(h == 1 and part == 1))
                        mm.then_inc(fn_mm, 1)

                un, u0 = units(layer), U0[layer]
                pe.wait_ge(rope, 15 * (layer + 1))
                pe.wait_ge(fn_rest, fc0 + 2 * streams(layer))
                for j in range(len(un) + 2):
                    if j < len(un):
                        s, qi, t, half = un[j]
                        k0, nk = (0, 4) if s == 0 else (2, 2)
                        ps = psA[j % 2]
                        if j >= 2:
                            pe.wait_ge(expd, 2 * (u0 + j - 1))
                        rows = slice(64 * half, 64 * half + 64)
                        q0 = SEQ * s + P * qi
                        mm = pe.matmul(ps[:, 0:nk * P], q[rows, t, q0:q0 + P], k[rows, k0 * P:(k0 + nk) * P],
                                       start=True, stop=True)
                        if s == 0:
                            mm = pe.matmul(ps[:, (1 - qi) * P:(2 - qi) * P], M("ident"), M(f"mask{qi}"),
                                           start=False, stop=True, skip_group_check=True)
                        mm.then_inc(s_mm, 1)
                    if j >= 2:
                        s, qi, t, half = un[j - 2]
                        k0, nk = (0, 4) if s == 0 else (2, 2)
                        pair = (j - 2) // 2
                        pe.wait_ge(pt, u0 + j - 1)
                        if half == 0 and pair >= 2:
                            pe.wait_ge(o_rest, u0 // 2 + pair - 1)
                        for b in range(nk):
                            mm = pe.matmul(psB[pair % 2][64 * half:64 * half + 64, 0:P],
                                           v[:, k0 + b, 64 * half:64 * half + 64],
                                           probT[:, j % 2, b * P:(b + 1) * P], start=(b == 0), stop=(b == nk - 1))
                        mm.then_inc(o_mm, 1)
                    if 1 <= j <= len(un):
                        s = un[j - 1][0]
                        nk = 4 if s == 0 else 2
                        pe.wait_ge(pn, u0 + j)
                        if j >= 3:
                            pe.wait_ge(pt, u0 + j - 2)
                        for b in range(nk):
                            mm = pe.transpose(psA[2 + (j - 1) % 2][:, b * P:(b + 1) * P],
                                              prob[:, (j - 1) % 2, b * P:(b + 1) * P], M("ident"))
                        mm.then_inc(t_mm, 1)

                pe.wait_ge(o_rest, (u0 + len(un)) // 2)

                def merge(st, hi, lo, tiles, wait):
                    reduce_in_front(st)
                    begin(st)
                    from_h(st, T, psA[st.slot][:, 0:T])
                    reduction_read(st)
                    if wait is not None:
                        pe.wait_ge(*wait)
                    for c in range(tiles):
                        mm = product(psB[st.slot][:, 0:T], st, KD + c, hi[:, c, 0:T], lo[:, c, 0:T],
                                     c == 0, c == tiles - 1)
                    mm.then_inc(chunk_done, 1)

                walk(pe, layer, "fn", lambda st: merge(st, y_hi[:, 0:2, :], y_lo[:, 0:2, :], 2, None))
                walk(pe, layer, "sc", lambda st: merge(st, y_hi[:, 2:4, :], y_lo[:, 2:4, :], 2,
                                                       (sc_rest, 2 * layer + 2)), skip=1 - layer)
                m0 = n0 + START["at"]
                pe.wait_ge(evac, m0 - 3)
                pe.wait_ge(tap, CONF_K * (layer + 1))
                pe.wait_ge(tap_pool, 2 * CONF_K * (layer + 1))
                for c in range(2):
                    mm = pe.matmul(psB[m0 % 4][:, 0:T], M("mean"), acc[:, c, 0:T], start=(c == 0), stop=(c == 1))
                mm.then_inc(ln_mean, 1)
                for idx in range(LEN["at"]):
                    st = Step(m0 + idx, idx)
                    reduce_in_front(st)
                    begin(st)
                    if idx % 3 < 2:
                        mm = from_h(st, T, psA[st.slot][:, 0:T])
                        reduction_read(st)
                    else:
                        if idx == 8:
                            pe.wait_ge(ln_xc, 2 * layer + 2)
                        if idx == 11:
                            pe.wait_ge(ln_root, layer + 1)
                        for half, ps in enumerate((psA, psB)):
                            for c in range(4):
                                mm = product(ps[st.slot][:, 0:T], st, 4 * half + c, y_hi[:, 4 + c, 0:T],
                                             y_lo[:, 4 + c, 0:T], c == 0, c == 3)
                    mm.then_inc(chunk_done, 1)
                    if idx == 6:
                        pe.wait_ge(ln_sq, 2 * layer + 2)
                        pe.wait_ge(evac, m0)
                        for c, sq in enumerate((sqb, sqa)):
                            mm = pe.matmul(psB[(m0 + 3) % 4][:, 0:T], M("mean"), sq[:, 0:T],
                                           start=(c == 0), stop=(c == 1))
                        mm.then_inc(ln_var, 1)
                walk(pe, layer, "cf", lambda st: merge(st, yc_hi, yc_lo, 2, (ln_rest, 2 * layer + 2)),
                     skip=2 * (1 - layer))

                def project(st):
                    reduce_in_front(st)
                    begin(st)
                    for kk in range(KD):
                        mm = product(psA[st.slot][:, 0:T], st, kk, mg_hi[:, kk, 0:T], mg_lo[:, kk, 0:T],
                                     kk == 0, kk == KD - 1)
                    mm.then_inc(chunk_done, 1)
                    reduction_read(st, 1)
                lead(layer, "out", T, KD, mg_hi, mg_lo, (m_rest, 8 * layer))
                walk(pe, layer, "out", project, lead=AHEAD)
                norm_stat(layer, 1, T)

                for f in range(2):
                    def lift(st):
                        reduce_in_front(st)
                        begin(st)
                        from_h(st, T, psA[st.slot][:, 0:T]).then_inc(chunk_done, 1)
                        reduction_read(st, 1)
                    straight = LEN["up0"] if layer == 0 else 0
                    if f == 0:
                        lead(layer, "up0", T, KD, h_hi, h_lo, (h_rest, 8 * (2 * layer + 1)))
                        walk(pe, layer, "up0", lift, lead=AHEAD, skip=straight)
                    else:
                        walk(pe, layer, "up1", lift, skip=straight)

                    def lower(st):
                        begin(st)
                        for c in range(HALF_FF):
                            mm = product(psA[st.slot][:, 0:T], st, c, hid_hi[:, c, 0:T], hid_lo[:, c, 0:T],
                                         c == 0, c == HALF_FF - 1)
                        mm.then_inc(chunk_done, 1)
                    name = f"dn{f}"
                    lead(layer, name, T, HALF_FF, hid_hi, hid_lo, (hid_rest, HALF_FF * (2 * layer + f)))
                    walk(pe, layer, name, lower, lead=AHEAD)
            pe.wait_ge(sq_sum, 7 * (2 * DEPTH + 1))
            pe.matmul(psB[0][:, 0:SEQ], M("mean"), sqa[:, 0:SEQ], start=True, stop=True).then_inc(stat, 1)

        @block.scalar
        def _(act):
            def head(st, tiles):
                if st.i is None and st.n + AHEAD >= TOTAL:
                    return
                r, full = st.filled("w", AHEAD)
                act.wait_ge(raw_full[r], full)
                if st.n >= 1:
                    act.wait_ge(chunk_done, st.up(st.n))
                s = (st.n + AHEAD) % SLOTS
                act.activation(w_hi[:, s, 0:tiles * P], raw[:, r, 0:tiles * P], ACT.Copy).then_inc(head_done, 1)

            def size(st, layer, name):
                return SIZE[START[name]] if st.i is not None else SIZE[(st.n + AHEAD) % PER_LAYER]

            def square(count, o, T, direct, before):
                if before is not None:
                    act.wait_ge(*before)
                if count % 8 >= 2:
                    act.wait_ge(sq_sum, 7 * (count // 8) + count % 8 - 1)
                src = X[:, o, 0:T] if isinstance(o, int) else X[:, bass.ds(o, 1), 0:T].rearrange("p a t -> p (a t)")
                act.activation((sqa if direct else sqb)[:, 0:T], src, ACT.Square).then_inc(sq_done, 1)

            def norm(layer, which, T):
                r = 2 * layer + which
                act.wait_ge(stat, r + 1)
                act.wait_ge(sq_sum, 7 * (r + 1))
                act.activation(sqb[:, 0:T], psB[0][:, 0:T], ACT.Sqrt, bias=V("eps", 0)).then_inc(root, 1)
                for kk in range(KD):
                    act.wait_ge(ht, 8 * r + kk + 1)
                    for s in range(T // SEQ):
                        cols = slice(s * SEQ, (s + 1) * SEQ)
                        op = act.activation(h_hi[:, kk, cols], tmp[kk % 2][:, cols], ACT.Identity,
                                            bias=mod[:, layer, 24 * which + kk, s:s + 1])
                    op.then_inc(h_head, 1)

            for kk in range(4):
                act.dma_start(X[:, 2 * kk:2 * kk + 2, :], io["x"][:, 2 * kk:2 * kk + 2, :]).then_inc(x_full, 16)
            act.dma_start(mat[:, :], io["mat"]).then_inc(mats_in, 16)
            act.wait_ge(vecs_in, 16)
            act.activation(csil[:, :, :].rearrange("p k c -> p (k c)"), vec[:, VEC["cc"]:VEC["cc"] + 2 * KD],
                           ACT.Silu).then_inc(csil_done, 1)
            act.wait_ge(x_full, 64)
            for kk in range(KD):
                square(kk, kk, NT, kk == 0, None)
            for g in range(2):
                act.wait_ge(ada_pe, 8 * (g + 1))
                for half in range(2):
                    act.activation(ada_sum[0:2, g, half * 512:(half + 1) * 512], psA[2 * g + half][0:2, :], ACT.Copy)\
                        .then_inc(ada_row, 1)
            for ahead in range(AHEAD):
                head(Step(ahead - AHEAD, 0), 8)

            for layer in range(DEPTH):
                n0 = layer * PER_LAYER
                T = SEQ * streams(layer)
                norm(layer, 0, NT)
                for idx in range(LEN["in"]):
                    st = Step(n0 + idx, idx)
                    head(st, size(st, layer, "in"))
                    if idx in (14, 16):
                        act.wait_ge(chunk_done, st.n + 1)
                        act.activation(sig[(idx - 14) // 2][:, 0:T], psA[st.slot][:, 0:T], ACT.Sigmoid)\
                            .then_inc(sigd, 1)
                fc0 = 4 * layer
                for tb in range(T // P):
                    act.wait_ge(fc_mm, fc0 + tb + 1)
                    act.activation(f_mid(layer, tb), psA[tb][:, :].rearrange("p (c n) -> p c n", c=2), ACT.Copy)\
                        .then_inc(fc, 1)
                for j in range(2 * streams(layer)):
                    s, c = divmod(j, 2)
                    act.wait_ge(fn_mm, fc0 + j + 1)
                    act.activation(y_hi[:, c, s * SEQ:(s + 1) * SEQ], psA[j][:, 0:SEQ], ACT.Copy)\
                        .then_inc(fn_head, 1)
                for c in range(2):
                    act.wait_ge(sc_step, 8 * layer + 7 + c)
                    act.activation(y_hi[:, 2 + c, 0:T], pc[:, c, 0:T], ACT.Copy).then_inc(sc_head, 1)

                un, u0 = units(layer), U0[layer]
                act.wait_ge(nsink_done, 1)
                for j in range(len(un) + 3):
                    if j < len(un):
                        s, qi, t, half = un[j]
                        width = (4 if s == 0 else 2) * P
                        h = layer * N_HEADS + t + 4 * half
                        act.wait_ge(negm, 2 * (u0 + j + 1))
                        if j >= 2:
                            act.wait_ge(t_mm, u0 + j - 1)
                        act.activation(prob[:, j % 2, 0:width], psA[j % 2][:, 0:width], ACT.Exp,
                                       bias=small[:, j % 2, 1:2], scale=HEAD ** -0.5,
                                       accum_out=small[:, j % 2, 2:3]).then_inc(expd, 1)
                        act.activation(small[:, j % 2, 3:4], nsink[:, h:h + 1], ACT.Exp,
                                       bias=small[:, j % 2, 1:2], scale=-1.0).then_inc(expd, 1)
                    if 1 <= j <= len(un):
                        width = (4 if un[j - 1][0] == 0 else 2) * P
                        act.wait_ge(t_mm, u0 + j)
                        if j >= 3:
                            act.wait_ge(o_mm, u0 + j - 2)
                        act.activation(probT[:, (j - 1) % 2, 0:width], psA[2 + (j - 1) % 2][:, 0:width], ACT.Copy)\
                            .then_inc(pt, 1)
                    if j >= 3 and j % 2 == 1:
                        pair = (j - 3) // 2
                        s, qi, t, _ = un[2 * pair]
                        c0 = SEQ * s + P * qi
                        act.wait_ge(o_mm, u0 + 2 * pair + 2)
                        if pair == 0:
                            act.wait_ge(sc_rest, 2 * layer + 2)
                        act.activation(y_hi[:, 4 + t, c0:c0 + P], psB[pair % 2][:, 0:P], ACT.Copy)\
                            .then_inc(o_head, 1)

                s0 = 34 * layer + 2

                def gate(name, b):
                    def step(st):
                        head(st, size(st, layer, name))
                        act.wait_ge(chunk_done, st.up(st.n + 1))
                        act.wait_ge(evac, st.up(st.n - (st.idx > 0)))
                        act.activation(sig[st.n % 2][:, 0:T], psA[st.slot][:, 0:T], ACT.Sigmoid).then_inc(sigd, 1)
                        if name == "cf" and st.i is None and st.idx > 0:
                            merged_head(st.idx - 1)
                    return step

                def merged_head(o):
                    act.wait_ge(m_sum, 24 * layer + 16 + o + 1)
                    act.activation(mg_hi[:, o, 0:T], branch_sum(layer, o), ACT.Copy).then_inc(m_head, 1)

                walk(act, layer, "fn", gate("fn", 0), keep=AHEAD)
                walk(act, layer, "sc", gate("sc", 1), keep=AHEAD)
                m0 = n0 + START["at"]
                for idx in range(LEN["at"]):
                    st = Step(m0 + idx, idx)
                    head(st, size(st, layer, "at"))
                    if idx % 3 < 2:
                        o = idx // 3 * 2 + idx % 3
                        act.wait_ge(chunk_done, st.n + 1)
                        act.wait_ge(evac, m0 if o < 2 else m0 + o // 2 * 3)
                        act.activation(sig[o % 2][:, 0:T], psA[st.slot][:, 0:T], ACT.Sigmoid).then_inc(sigd, 1)
                    if idx == 2:
                        for c, sq in enumerate((sqb, sqa)):
                            act.wait_ge(ln_xc, 2 * layer + c + 1)
                            act.activation(sq[:, 0:T], acc[:, c, 0:T], ACT.Square).then_inc(ln_sq, 1)
                    if idx == 7:
                        act.wait_ge(ln_var, layer + 1)
                        act.activation(sqb[:, 0:T], psB[(m0 + 3) % 4][:, 0:T], ACT.Sqrt, bias=V("eps", 0),
                                       scale=float(D // CONF_W)).then_inc(ln_root, 1)
                    if idx == 9:
                        for c in range(2):
                            act.wait_ge(ln_n, 2 * layer + c + 1)
                            act.activation(acc[:, c, 0:T], acc[:, c, 0:T], ACT.Silu, bias=V("ln_b", 2 * layer + c),
                                           scale=V("ln_g", 2 * layer + c)).then_inc(ln_silu, 1)
                        for c in range(2):
                            act.wait_ge(ln_silu, 2 * layer + c + 1)
                            act.activation(yc_hi[:, c, 0:T], acc[:, c, 0:T], ACT.Copy).then_inc(ln_head, 1)
                for idx in range(LEN["cf"]):
                    gate("cf", 3)(Step(n0 + START["cf"] + idx, idx))
                merged_head(KD - 1)

                def squares(name, r):
                    def step(st):
                        head(st, size(st, layer, name))
                        o = st.up(st.idx)
                        square(8 * r + st.idx, o, T, st.idx == 0, (evac, st.up(st.n + 1)))
                    return step
                for idx in range(LEN["out"]):
                    squares("out", 2 * layer + 1)(Step(n0 + START["out"] + idx, idx))
                norm(layer, 1, T)

                for f in range(2):
                    p0 = HALF_FF * (2 * layer + f)

                    def hidden_head(n, pair, b):
                        act.wait_ge(evac, n)
                        dst = hid_hi[:, bass.ds(pair, 1), 0:T].rearrange("p a t -> p (a t)")
                        act.activation(dst, sig[b][:, 0:T], ACT.Copy).then_inc(hid_head, 1)

                    def lift(st):
                        head(st, size(st, layer, f"up{f}"))
                        pair, b = st.idx // 2, (st.idx // 2) % 2
                        if st.idx % 2 == 0:
                            if st.i is not None or st.idx:
                                hidden_head(st.up(st.n), st.up(pair - 1, 2), 1 - b)
                            act.wait_ge(chunk_done, st.up(st.n + 1))
                            act.wait_ge(evac, st.up(st.n - 2))
                            act.activation(tmp[b][:, 0:T], psA[st.slot][:, 0:T], ACT.Identity,
                                           bias=Vd("ffn_b", st.up(p0 + pair, 2)),
                                           scale=Vd("ffn_w", st.up(3 * (p0 + pair) + 1, 6))).then_inc(cv, 1)
                        else:
                            act.wait_ge(evac, st.up(st.n))
                            act.activation(tmp[b][:, 0:T], tmp[b][:, 0:T], ACT.Silu).then_inc(silu, 1)
                    walk(act, layer, f"up{f}", lift, skip=1 if layer else LEN["up0"], keep=AHEAD)
                    hidden_head(n0 + START[f"dn{f}"], HALF_FF - 1, (HALF_FF - 1) % 2)
                    if f == 0:
                        walk(act, layer, "dn0", lambda st: head(st, size(st, layer, "dn0")), keep=AHEAD)
                    else:
                        for idx in range(LEN["dn1"]):
                            squares("dn1", 2 * layer + 2)(Step(n0 + START["dn1"] + idx, idx))
            act.wait_ge(stat, 2 * DEPTH + 1)
            act.wait_ge(sq_sum, 7 * (2 * DEPTH + 1))
            act.activation(sqb[:, 0:SEQ], psB[0][:, 0:SEQ], ACT.Sqrt, bias=V("eps", 0)).then_inc(root, 1)

        @block.vector
        def _(dve):
            def rest(st, tiles):
                if st.i is None and st.n + AHEAD >= TOTAL:
                    return
                s = (st.n + AHEAD) % SLOTS
                r, _ = st.filled("w", AHEAD)
                dve.wait_ge(head_done, st.up(st.n + AHEAD + 1))
                dve.tensor_tensor(w_lo[:, s, 0:tiles * P], raw[:, r, 0:tiles * P],
                                  w_hi[:, s, 0:tiles * P].bitcast(F32), ALU.subtract).then_inc(rest_done, 1)

            def size(st, name):
                return SIZE[START[name]] if st.i is not None else SIZE[(st.n + AHEAD) % PER_LAYER]

            def ada_step(a):
                p, g, kk = PLACE[("ada", a)], a // 8, a % 8
                dve.wait_ge(raw_full[p % SLOTS], 16 * (p // SLOTS + 1))
                if kk == 0:
                    dve.wait_ge(reduced, POS[g])
                else:
                    dve.wait_ge(ada_acc, ADA_STEPS[a] - ada_vectors(a))
                for vv in range(ada_vectors(a)):
                    w, dst, c = raw[:, p % SLOTS, 0:KD * P], ada_sum[:, vv, :], csil[:, kk, vv:vv + 1]
                    if kk == 0:
                        op = dve.tensor_scalar(dst, w, c, None, ALU.mult)
                    else:
                        op = dve.scalar_tensor_tensor(dst, w, c, dst, ALU.mult, ALU.add)
                    op.then_inc(ada_acc, 1)

            def read_mod(g, bank):
                dve.wait_ge(reduced, POS[g] + 1)
                layer, c0 = g // 6, KD * (g % 6)
                b = VEC["b_ada"] + KD * g
                vs = ada_vectors(8 * g)
                ps = bank[:, 0:2 * KD].rearrange("p (c v) -> p v c", v=2)[:, 0:vs, :]
                for vv in range(vs):
                    op = dve.tensor_tensor(mod[:, layer, c0:c0 + KD, vv], ps[:, vv, :], vec[:, b:b + KD], ALU.add)
                op.then_inc(mod_done, 1)
                if g % 6 in (1, 4):
                    dve.wait_ge(mod_done, POS[g] + 1)
                    which = g % 6 // 3
                    gv = VEC["g_mix" if which == 0 else "g_ffn"] + KD * layer
                    for vv in range(2):
                        if vv < vs:
                            op = dve.scalar_tensor_tensor(gsc[:, which, vv, :], mod[:, layer, c0:c0 + KD, vv],
                                                          1.0, vec[:, gv:gv + KD], ALU.add, ALU.mult)
                    op.then_inc(gsc_done, 1)

            def ada_behind(st):
                if st.i is None:
                    if st.n + 1 in REDUCE:
                        read_mod(REDUCE[st.n + 1], psB[(st.n + 1) % SLOTS])
                    if st.n in ADA_AT:
                        ada_step(ADA_AT[st.n])

            def add_square(count, T):
                r, o = divmod(count, 8)
                if o:
                    dve.wait_ge(sq_done, count + 1)
                    if o > 1:
                        dve.wait_ge(sq_sum, 7 * r + o - 1)
                    dve.tensor_tensor(sqa[:, 0:T], sqa[:, 0:T], sqb[:, 0:T], ALU.add).then_inc(sq_sum, 1)

            def norm(layer, which, T):
                r = 2 * layer + which
                dve.wait_ge(root, r + 1)
                dve.reciprocal(sqb[:, 0:T], sqb[:, 0:T]).then_inc(inv, 1)
                dve.wait_ge(inv, r + 1)
                dve.wait_ge(gsc_done, r + 1)
                for kk in range(KD + 1):
                    if kk < KD:
                        if kk >= 2:
                            dve.wait_ge(h_rest, 8 * r + kk - 1)
                        for s in range(T // SEQ):
                            cols = slice(s * SEQ, (s + 1) * SEQ)
                            op = dve.scalar_tensor_tensor(tmp[kk % 2][:, cols], X[:, kk, cols],
                                                          gsc[:, which, s, kk:kk + 1], sqb[:, cols],
                                                          ALU.mult, ALU.mult)
                        op.then_inc(ht, 1)
                    if kk >= 1:
                        c = kk - 1
                        dve.wait_ge(h_head, 8 * r + c + 1)
                        for s in range(T // SEQ):
                            cols = slice(s * SEQ, (s + 1) * SEQ)
                            op = dve.scalar_tensor_tensor(h_lo[:, c, cols], tmp[c % 2][:, cols],
                                                          mod[:, layer, 24 * which + c, s:s + 1],
                                                          h_hi[:, c, cols].bitcast(F32), ALU.add, ALU.subtract)
                        op.then_inc(h_rest, 1)

            dve.wait_ge(vecs_in, 16)
            dve.tensor_scalar(nsink[:, :], vec[:, VEC["sink"]:VEC["sink"] + DEPTH * N_HEADS], -1.0, None, ALU.mult)\
                .then_inc(nsink_done, 1)
            for kk in range(KD):
                add_square(kk, NT)
            for g in range(2):
                read_mod(g, psB[1 + g])
            for ahead in range(AHEAD):
                rest(Step(ahead - AHEAD, 0), 8)

            for layer in range(DEPTH):
                n0 = layer * PER_LAYER
                S = streams(layer)
                T = SEQ * S
                norm(layer, 0, NT)
                dve.wait_ge(pads, 2 * (layer + 1))
                for idx in range(LEN["in"]):
                    st = Step(n0 + idx, idx)
                    rest(st, size(st, "in"))
                    ps = psA[st.slot]
                    if idx in (14, 16):
                        continue
                    dve.wait_ge(chunk_done, st.n + 1)
                    if idx < 4:
                        dve.tensor_copy(q[:, idx, 0:T], ps[:, 0:T]).then_inc(evac, 1)
                    elif idx == 4:
                        dve.tensor_copy(k[:, :], ps[:, :]).then_inc(evac, 1)
                    elif idx == 5:
                        dve.tensor_copy(v[:, :, :].rearrange("p b n -> p (b n)"), ps[:, :]).then_inc(evac, 1)
                    elif idx < 8:
                        dve.tensor_copy(f_in(layer, idx - 6), ps[:, 0:T]).then_inc(evac, 1)
                    elif idx in (8, 10):
                        dve.tensor_copy(pc[:, (idx - 8) // 2, 0:T], ps[:, 0:T]).then_inc(evac, 1)
                    elif idx in (9, 11):
                        c = (idx - 9) // 2
                        dve.wait_ge(evac, st.n)
                        dve.tensor_tensor(cx[:, c, 0:S, 1:1 + SEQ], both(ps[:, 0:T], T), both(pc[:, c, 0:T], T),
                                          ALU.mult).then_inc(evac, 1)
                    elif idx in (12, 13):
                        dve.tensor_copy(pb[:, idx - 12, 0:T], ps[:, 0:T]).then_inc(evac, 1)
                    else:
                        c = (idx - 15) // 2
                        dve.wait_ge(sigd, 34 * layer + c + 1)
                        dve.tensor_tensor(glu[:, c, 0:S, PAD:PAD + SEQ], both(ps[:, 0:T], T),
                                          both(sig[c][:, 0:T], T), ALU.mult).then_inc(evac, 2)
                    ada_behind(st)
                for j in range(5):
                    dst = q[:, j, 0:SEQ] if j < 4 else k[:, 0:SEQ]
                    r = 15 * layer + 3 * j
                    dve.wait_ge(rot, 5 * layer + j + 1)
                    if j >= 2:
                        dve.wait_ge(rope, r - 3)
                    dve.tensor_tensor(tmp[j % 2][:, 0:SEQ], psB[j % 2][:, 0:SEQ], M("sin", SEQ), ALU.mult)\
                        .then_inc(rope, 1)
                    dve.tensor_tensor(dst, dst, M("cos", SEQ), ALU.mult).then_inc(rope, 1)
                    dve.wait_ge(rope, r + 2)
                    dve.tensor_tensor(dst, dst, tmp[j % 2][:, 0:SEQ], ALU.add).then_inc(rope, 1)
                fc0 = 4 * layer
                for step in range(4):
                    for c in range(2):
                        w = 3 * (2 * layer + c)
                        u = both(pc[:, c, 0:T], T)
                        if step:
                            dve.wait_ge(sc_step, 8 * layer + 2 * step - 1 + c)
                        if step == 0:
                            op = dve.tensor_scalar(u, cx[:, c, 0:S, 0:SEQ], V("sc_w", w), None, ALU.mult)
                        elif step < 3:
                            op = dve.scalar_tensor_tensor(u, cx[:, c, 0:S, step:step + SEQ], V("sc_w", w + step), u,
                                                          ALU.mult, ALU.add)
                        else:
                            op = dve.tensor_tensor(u, u, both(pb[:, c, 0:T], T), ALU.mult)
                        op.then_inc(sc_step, 1)
                for j in range(2 * S):
                    s, c = divmod(j, 2)
                    dve.wait_ge(fn_head, fc0 + j + 1)
                    dve.tensor_tensor(y_lo[:, c, s * SEQ:(s + 1) * SEQ], psA[j][:, 0:SEQ],
                                      y_hi[:, c, s * SEQ:(s + 1) * SEQ].bitcast(F32), ALU.subtract)\
                        .then_inc(fn_rest, 1)
                for c in range(2):
                    dve.wait_ge(sc_head, 2 * layer + c + 1)
                    dve.tensor_tensor(y_lo[:, 2 + c, 0:T], pc[:, c, 0:T], y_hi[:, 2 + c, 0:T].bitcast(F32),
                                      ALU.subtract).then_inc(sc_rest, 1)

                def conv_tap(j):
                    w = V("conf_w", TAPS * layer + j)
                    src, dst = glu[:, 0, 0:S, j:j + SEQ], both(acc[:, 0, 0:T], T)
                    if j == 0:
                        op = dve.tensor_scalar(dst, src, w, V("conf_b", 2 * layer), ALU.mult, ALU.add)
                    else:
                        dve.wait_ge(tap, CONF_K * layer + j)
                        op = dve.scalar_tensor_tensor(dst, src, w, dst, ALU.mult, ALU.add)
                    op.then_inc(tap, 1)

                un, u0 = units(layer), U0[layer]
                per = -(-CONF_K // len(un))
                todo = 0
                for j in range(len(un) + 4):
                    if j < len(un):
                        s, qi, t, half = un[j]
                        width = (4 if s == 0 else 2) * P
                        h = layer * N_HEADS + t + 4 * half
                        dve.wait_ge(s_mm, u0 + j + 1)
                        dve.tensor_reduce(small[:, j % 2, 0:1], psA[j % 2][:, 0:width], AX.X, ALU.max)\
                            .then_inc(negm, 1)
                        dve.wait_ge(negm, 2 * (u0 + j) + 1)
                        dve.tensor_scalar(small[:, j % 2, 1:2], small[:, j % 2, 0:1], -HEAD ** -0.5,
                                          nsink[:, h:h + 1], ALU.mult, ALU.min).then_inc(negm, 1)
                    if 1 <= j <= len(un):
                        b = (j - 1) % 2
                        width = (4 if un[j - 1][0] == 0 else 2) * P
                        dve.wait_ge(expd, 2 * (u0 + j))
                        dve.tensor_tensor(small[:, b, 4:5], small[:, b, 2:3], small[:, b, 3:4], ALU.add)\
                            .then_inc(den, 1)
                        dve.wait_ge(den, 2 * (u0 + j - 1) + 1)
                        dve.reciprocal(small[:, b, 4:5], small[:, b, 4:5]).then_inc(den, 1)
                        dve.wait_ge(den, 2 * (u0 + j))
                        dve.tensor_scalar(prob[:, b, 0:width], prob[:, b, 0:width], small[:, b, 4:5], None,
                                          ALU.mult).then_inc(pn, 1)
                    for _ in range(per):
                        if todo < CONF_K:
                            conv_tap(todo)
                            todo += 1
                    if j >= 4 and j % 2 == 0:
                        pair = (j - 4) // 2
                        s, qi, t, _ = un[2 * pair]
                        c0 = SEQ * s + P * qi
                        dve.wait_ge(o_head, u0 // 2 + pair + 1)
                        dve.tensor_tensor(y_lo[:, 4 + t, c0:c0 + P], psB[pair % 2][:, 0:P],
                                          y_hi[:, 4 + t, c0:c0 + P].bitcast(F32), ALU.subtract).then_inc(o_rest, 1)

                def dyn_sum(st_o):
                    c0 = 0 if layer == 0 else SEQ
                    if isinstance(st_o, int):
                        return X[:, st_o, c0:c0 + T]
                    return X[:, bass.ds(st_o, 1), c0:c0 + T].rearrange("p a t -> p (a t)")

                def branch(name, b):
                    def step(st):
                        rest(st, size(st, name))
                        if name == "cf" and st.idx > 0:
                            merged_rest(st.idx - 1)
                        o = st.up(st.idx)
                        dve.wait_ge(sigd, st.up(34 * layer + 2 + 8 * b + st.idx + 1))
                        dve.wait_ge(chunk_done, st.up(st.n + 1))
                        ps, sg = psB[st.slot][:, 0:T], sig[st.n % 2][:, 0:T]
                        if b == 0:
                            dve.tensor_tensor(dyn_sum(o), ps, sg, ALU.mult).then_inc(evac, 1)
                        else:
                            g = 8 * (b - 1) + st.idx
                            if g >= 2:
                                dve.wait_ge(m_sum, st.up(24 * layer + g - (st.idx > 0)))
                            t = tmp[st.n % 2][:, 0:T]
                            dve.tensor_tensor(t, ps, sg, ALU.mult).then_inc(evac, 1)
                        if layer == 0:
                            ada_behind(st)
                    return step

                def merged_rest(o):
                    dve.wait_ge(m_head, 8 * layer + o + 1)
                    dve.tensor_tensor(mg_lo[:, o, 0:T], branch_sum(layer, o), mg_hi[:, o, 0:T].bitcast(F32),
                                      ALU.subtract).then_inc(m_rest, 1)

                walk(dve, layer, "fn", branch("fn", 0), keep=AHEAD)
                walk(dve, layer, "sc", branch("sc", 1), keep=AHEAD)
                m0 = n0 + START["at"]
                for idx in range(LEN["at"]):
                    st = Step(m0 + idx, idx)
                    rest(st, size(st, "at"))
                    if idx == 1:
                        dve.wait_ge(ln_mean, layer + 1)
                        for c in range(2):
                            dve.scalar_tensor_tensor(acc[:, c, 0:T], psB[m0 % 4][:, 0:T], -float(D // CONF_W),
                                                     acc[:, c, 0:T], ALU.mult, ALU.add).then_inc(ln_xc, 1)
                    if idx % 3 == 2:
                        for half, ps in enumerate((psA, psB)):
                            o = idx // 3 * 2 + half
                            if half == 0:
                                dve.wait_ge(sigd, 34 * layer + 2 + 16 + o + 2)
                                dve.wait_ge(chunk_done, st.n + 1)
                                dve.wait_ge(m_sum, 24 * layer + 8 + o)
                            t = tmp[half][:, 0:T]
                            op = dve.tensor_tensor(t, ps[st.slot][:, 0:T], sig[half][:, 0:T], ALU.mult)
                        op.then_inc(evac, 3)
                    if layer == 0:
                        ada_behind(st)
                    if idx == 8:
                        dve.wait_ge(ln_root, layer + 1)
                        dve.reciprocal(sqb[:, 0:T], sqb[:, 0:T]).then_inc(ln_inv, 1)
                        dve.wait_ge(ln_inv, layer + 1)
                        for c in range(2):
                            dve.tensor_tensor(acc[:, c, 0:T], acc[:, c, 0:T], sqb[:, 0:T], ALU.mult)\
                                .then_inc(ln_n, 1)
                    if idx == 10:
                        for c in range(2):
                            dve.wait_ge(ln_head, 2 * layer + c + 1)
                            dve.tensor_tensor(yc_lo[:, c, 0:T], acc[:, c, 0:T], yc_hi[:, c, 0:T].bitcast(F32),
                                              ALU.subtract).then_inc(ln_rest, 1)
                for idx in range(LEN["cf"]):
                    branch("cf", 3)(Step(n0 + START["cf"] + idx, idx))
                merged_rest(KD - 1)

                def residual(name, which, r, ada_col):
                    def step(st):
                        rest(st, size(st, name))
                        if r is not None and st.idx > 0:
                            add_square(8 * r + st.idx - 1, T)
                        dve.wait_ge(chunk_done, st.up(st.n + 1))
                        o = st.up(st.idx)
                        for s in range(S):
                            cols = slice(s * SEQ, (s + 1) * SEQ)
                            old = x_in if layer == 0 and name == "out" else X
                            if st.i is None:
                                dst, src = X[:, st.idx, cols], old[:, st.idx, cols]
                                g = mod[:, layer, ada_col + st.idx, s:s + 1]
                            else:
                                dst = X[:, bass.ds(o, 1), cols].rearrange("p a t -> p (a t)")
                                src = dst
                                g = mod[:, layer, bass.ds(o + ada_col, 1), s:s + 1].rearrange("p a b -> p (a b)")
                            op = dve.scalar_tensor_tensor(dst, psA[st.slot][:, cols], g, src, ALU.mult, ALU.add)
                        op.then_inc(evac, 1)
                        if layer == 0:
                            ada_behind(st)
                    return step

                if layer == 0:
                    dve.wait_ge(x_again, 16)
                for idx in range(LEN["out"]):
                    residual("out", 1, 2 * layer + 1, 16)(Step(n0 + START["out"] + idx, idx))
                add_square(8 * (2 * layer + 1) + 7, T)
                norm(layer, 1, T)

                for f in range(2):
                    p0 = HALF_FF * (2 * layer + f)

                    def lift(st):
                        rest(st, size(st, f"up{f}"))
                        pair, b = st.idx // 2, (st.idx // 2) % 2
                        ps = psA[st.slot][:, 0:T]
                        dve.wait_ge(chunk_done, st.up(st.n + 1))
                        if st.idx % 2 == 0:
                            w = 3 * p0 + 3 * pair
                            c0 = 2 * p0 + 2 * pair
                            t3, p3 = both(tmp[b][:, 0:T], T), both(ps, T)
                            dve.wait_ge(cv, st.up(c0 + 1, 4))
                            dve.scalar_tensor_tensor(t3[:, :, 1:SEQ], p3[:, :, 0:SEQ - 1], Vd("ffn_w", st.up(w, 6)),
                                                     t3[:, :, 1:SEQ], ALU.mult, ALU.add).then_inc(cv, 1)
                            dve.wait_ge(cv, st.up(c0 + 2, 4))
                            dve.scalar_tensor_tensor(t3[:, :, 0:SEQ - 1], p3[:, :, 1:SEQ],
                                                     Vd("ffn_w", st.up(w + 2, 6)), t3[:, :, 0:SEQ - 1],
                                                     ALU.mult, ALU.add).then_inc(evac, 1)
                        else:
                            dve.wait_ge(silu, st.up(p0 + pair + 1, 2))
                            if st.i is not None or pair >= 2:
                                dve.wait_ge(hid_rest, st.up(p0 + pair - 1, 2))
                            dve.tensor_tensor(sig[b][:, 0:T], ps, tmp[b][:, 0:T], ALU.mult).then_inc(evac, 1)
                        if layer == 0:
                            ada_behind(st)
                    walk(dve, layer, f"up{f}", lift, skip=1 if layer else LEN["up0"], keep=AHEAD)
                    name = f"dn{f}"
                    if f == 0:
                        walk(dve, layer, name, residual(name, 1, None, 40), keep=AHEAD)
                    else:
                        for idx in range(LEN[name]):
                            residual(name, 1, 2 * layer + 2, 40)(Step(n0 + START[name] + idx, idx))
                        add_square(8 * (2 * layer + 2) + 7, T)
            dve.wait_ge(root, 2 * DEPTH + 1)
            dve.reciprocal(sqb[:, 0:SEQ], sqb[:, 0:SEQ]).then_inc(inv, 1)
            dve.wait_ge(inv, 2 * DEPTH + 1)
            for kk in range(KD):
                dve.scalar_tensor_tensor(y_out[:, kk, :], X[:, kk, 0:SEQ], V("g_final", kk), sqb[:, 0:SEQ],
                                         ALU.mult, ALU.mult).then_inc(fin, 1)


def constants():
    import numpy as np
    m = np.zeros((P, NMAT), np.float64)

    def put(name, a, off=0):
        m[:a.shape[0], MAT[name] + off:MAT[name] + off + a.shape[1]] = a
    put("ident", np.eye(P))
    put("mean", np.full((P, P), 1.0 / D))
    r = np.zeros((P, P))
    for g in range(P // 32):
        for j in range(16):
            a, b = 32 * g + j, 32 * g + 16 + j
            r[b, a] = -1.0
            r[a, b] = 1.0
    put("rot", r)
    i = np.arange(P)
    put("mask0", np.where(i[None, :] <= i[:, None], 0.0, -1e30))
    put("mask1", np.where(i[None, :] >= i[:, None], 0.0, -1e30))
    c = np.arange(64)
    ang = 2 * np.pi * np.outer(c, c) / 64
    put("chan", np.kron(np.eye(2), np.cos(ang)))
    put("chan", np.kron(np.eye(2), np.sin(ang)), 128)
    n = np.arange(SEQ)
    ang = 2 * np.pi * (np.outer(n, n) % SEQ) / SEQ
    scale = 1.0 / np.sqrt(SEQ * 64)
    for h in range(2):
        put("pos", np.cos(ang)[h * P:(h + 1) * P] * scale, 512 * h)
        put("pos", -np.sin(ang)[h * P:(h + 1) * P] * scale, 512 * h + 256)
    m = m.astype(np.float32)
    inv = np.float32(10000.0) ** (-np.arange(16, dtype=np.float32) / np.float32(16))
    pos = np.stack([n // 64, n % 64]).astype(np.float32)
    a = np.zeros((64, SEQ), np.float32)
    for axis in range(2):
        for half in range(2):
            a[axis * 32 + half * 16:axis * 32 + half * 16 + 16] = pos[axis][None, :] * inv[:, None]
    m[:, MAT["cos"]:MAT["cos"] + SEQ] = np.tile(np.cos(a), (2, 1))
    m[:, MAT["sin"]:MAT["sin"] + SEQ] = np.tile(np.sin(a), (2, 1))
    return m


def kernel(**inputs):
    import numpy as np
    import concourse.bacc as bacc
    from concourse.bass_utils import run_bass_kernel_spmd as run

    a = {name: np.asarray(x) for name, x in inputs.items()}

    def tiles(w):
        kk, mm = w.shape
        return w.reshape(kk // P, P, mm // P, P).transpose(2, 0, 1, 3)

    def chunks(t):
        n, c = t.shape[:2]
        return np.ascontiguousarray(t.transpose(0, 2, 1, 3).reshape(n, P, c * P))

    def channels(x):
        return x.T.reshape(-1, P, x.shape[0]).transpose(1, 0, 2)

    arrays = {"mat": constants()}
    heads = np.concatenate([np.arange(HEAD) + HEAD * h for t in range(4) for h in (t, t + 4)])
    arrays["x"] = np.ascontiguousarray(np.concatenate([channels(a["x"][0]), channels(a["ctx"][0])], axis=2))
    vec = np.zeros((P, NVEC), np.float32)

    def put(name, cols, off=0):
        vec[:, VEC[name] + off:VEC[name] + off + cols.shape[1]] = cols
    put("cc", np.stack([a["c"][0].reshape(KD, P), a["c_ctx"].reshape(KD, P)], 2).transpose(1, 0, 2).reshape(P, -1))
    put("b_ada", a["b_ada"].reshape(-1, P).T)
    put("g_mix", a["g_mix"].reshape(-1, P).T)
    put("g_ffn", a["g_ffn"].reshape(-1, P).T)
    put("g_final", a["g_final"].reshape(-1, P).T)
    put("sink", np.broadcast_to(a["attn_sink"].reshape(1, -1), (P, DEPTH * N_HEADS)))
    put("conf_w", a["conf_dw_w"].reshape(DEPTH, CONF_K, 2, P).transpose(3, 0, 2, 1).reshape(P, -1))
    put("conf_b", a["conf_dw_b"].reshape(-1, P).T)
    put("ln_g", a["conf_ln_g"].reshape(-1, P).T)
    put("ln_b", a["conf_ln_b"].reshape(-1, P).T)
    put("sc_w", a["sc_w"].reshape(DEPTH, SC_K, 2, P).transpose(3, 0, 2, 1).reshape(P, -1))
    put("ffn_w", a["ffn_dw_w"].reshape(DEPTH, 3, 2 * HALF_FF, P).transpose(3, 0, 2, 1).reshape(P, -1))
    put("ffn_b", a["ffn_dw_b"].reshape(-1, P).T)
    vec[:, VEC["eps"]] = EPS
    vec[:, VEC["one"]] = 1.0
    arrays["vec"] = vec
    arrays["w_ada"] = np.ascontiguousarray(a["w_ada"].reshape(DEPTH, KD, P, 6, D).transpose(0, 3, 1, 2, 4)
                                           .reshape(-1, P, D))
    for layer in range(DEPTH):
        w = a["w_in"][layer]
        at = np.cumsum([0, Q_W, KV_W, KV_W, 2 * CONF_W, SC_W, SC_W, SC_W, FN_W])
        wq, wk, wv, wcf, wb, wc, wx, wf = (tiles(w[:, s:e]) for s, e in zip(at[:-1], at[1:]))
        wq = tiles(w[:, heads])
        gates = tiles(w[:, at[-1]:]).reshape(4, KD, KD, P, P)
        arrays[f"w_in{layer}"] = chunks(np.concatenate(
            [wq, wk, wv, wf, wc[0:1], wx[0:1], wc[1:2], wx[1:2], wb, wcf[2:3], wcf[0:1], wcf[3:4], wcf[1:2]]))
        br = [tiles(a["w_br_attn"][layer][heads]), tiles(a["w_br_conf"][layer]), tiles(a["w_br_sconv"][layer]),
              tiles(a["w_br_fourier"][layer])]
        for name, b in (("fn", 3), ("sc", 2), ("cf", 1)):
            arrays[f"w_{name}{layer}"] = chunks(np.concatenate([gates[b], br[b]], axis=1))
        at_chunks = []
        for o in range(0, KD, 2):
            at_chunks += [gates[0][o], gates[0][o + 1], np.concatenate([br[0][o], br[0][o + 1]])]
        arrays[f"w_at{layer}"] = chunks(np.stack(at_chunks))
        arrays[f"w_out{layer}"] = chunks(tiles(a["w_out"][layer]))
        up = tiles(a["w_up"][layer]).reshape(2, 2, HALF_FF, KD, P, P)
        down = tiles(a["w_down"][layer])
        for f in range(2):
            arrays[f"w_up{f}{layer}"] = chunks(up[:, f].transpose(1, 0, 2, 3, 4).reshape(2 * HALF_FF, KD, P, P))
            arrays[f"w_dn{f}{layer}"] = chunks(down[:, f * HALF_FF:(f + 1) * HALF_FF])

    nc = bacc.Bacc("TRN2", target_bir_lowering=False, num_devices=1)
    io = {name: nc.dram_tensor(name, x.shape, F32, kind="ExternalInput").ap() for name, x in arrays.items()}
    io["out"] = nc.dram_tensor("out", (P, KD, SEQ), F32, kind="ExternalOutput").ap()
    program(nc, io)
    r = run(nc, [arrays], core_ids=[0])
    return np.ascontiguousarray(r.results[0]["out"].transpose(2, 1, 0).reshape(1, SEQ, D))
```

```python
from contextlib import ExitStack

import concourse.bass as bass
from concourse import mybir

F32 = mybir.dt.float32
F32R = mybir.dt.float32r
ALU = mybir.AluOpType
ACT = mybir.ActivationFunctionType
AX = mybir.AxisListType

P = 128
D = 1024
DEPTH = 2
SEQ = 256
CTX = 256
KD = D // P
N_HEADS = 8
HEAD = 64
Q_W, KV_W = 512, 128
CONF_W, CONF_K = 256, 31
SC_W, SC_K = 256, 3
FN_W = 256
D_FF = 2816
HALF_FF = D_FF // 2 // P
EPS = 1e-6
NT = SEQ + CTX
PAD = (CONF_K - 1) // 2
SLOTS = 4
AHEAD = 3
TAPS = 2 * CONF_K
TAPS_V = 16
POOL_STEPS = 2 * (TAPS - TAPS_V) + 1
ADA_A, ADA_B = 16, 32
ADA_L = ADA_A + ADA_B

PHASES = [("in", 18, 8), ("fn", 8, 10), ("sc", 8, 10), ("at", 12, 8), ("cf", 8, 10), ("out", 8, 8),
          ("up0", 22, 8), ("dn0", 8, HALF_FF), ("up1", 22, 8), ("dn1", 8, HALF_FF)]
START, SIZE, LEN = {}, [], {}
for _name, _count, _tiles in PHASES:
    START[_name] = len(SIZE)
    LEN[_name] = _count
    SIZE += [_tiles] * _count
PER_LAYER = len(SIZE)
TOTAL = DEPTH * PER_LAYER

ADA_START = {2: START["in"] + 2, 3: START["fn"], 4: START["sc"] + 1, 5: START["at"] + 3, 6: START["cf"] + 1,
             8: START["up0"], 9: START["up0"] + 10, 7: START["up0"] + 21, 10: START["up1"] + 1,
             11: START["up1"] + 10}
ORDER = [1, 0] + sorted(ADA_START, key=ADA_START.get)
POS = {_g: _p for _p, _g in enumerate(ORDER)}
REDUCE = {ADA_START[_g] + 10 - (_g == 3) + (_g == 6): _g for _g in ADA_START}
ADA_AT = {ADA_START[_g] + _k: 8 * _g + _k for _g in ADA_START for _k in range(8)}
assert len(ADA_AT) == DEPTH * ADA_L - ADA_A and max(REDUCE) < START["dn1"]
ADA_LOADS = [(0, 1), (1, 1)] + [(_i, 2) for _i in range(2, ADA_A, 2)]
SPLIT_IN_NORM = {0: 0, 2: 1, 4: 2}
FILLS = []
for _n in range(TOTAL):
    FILLS.append(("w", _n))
    if _n - AHEAD in ADA_AT:
        FILLS.append(("ada", ADA_AT[_n - AHEAD]))
PLACE = {_f: _p for _p, _f in enumerate(FILLS)}


def ada_vectors(a):
    return 2 if a < ADA_L or a % ADA_L < 16 else 1


ADA_STEPS, _s = {}, 0
for _kind, _a in FILLS:
    if _kind == "ada":
        _s += ada_vectors(_a)
        ADA_STEPS[_a] = _s


VEC, _at = {}, 0
for _name, _n in [("cc", 2 * KD), ("b_ada", DEPTH * ADA_L), ("g_mix", DEPTH * KD), ("g_ffn", DEPTH * KD),
                  ("g_final", KD), ("sink", DEPTH * N_HEADS), ("conf_w", DEPTH * TAPS), ("conf_b", DEPTH * 2),
                  ("ln_g", DEPTH * 2), ("ln_b", DEPTH * 2), ("sc_w", DEPTH * 2 * SC_K),
                  ("ffn_w", DEPTH * 2 * HALF_FF * 3), ("ffn_b", DEPTH * 2 * HALF_FF), ("eps", 1), ("one", 1)]:
    VEC[_name] = _at
    _at += _n
NVEC = _at
MAT, _at = {}, 0
for _name, _n in [("ident", 128), ("mean", 128), ("rot", 128), ("mask0", 128), ("mask1", 128),
                  ("chan", 256), ("pos", 1024), ("cos", 256), ("sin", 256), ("fold", 32)]:
    MAT[_name] = _at
    _at += _n
NMAT = _at


def normed(r, s):
    return (2 * r if r < 4 else 7) + s + 1


class Step:

    def __init__(self, n, idx, i=None):
        self.n, self.idx, self.i = n, idx, i
        self.slot = n % SLOTS

    def up(self, base, per=4):
        return base if self.i is None else base + per * self.i

    def filled(self, item, ahead=0):
        p = PLACE[(item, self.n + ahead)]
        per = 0 if self.i is None else (PLACE[(item, self.n + ahead + SLOTS)] - p) * 16 // SLOTS
        return p % SLOTS, self.up(16 * (p // SLOTS + 1), per)


def walk(eng, layer, name, step, lead=0, skip=0, keep=0):
    first, count = layer * PER_LAYER + START[name], LEN[name]
    if lead:
        skip = max(skip, -(-lead // SLOTS))
    groups = (count - keep) // SLOTS
    if groups - skip < 2:
        skip = groups = 0
    for idx in range(lead, min(skip * SLOTS, count)):
        step(Step(first + idx, idx))
    if groups:
        with eng.Fori(skip, groups) as i:
            for j in range(SLOTS):
                step(Step(first + j, j, i))
        lead = 0
    for idx in range(max(lead, groups * SLOTS), count):
        step(Step(first + idx, idx))


def program(nc, io):
    ctx = ExitStack()
    with ctx:
        base = -(-nc.sbuf_base // 32) * 32
        top = [base]

        def at(name, shape, dt, offset):
            return nc.alloc_sbuf_tensor_at(name, [P] + shape, dt, offset=offset)

        def place(name, shape, dt=F32):
            size = 4
            for s in shape:
                size *= s
            offset = top[0]
            top[0] += -(-size // 32) * 32
            return at(name, shape, dt, offset)

        SLOT = HALF_FF * P
        raw = place("raw", [SLOTS, SLOT])
        w_hi = place("w_hi", [SLOTS, SLOT], F32R)
        w_lo = place("w_lo", [SLOTS, SLOT], F32R)
        ada_first = at("ada_first", [ADA_A, KD * P], F32, base)
        assert ADA_A * KD * P <= 3 * SLOTS * SLOT
        ada_sum = place("ada_sum", [2, KD * P])
        X = place("X", [KD, NT])
        h_off = top[0]
        h_hi = place("h_hi", [KD, NT], F32R)
        h_lo = place("h_lo", [KD, NT], F32R)
        y_off = top[0]
        y_hi = place("y_hi", [8, NT], F32R)
        y_lo = place("y_lo", [8, NT], F32R)
        yc_hi = place("yc_hi", [2, NT], F32R)
        yc_lo = place("yc_lo", [2, NT], F32R)
        top[0] = max(top[0], y_off + 4 * (16 * NT + 2 * NT + 2 * 2 * (SEQ + 2)))
        q_off = top[0]
        q = place("q", [4, NT])
        k = place("k", [NT])
        v = place("v", [NT // P, KV_W])
        glu = place("glu", [2, 2, SEQ + 2 * PAD])
        acc = place("acc", [2, NT])
        t_off = top[0]
        prob2 = place("prob", [2, NT])
        probT = place("probT", [2, NT])
        sqb = place("sqb", [NT])
        sqa = place("sqa", [NT])
        mat = place("mat", [NMAT])
        vec = place("vec", [NVEC])
        csil = place("csil", [KD, 2])
        mod = place("mod", [2, ADA_L, 2])
        gsc = place("gsc", [2, 2, KD])
        nsink = place("nsink", [DEPTH * N_HEADS])
        small = place("small", [3, 6])
        root_col = place("root_col", [NT // P])
        ada_part = place("ada_part", [2, P * KD // 32])
        prob = [prob2[:, 0, :], prob2[:, 1, :], sqa[:, :]]
        assert top[0] <= nc.sbuf_usable_end, (top[0], nc.sbuf_usable_end)
        mg_hi = at("mg_hi", [KD, NT], F32R, y_off)
        mg_lo = at("mg_lo", [KD, NT], F32R, y_off + 4 * KD * NT)
        assert y_off + 4 * NT * 2 * HALF_FF <= t_off
        hid_hi = at("hid_hi", [HALF_FF, NT], F32R, y_off)
        hid_lo = at("hid_lo", [HALF_FF, NT], F32R, y_off + 4 * HALF_FF * NT)
        x_in = at("x_in", [KD, NT], F32, q_off)
        pc = at("pc", [2, NT], F32, y_off + 4 * 16 * NT)
        cx = at("cx", [2, 2, SEQ + 2], F32, y_off + 4 * 18 * NT)
        tmp = [at(f"tmp{b}", [NT], F32, t_off + 4 * NT * b) for b in range(2)]
        sig = [at(f"sig{b}", [NT], F32, t_off + 4 * NT * (2 + b)) for b in range(2)]
        y_out = at("y_out", [KD, SEQ], F32, h_off)

        psA = [ctx.enter_context(nc.psum_tensor(f"psA{b}", [P, 512], F32)) for b in range(4)]
        psB = [ctx.enter_context(nc.psum_tensor(f"psB{b}", [P, 512], F32)) for b in range(4)]

        spread_bank = [psB[3], psB[0]]
        score_bank = [psA[0], psA[1], psB[2]]

        def sem(name):
            return ctx.enter_context(nc.semaphore(name))

        raw_full = [sem(f"raw_full{s}") for s in range(SLOTS)]
        ada_in = [sem(f"ada_in{j}") for j in range(len(ADA_LOADS))]
        x_full = [sem(f"x_full{j}") for j in range(4)]
        mats_in, vecs_in, x_again, stored = map(sem, ("mats_in", "vecs_in", "x_again", "stored"))
        head_done, rest_done = sem("head_done"), sem("rest_done")
        chunk_done = sem("chunk_done")
        evac = sem("evac")
        ada_pe, ada_row, ada_acc, reduced = sem("ada_pe"), sem("ada_row"), sem("ada_acc"), sem("ada_reduced")
        folded, v_mm, v_done, inv_col, spread, sq_last, half_done, x_half = map(sem, (
            "folded", "v_mm", "v_done", "inv_col", "spread", "sq_last", "half_done", "x_half"))
        tap_pool = sem("tap_pool")
        csil_done, nsink_done, mod_done, gsc_done = map(sem, ("csil_done", "nsink_done", "mod_done", "gsc_done"))
        sq_done, sq_sum, stat, root, inv, ht, h_head, h_rest = map(sem, (
            "sq_done", "sq_sum", "stat", "root", "inv", "ht", "h_head", "h_rest"))
        pads, rot, rope, fc_mm, fc, fn_mm, fn_head, fn_rest = map(sem, (
            "pads", "rot", "rope", "fc_mm", "fc", "fn_mm", "fn_head", "fn_rest"))
        sc_step, sc_head, sc_rest, sigd = map(sem, ("sc_step", "sc_head", "sc_rest", "sigd"))
        s_mm, negm, expd, den, pn, t_mm, pt, o_mm, o_head, o_rest = map(sem, (
            "s_mm", "negm", "expd", "den", "pn", "t_mm", "pt", "o_mm", "o_head", "o_rest"))
        tap, ln_mean, ln_xc, ln_sq, ln_var, ln_root, ln_inv, ln_n, ln_silu, ln_head, ln_rest = map(sem, (
            "tap", "ln_mean", "ln_xc", "ln_sq", "ln_var", "ln_root", "ln_inv", "ln_n", "ln_silu", "ln_head",
            "ln_rest"))
        m_sum, m_head, m_rest = map(sem, ("m_sum", "m_head", "m_rest"))
        cv, silu, hid_head, hid_rest, fin = map(sem, ("cv", "silu", "hid_head", "hid_rest", "fin"))

        def M(name, n=128, off=0):
            return mat[:, MAT[name] + off:MAT[name] + off + n]

        def V(name, i):
            return vec[:, VEC[name] + i:VEC[name] + i + 1]

        def Vd(name, i):
            return vec[:, bass.ds(VEC[name] + i, 1)]

        def streams(layer):
            return 2 if layer == 0 else 1

        def norm_streams(r):
            return 2 if r < 3 else 1

        def both(ap, T):
            return ap.rearrange("p (s t) -> p s t", s=T // SEQ)

        def branch_sum(layer, o):
            return X[:, o, 0:NT] if layer == 0 else X[:, o, SEQ:NT]

        def f_in(layer, c):
            return X[:, c, 0:NT] if layer == 0 else X[:, c, SEQ:NT]

        def pb(layer, c):
            return X[:, 6 + c, 0:NT] if layer == 0 else X[:, 6 + c, SEQ:NT]

        def f_mid(layer, tb):
            if layer == 0:
                return X[:, 2 + tb, :].rearrange("p (c n) -> p c n", c=2)
            return X[:, 2 + 2 * tb:4 + 2 * tb, SEQ:NT]

        def units(layer):
            return [(s, qi, t, half) for qi in range(2) for t in range(4) for s in range(streams(layer))
                    for half in range(2)]

        NU = [len(units(0)), len(units(1))]
        U0 = [0, NU[0]]

        def first_free(slot):
            return min(ADA_A, -(-(slot + 1) * SLOT // (KD * P)))

        block = ctx.enter_context(nc.Block())

        @block.sync
        def _(sp):
            sp.dma_start(vec[:, :], io["vec"]).then_inc(vecs_in, 16)

            def slot_free(p, shift=0):
                if p >= SLOTS:
                    item, m = FILLS[p - SLOTS]
                    if item == "w":
                        sp.wait_ge(rest_done, m + 1 + shift)
                    else:
                        sp.wait_ge(ada_acc, ADA_STEPS[m])

            def load_ada(a):
                p = PLACE[("ada", a)]
                slot_free(p)
                sp.dma_start(raw[:, p % SLOTS, 0:KD * P], io["w_ada"][a]).then_inc(raw_full[p % SLOTS], 16)

            for j, (i, count) in enumerate(ADA_LOADS):
                a = 8 * ORDER[i // 8] + i % 8
                sp.dma_start(ada_first[:, i:i + count, :], io["w_ada"][a:a + count].rearrange("a p n -> p a n"))\
                    .then_inc(ada_in[j], 16)
                if 1 <= j < 5:
                    k0 = 2 * (j - 1)
                    sp.dma_start(X[:, k0:k0 + 2, :], io["x"][:, k0:k0 + 2, :]).then_inc(x_full[j - 1], 16)
                if j == 6:
                    sp.dma_start(mat[:, :], io["mat"]).then_inc(mats_in, 16)
            sp.wait_ge(ada_pe, first_free(SLOTS - 1))
            for layer in range(DEPTH):
                for name, _, tiles in PHASES:
                    src = io[f"w_{name}{layer}"]

                    def load(st):
                        p = PLACE[("w", st.n)]
                        slot_free(p, 0 if st.i is None else SLOTS * st.i)
                        dst = raw[:, p % SLOTS, 0:tiles * P]
                        if st.i is None:
                            sp.dma_start(dst, src[st.idx]).then_inc(raw_full[p % SLOTS], 16)
                            if st.n - AHEAD in ADA_AT:
                                load_ada(ADA_AT[st.n - AHEAD])
                        else:
                            sp.dma_start(dst, src[bass.ds(st.up(st.idx), 1)].rearrange("a p n -> p (a n)"))\
                                .then_inc(raw_full[p % SLOTS], 16)

                    walk(sp, layer, name, load, skip=LEN[name] if layer == 0 or name == "in" else 0)
                    if layer == 0 and name == "cf":
                        sp.wait_ge(chunk_done, START["fn"] + 1)
                        sp.wait_ge(tap, TAPS_V)
                        sp.wait_ge(tap_pool, POOL_STEPS)
                        sp.dma_start(x_in[:, :, :], io["x"]).then_inc(x_again, 16)
            for kk in range(KD):
                sp.wait_ge(fin, kk + 1)
                sp.dma_start(io["out"][:, kk, :], y_out[:, kk, :]).then_inc(stored, 16)
            sp.wait_ge(stored, 16 * KD)

        @block.gpsimd
        def _(pool):
            pool.memset(glu[:, :, :, :], 0.0).then_inc(pads, 1)
            pool.memset(cx[:, :, :, :], 0.0).then_inc(pads, 1)
            for layer in range(DEPTH):
                if layer:
                    pool.wait_ge(chunk_done, PER_LAYER)
                    pool.memset(cx[:, :, :, :], 0.0).then_inc(pads, 1)
                    pool.memset(glu[:, :, :, :], 0.0).then_inc(pads, 1)
                S = streams(layer)
                part, dst = both(sqb[:, 0:SEQ * S], SEQ * S), both(acc[:, 1, 0:SEQ * S], SEQ * S)
                c0 = POOL_STEPS * layer
                pool.wait_ge(evac, layer * PER_LAYER + LEN["in"])
                for j in range(CONF_K):
                    w = V("conf_w", TAPS * layer + CONF_K + j)
                    src = glu[:, 1, 0:S, j:j + SEQ]
                    if j == 0:
                        pool.tensor_scalar(dst, src, w, V("conf_b", 2 * layer + 1), ALU.mult, ALU.add)\
                            .then_inc(tap_pool, 2)
                        continue
                    pool.wait_ge(tap_pool, c0 + 2 * j)
                    pool.tensor_scalar(part, src, w, 0.0, ALU.mult, ALU.add).then_inc(tap_pool, 1)
                    pool.wait_ge(tap_pool, c0 + 2 * j + 1)
                    pool.tensor_tensor(dst, dst, part, ALU.add).then_inc(tap_pool, 1)

                T = SEQ * S
                n0 = layer * PER_LAYER
                s0 = 12 * layer
                for c in range(2):
                    w = 3 * (2 * layer + c)
                    u = both(pc[:, c, 0:T], T)
                    for step in range(6):
                        if step or c:
                            pool.wait_ge(sc_step, s0 + 6 * c + step)
                        tap3 = (step + 1) // 2
                        if step == 5:
                            op = pool.tensor_tensor(u, u, both(pb(layer, c), T), ALU.mult)
                        elif step in (0, 1, 3):
                            op = pool.tensor_scalar(part if step else u, cx[:, c, 0:S, tap3:tap3 + SEQ],
                                                    V("sc_w", w + tap3), 0.0, ALU.mult, ALU.add)
                        else:
                            op = pool.tensor_tensor(u, u, part, ALU.add)
                        op.then_inc(sc_step, 1)

                pool.wait_ge(s_mm, U0[layer] + NU[layer])
                mine = both(q[:, 0, 0:T], T)
                for j in range(TAPS_V, CONF_K):
                    w, done = V("conf_w", TAPS * layer + j), c0 + 2 * CONF_K + 2 * (j - TAPS_V)
                    src = glu[:, 0, 0:S, j:j + SEQ]
                    pool.wait_ge(tap_pool, done)
                    if j == TAPS_V:
                        pool.tensor_scalar(mine, src, w, 0.0, ALU.mult, ALU.add).then_inc(tap_pool, 2)
                        continue
                    pool.tensor_scalar(part, src, w, 0.0, ALU.mult, ALU.add).then_inc(tap_pool, 1)
                    pool.wait_ge(tap_pool, done + 1)
                    pool.tensor_tensor(mine, mine, part, ALU.add).then_inc(tap_pool, 1)


                def add(n, idx, o, b):
                    pool.wait_ge(evac, n + idx + 1)
                    dst = branch_sum(layer, o)
                    pool.tensor_tensor(dst, dst, tmp[b][:, 0:T], ALU.add).then_inc(m_sum, 1)
                for idx in range(LEN["sc"]):
                    add(n0 + START["sc"], idx, idx, idx % 2)
                pool.wait_ge(tap, TAPS_V * (layer + 1))
                pool.wait_ge(tap_pool, c0 + POOL_STEPS - 1)
                tile0 = both(acc[:, 0, 0:T], T)
                pool.tensor_tensor(tile0, tile0, mine, ALU.add).then_inc(tap_pool, 1)
                for idx in range(2, LEN["at"], 3):
                    for half in range(2):
                        add(n0 + START["at"], idx, idx // 3 * 2 + half, half)
                for idx in range(LEN["cf"]):
                    add(n0 + START["cf"], idx, idx, idx % 2)

                for f in range(2):
                    p0 = HALF_FF * (2 * layer + f)

                    def hidden_rest(st):
                        if st.idx % 2:
                            pair, b = st.idx // 2, (st.idx // 2) % 2
                            pool.wait_ge(hid_head, st.up(p0 + pair + 1, 2))
                            dst = hid_lo[:, bass.ds(st.up(pair, 2), 1), 0:T].rearrange("p a t -> p (a t)")
                            src = hid_hi[:, bass.ds(st.up(pair, 2), 1), 0:T].rearrange("p a t -> p (a t)")
                            pool.tensor_tensor(dst, sig[b][:, 0:T], src.bitcast(F32), ALU.subtract)\
                                .then_inc(hid_rest, 1)
                    walk(pool, layer, f"up{f}", hidden_rest)

        @block.tensor
        def _(pe):
            def product(out, st, tile, hi, lo, first, last):
                w0 = w_hi[:, st.slot, tile * P:(tile + 1) * P]
                w1 = w_lo[:, st.slot, tile * P:(tile + 1) * P]
                pe.matmul(out, w0, hi, start=first, stop=False)
                pe.matmul(out, w0, lo, start=False, stop=False)
                return pe.matmul(out, w1, hi, start=False, stop=last)

            def begin(st):
                pe.wait_ge(rest_done, st.up(st.n + 1))
                if st.n >= SLOTS:
                    pe.wait_ge(evac, st.up(st.n - SLOTS + 1))

            def from_h(st, T, out):
                for kk in range(KD):
                    mm = product(out, st, kk, h_hi[:, kk, 0:T], h_lo[:, kk, 0:T], kk == 0, kk == KD - 1)
                return mm

            def ada_product(i):
                g, kk = ORDER[i // 8], i % 8
                for j, (first, _) in enumerate(ADA_LOADS):
                    if first == i:
                        pe.wait_ge(ada_in[j], 16)
                for half in range(2):
                    mm = pe.matmul(psA[2 * g + half][0:2, :], csil[:, kk, :],
                                   ada_first[:, i, half * 512:(half + 1) * 512], start=(kk == 0), stop=(kk == KD - 1))
                mm.then_inc(ada_pe, 1)

            def turn_group(g):
                pe.wait_ge(ada_row, 2 * (POS[g] + 1))
                for c in range(KD):
                    mm = pe.matmul(psB[1 + g][:, 2 * c:2 * c + 2], ada_sum[0:2, g, c * P:(c + 1) * P],
                                   mat[0:2, MAT["ident"]:MAT["ident"] + 2], start=True, stop=True)
                mm.then_inc(reduced, 1)

            def reduce_group(g, bank):
                vs = ada_vectors(8 * g)
                pe.wait_ge(folded, POS[g] - 1)
                for j in range(4):
                    rows = slice(32 * j, 32 * j + 32)
                    out = bank[rows, 0:2 * KD].rearrange("p (v c) -> p v c", v=2)[:, 0:vs, :]
                    part = ada_part[:, 0:vs, :].rearrange("p v (c j) -> p v c j", j=4)[:, :, :, j]
                    mm = pe.matmul(out, M("fold", 32), part, start=True, stop=True)
                mm.then_inc(reduced, 1)

            def reduce_in_front(st):
                if st.i is None and st.n in REDUCE:
                    pe.wait_ge(evac, st.n - SLOTS + 1)
                    reduce_group(REDUCE[st.n], psB[st.slot])

            def reduction_read(st, late=0):
                if st.i is None and st.n - late in REDUCE:
                    pe.wait_ge(mod_done, POS[REDUCE[st.n - late]] + 1)

            def lead(layer, name, T, count, hi, lo, ready, r=None):
                first = layer * PER_LAYER + START[name]
                sts = [Step(first + j, j) for j in range(AHEAD)]
                for st in sts:
                    begin(st)
                splits = [slice(0, T)] if r is None else [slice(SEQ * s, SEQ * (s + 1)) for s in range(T // SEQ)]
                for s, cols in enumerate(splits):
                    for kk in range(count):
                        if r is not None and s == 0 and kk == 3 and norm_streams(r) > 1:
                            spread_inverse(r, 1)
                        pe.wait_ge(ready[0], ready[1] + count * s + kk + 1)
                        for st in sts:
                            mm = product(psA[st.slot][:, cols], st, kk, hi[:, kk, cols], lo[:, kk, cols],
                                         kk == 0, kk == count - 1)
                            if kk == count - 1 and s == len(splits) - 1:
                                mm.then_inc(chunk_done, 1)

            def last_by_stream(st, hi, lo, count):
                begin(st)
                for s, bank in enumerate((psA[st.slot], psB[1])):
                    cols = slice(SEQ * s, SEQ * (s + 1))
                    for kk in range(count):
                        mm = product(bank[:, cols], st, kk, hi[:, kk, cols], lo[:, kk, cols],
                                     kk == 0, kk == count - 1)
                    mm.then_inc(chunk_done if s else half_done, 1)

            def mean_square(r, s):
                if s:
                    pe.wait_ge(root, normed(r, 0))
                for last, squares in enumerate((sqa, sqb)):
                    if last:
                        pe.wait_ge(sq_last, normed(r, s))
                    else:
                        pe.wait_ge(sq_sum, 6 * (r + 1))
                    for b in range(2 * s, 2 * s + 2):
                        mm = pe.matmul(psB[0][:, b:b + 1], squares[:, b * P:(b + 1) * P], M("mean")[:, 0:1],
                                       start=(not last and b == 2 * s), stop=bool(last), skip_group_check=True)
                mm.then_inc(stat, 1)

            def spread_inverse(r, s):
                pe.wait_ge(inv, normed(r, s))
                for b in range(2 * s, 2 * s + 2):
                    mm = pe.matmul(spread_bank[s][:, b * P:(b + 1) * P], M("mean"), sqb[:, b * P:(b + 1) * P],
                                   start=True, stop=True)
                mm.then_inc(spread, 1)

            def norm_stat(r):
                mean_square(r, 0)
                spread_inverse(r, 0)
                if norm_streams(r) > 1:
                    mean_square(r, 1)

            pe.wait_ge(csil_done, 1)
            for i in range(ADA_A):
                ada_product(i)
                if i == 11:
                    pe.wait_ge(mats_in, 16)
                    mean_square(0, 0)
                    mean_square(0, 1)
                if i == 13:
                    turn_group(ORDER[0])
                    spread_inverse(0, 0)
            turn_group(ORDER[1])

            for layer in range(DEPTH):
                n0 = layer * PER_LAYER
                T = SEQ * streams(layer)
                if layer:
                    norm_stat(2 * layer)
                fc0 = 4 * layer

                def fourier_channels():
                    pe.wait_ge(rope, 15 * (layer + 1))
                    pe.wait_ge(v_done, layer + 1)
                    for tb in range(T // P):
                        for c in range(2):
                            mm = pe.matmul(psB[tb][:, c * 256:(c + 1) * 256], f_in(layer, c)[:, tb * P:(tb + 1) * P],
                                           M("chan", 256), start=True, stop=True)
                        mm.then_inc(fc_mm, 1)

                def fourier_positions():
                    pe.wait_ge(fc, fc0 + T // P)
                    for s in range(streams(layer)):
                        for c in range(2):
                            out = psB[2 * s + c][:, 0:SEQ]
                            for h in range(2):
                                mid = f_mid(layer, 2 * s + h)
                                for part in range(2):
                                    mm = pe.matmul(out, mid[:, c, part * P:(part + 1) * P],
                                                   M("pos", SEQ, 512 * h + 256 * part),
                                                   start=(h == 0 and part == 0), stop=(h == 1 and part == 1))
                            mm.then_inc(fn_mm, 1)

                lead(layer, "in", T, KD, h_hi, h_lo, (h_rest, 32 * layer), 2 * layer)
                for idx in range(AHEAD, LEN["in"]):
                    st = Step(n0 + idx, idx)
                    reduce_in_front(st)
                    if not (layer and idx == 5):
                        begin(st)
                    if layer and idx == 4:
                        pair = [st, Step(n0 + 5, 5)]
                        begin(pair[1])
                        for s in range(2):
                            cols = slice(SEQ * s, SEQ * (s + 1))
                            if s:
                                pe.wait_ge(h_rest, 32 * layer + 16)
                            for one in pair:
                                for kk in range(KD):
                                    mm = product(psA[one.slot][:, cols], one, kk, h_hi[:, kk, cols],
                                                 h_lo[:, kk, cols], kk == 0, kk == KD - 1)
                                if s:
                                    mm.then_inc(chunk_done, 1)
                    if layer and idx in (4, 5):
                        continue
                    cols = NT if idx in (4, 5) else T
                    from_h(st, cols, psA[st.slot][:, 0:cols]).then_inc(chunk_done, 1)
                    reduction_read(st, 1)
                    if idx == 7:
                        pe.wait_ge(evac, n0 + 6)
                        for b in range(NT // P):
                            mm = pe.transpose(psB[2][:, b * P:(b + 1) * P], sig[0][:, b * P:(b + 1) * P], M("ident"))
                        mm.then_inc(v_mm, 1)
                    if 6 <= idx < 11:
                        j = idx - 6
                        pe.wait_ge(evac, n0 + j + 1)
                        if j >= 2:
                            pe.wait_ge(rope, 15 * layer + 3 * (j - 2) + 1)
                        src = q[:, j, 0:SEQ] if j < 4 else k[:, 0:SEQ]
                        pe.matmul(psB[1 + 2 * (j % 2)][:, 0:SEQ], M("rot"), src, start=True, stop=True)\
                            .then_inc(rot, 1)
                    if idx == 13:
                        fourier_channels()
                    if idx == 15:
                        fourier_positions()
                un, u0 = units(layer), U0[layer]
                pe.wait_ge(rope, 15 * (layer + 1))
                pe.wait_ge(v_done, layer + 1)
                m0 = n0 + START["fn"]
                for j in range(len(un) + 3):
                    if j == 0:
                        pe.wait_ge(evac, n0 + LEN["in"])
                        pe.wait_ge(fn_rest, fc0 + 2 * streams(layer))
                    if j < len(un):
                        s, qi, t, half = un[j]
                        k0, nk = (0, 4) if s == 0 else (2, 2)
                        ps = score_bank[j % 3]
                        if j >= 3:
                            pe.wait_ge(expd, 2 * (u0 + j - 2))
                        rows = slice(64 * half, 64 * half + 64)
                        q0 = SEQ * s + P * qi
                        mm = pe.matmul(ps[:, 0:nk * P], q[rows, t, q0:q0 + P], k[rows, k0 * P:(k0 + nk) * P],
                                       start=True, stop=True)
                        if s == 0:
                            mm = pe.matmul(ps[:, (1 - qi) * P:(2 - qi) * P], M("ident"), M(f"mask{qi}"),
                                           start=False, stop=True, skip_group_check=True)
                        mm.then_inc(s_mm, 1)
                    if 2 <= j < len(un) + 2:
                        nk = 4 if un[j - 2][0] == 0 else 2
                        pe.wait_ge(pn, u0 + j - 1)
                        if j >= 4:
                            pe.wait_ge(pt, u0 + j - 3)
                        for b in range(nk):
                            mm = pe.transpose(psA[2 + j % 2][:, b * P:(b + 1) * P],
                                              prob[(j - 2) % 3][:, b * P:(b + 1) * P], M("ident"))
                        mm.then_inc(t_mm, 1)
                    if j >= 3:
                        s, qi, t, half = un[j - 3]
                        k0, nk = (0, 4) if s == 0 else (2, 2)
                        pair = (j - 3) // 2
                        pe.wait_ge(pt, u0 + j - 2)
                        if half == 0 and pair >= 2:
                            pe.wait_ge(o_rest, u0 // 2 + pair - 1)
                        for b in range(nk):
                            mm = pe.matmul(psB[pair % 2][64 * half:64 * half + 64, 0:P],
                                           v[:, k0 + b, 64 * half:64 * half + 64],
                                           probT[:, (j - 3) % 2, b * P:(b + 1) * P], start=(b == 0),
                                           stop=(b == nk - 1))
                        mm.then_inc(o_mm, 1)
                    if j == len(un) + 1:
                        first = Step(m0, 0)
                        begin(first)
                        from_h(first, T, psA[first.slot][:, 0:T])

                def merge(st, hi, lo, tiles, wait):
                    if st.n == m0:
                        pe.wait_ge(o_rest, (u0 + len(un)) // 2 - 1)
                    else:
                        reduce_in_front(st)
                        begin(st)
                        from_h(st, T, psA[st.slot][:, 0:T])
                        reduction_read(st)
                    if wait is not None:
                        pe.wait_ge(*wait)
                    for c in range(tiles):
                        mm = product(psB[st.slot][:, 0:T], st, KD + c, hi[:, c, 0:T], lo[:, c, 0:T],
                                     c == 0, c == tiles - 1)
                    mm.then_inc(chunk_done, 1)

                merge(Step(m0, 0), y_hi[:, 0:2, :], y_lo[:, 0:2, :], 2, None)
                pe.wait_ge(o_rest, (u0 + len(un)) // 2)
                walk(pe, layer, "fn", lambda st: merge(st, y_hi[:, 0:2, :], y_lo[:, 0:2, :], 2, None), lead=1)
                walk(pe, layer, "sc", lambda st: merge(st, y_hi[:, 2:4, :], y_lo[:, 2:4, :], 2,
                                                       (sc_rest, 2 * layer + 2)), skip=1 - layer)
                m0 = n0 + START["at"]
                for idx in range(LEN["at"]):
                    st = Step(m0 + idx, idx)
                    reduce_in_front(st)
                    begin(st)
                    if idx % 3 < 2:
                        mm = from_h(st, T, psA[st.slot][:, 0:T])
                        reduction_read(st)
                    else:
                        if idx == 8:
                            pe.wait_ge(ln_xc, 2 * layer + 2)
                        if idx == 11:
                            pe.wait_ge(ln_root, layer + 1)
                        for half, ps in enumerate((psA, psB)):
                            for c in range(4):
                                mm = product(ps[st.slot][:, 0:T], st, 4 * half + c, y_hi[:, 4 + c, 0:T],
                                             y_lo[:, 4 + c, 0:T], c == 0, c == 3)
                    mm.then_inc(chunk_done, 1)
                    if idx == 1:
                        pe.wait_ge(evac, m0 - 3)
                        pe.wait_ge(tap, TAPS_V * (layer + 1))
                        pe.wait_ge(tap_pool, POOL_STEPS * (layer + 1))
                        for c in range(2):
                            mm = pe.matmul(psB[m0 % 4][:, 0:T], M("mean"), acc[:, c, 0:T], start=(c == 0), stop=(c == 1))
                        mm.then_inc(ln_mean, 1)
                    if idx == 6:
                        pe.wait_ge(ln_sq, 2 * layer + 2)
                        pe.wait_ge(evac, m0)
                        for c, sq in enumerate((sqb, sqa)):
                            mm = pe.matmul(psB[(m0 + 3) % 4][:, 0:T], M("mean"), sq[:, 0:T],
                                           start=(c == 0), stop=(c == 1))
                        mm.then_inc(ln_var, 1)
                walk(pe, layer, "cf", lambda st: merge(st, yc_hi, yc_lo, 2, (ln_rest, 2 * layer + 2)),
                     skip=2 * (1 - layer))

                def project(st):
                    if st.idx == KD - 1 and T == NT:
                        last_by_stream(st, mg_hi, mg_lo, KD)
                        return
                    reduce_in_front(st)
                    begin(st)
                    for kk in range(KD):
                        mm = product(psA[st.slot][:, 0:T], st, kk, mg_hi[:, kk, 0:T], mg_lo[:, kk, 0:T],
                                     kk == 0, kk == KD - 1)
                    mm.then_inc(chunk_done, 1)
                    reduction_read(st, 1)
                lead(layer, "out", T, KD, mg_hi, mg_lo, (m_rest, 8 * layer))
                walk(pe, layer, "out", project, lead=AHEAD)
                norm_stat(2 * layer + 1)

                for f in range(2):
                    def lift(st):
                        reduce_in_front(st)
                        begin(st)
                        from_h(st, T, psA[st.slot][:, 0:T]).then_inc(chunk_done, 1)
                        reduction_read(st, 1)
                    straight = LEN["up0"] if layer == 0 else 0
                    if f == 0:
                        lead(layer, "up0", T, KD, h_hi, h_lo, (h_rest, 16 * (2 * layer + 1)),
                             2 * layer + 1)
                        walk(pe, layer, "up0", lift, lead=AHEAD, skip=straight)
                    else:
                        walk(pe, layer, "up1", lift, skip=straight)

                    def lower(st):
                        if st.idx == KD - 1 and T == NT and f == 1:
                            last_by_stream(st, hid_hi, hid_lo, HALF_FF)
                            return
                        begin(st)
                        for c in range(HALF_FF):
                            mm = product(psA[st.slot][:, 0:T], st, c, hid_hi[:, c, 0:T], hid_lo[:, c, 0:T],
                                         c == 0, c == HALF_FF - 1)
                        mm.then_inc(chunk_done, 1)
                    name = f"dn{f}"
                    lead(layer, name, T, HALF_FF, hid_hi, hid_lo, (hid_rest, HALF_FF * (2 * layer + f)))
                    walk(pe, layer, name, lower, lead=AHEAD)
            norm_stat(2 * DEPTH)

        @block.scalar
        def _(act):
            def head(st, tiles):
                if st.i is None and st.n + AHEAD >= TOTAL:
                    return
                r, full = st.filled("w", AHEAD)
                act.wait_ge(raw_full[r], full)
                if st.n >= 1:
                    act.wait_ge(chunk_done, st.up(st.n))
                s = (st.n + AHEAD) % SLOTS
                act.activation(w_hi[:, s, 0:tiles * P], raw[:, r, 0:tiles * P], ACT.Copy).then_inc(head_done, 1)

            def size(st, layer, name):
                return SIZE[START[name]] if st.i is not None else SIZE[(st.n + AHEAD) % PER_LAYER]

            def early_table(func):
                act.activation(small[:, 0, 5:6], V("one", 0), func)

            def square(count, o, T, direct, before):
                if before is not None:
                    act.wait_ge(*before)
                if count % 8 >= 2:
                    act.wait_ge(sq_sum, 6 * (count // 8) + count % 8 - 1)
                src = X[:, o, 0:T] if isinstance(o, int) else X[:, bass.ds(o, 1), 0:T].rearrange("p a t -> p (a t)")
                act.activation((sqa if direct else sqb)[:, 0:T], src, ACT.Square).then_inc(sq_done, 1)

            def last_squares(r, written):
                early_table(ACT.Sqrt)
                act.wait_ge(sq_sum, 6 * (r + 1))
                for s in range(norm_streams(r)):
                    cols = slice(SEQ * s, SEQ * (s + 1))
                    if written:
                        act.wait_ge(*written[s])
                    act.activation(sqb[:, cols], X[:, KD - 1, cols], ACT.Square).then_inc(sq_last, 1)

            def norm_root(r):
                for s in range(norm_streams(r)):
                    act.wait_ge(stat, normed(r, s))
                    act.activation(root_col[:, 2 * s:2 * s + 2], psB[0][:, 2 * s:2 * s + 2], ACT.Sqrt,
                                   bias=V("eps", 0)).then_inc(root, 1)

            def norm(layer, which):
                r = 2 * layer + which
                if r:
                    norm_root(r)
                if r == 0:
                    act.wait_ge(mod_done, 2)
                for s in range(norm_streams(r)):
                    cols = slice(s * SEQ, (s + 1) * SEQ)
                    for kk in range(KD):
                        if r == 2 and s == 1 and kk in SPLIT_IN_NORM:
                            head(Step(PER_LAYER + SPLIT_IN_NORM[kk], SPLIT_IN_NORM[kk]), SIZE[AHEAD])
                        act.wait_ge(ht, 16 * r + KD * s + kk + 1)
                        act.activation(h_hi[:, kk, cols], tmp[kk % 2][:, cols], ACT.Identity,
                                       bias=mod[:, layer, 24 * which + kk, s:s + 1]).then_inc(h_head, 1)

            act.wait_ge(vecs_in, 16)
            act.activation(csil[:, :, :].rearrange("p k c -> p (k c)"), vec[:, VEC["cc"]:VEC["cc"] + 2 * KD],
                           ACT.Silu).then_inc(csil_done, 1)
            for kk in range(KD - 1):
                if kk % 2 == 0:
                    act.wait_ge(x_full[kk // 2], 16)
                square(kk, kk, NT, kk == 0, None)
            last_squares(0, None)
            def ada_rows(g, half):
                act.activation(ada_sum[0:2, g, half * 512:(half + 1) * 512], psA[2 * g + half][0:2, :], ACT.Copy)\
                    .then_inc(ada_row, 1)

            act.wait_ge(ada_pe, 8)
            for half in range(2):
                ada_rows(ORDER[0], half)
            norm_root(0)
            for ahead in range(AHEAD):
                act.wait_ge(ada_pe, first_free(SLOTS + ahead))
                head(Step(ahead - AHEAD, 0), 8)
            act.wait_ge(ada_pe, ADA_A)
            ada_rows(ORDER[1], 0)

            for layer in range(DEPTH):
                n0 = layer * PER_LAYER
                T = SEQ * streams(layer)
                norm(layer, 0)
                for idx in range(LEN["in"]):
                    st = Step(n0 + idx, idx)
                    if not (layer and idx in SPLIT_IN_NORM.values()):
                        head(st, size(st, layer, "in"))
                    fc0 = 4 * layer
                    if idx == 14:
                        for tb in range(T // P):
                            act.wait_ge(fc_mm, fc0 + tb + 1)
                            act.activation(f_mid(layer, tb), psB[tb][:, :].rearrange("p (c n) -> p c n", c=2),
                                           ACT.Copy).then_inc(fc, 1)
                    if idx == 16:
                        for j in range(2 * streams(layer)):
                            s, c = divmod(j, 2)
                            act.wait_ge(fn_mm, fc0 + j + 1)
                            act.activation(y_hi[:, c, s * SEQ:(s + 1) * SEQ], psB[j][:, 0:SEQ], ACT.Copy)\
                                .then_inc(fn_head, 1)
                    if idx in (14, 16):
                        act.wait_ge(chunk_done, st.n + 1)
                        act.activation(sig[(idx - 14) // 2][:, 0:T], psA[st.slot][:, 0:T], ACT.Sigmoid)\
                            .then_inc(sigd, 1)
                early_table(ACT.Exp)

                un, u0 = units(layer), U0[layer]
                act.wait_ge(nsink_done, 1)
                for j in range(len(un) + 4):
                    if j >= 5 and j % 2 == 1:
                        pair = (j - 5) // 2
                        s, qi, t, _ = un[2 * pair]
                        c0 = SEQ * s + P * qi
                        act.wait_ge(o_mm, u0 + 2 * pair + 2)
                        act.activation(y_hi[:, 4 + t, c0:c0 + P], psB[pair % 2][:, 0:P], ACT.Copy)\
                            .then_inc(o_head, 1)
                    if 2 <= j < len(un) + 2:
                        width = (4 if un[j - 2][0] == 0 else 2) * P
                        act.wait_ge(t_mm, u0 + j - 1)
                        if j >= 4:
                            act.wait_ge(o_mm, u0 + j - 3)
                        act.activation(probT[:, j % 2, 0:width], psA[2 + j % 2][:, 0:width], ACT.Copy)\
                            .then_inc(pt, 1)
                    if j < len(un):
                        s, qi, t, half = un[j]
                        width = (4 if s == 0 else 2) * P
                        h = layer * N_HEADS + t + 4 * half
                        act.wait_ge(negm, 2 * (u0 + j + 1))
                        if j >= 3:
                            act.wait_ge(t_mm, u0 + j - 2)
                        act.activation(prob[j % 3][:, 0:width], score_bank[j % 3][:, 0:width], ACT.Exp,
                                       bias=small[:, j % 3, 1:2], scale=HEAD ** -0.5,
                                       accum_out=small[:, j % 3, 2:3]).then_inc(expd, 1)
                        act.activation(small[:, j % 3, 3:4], nsink[:, h:h + 1], ACT.Exp,
                                       bias=small[:, j % 3, 1:2], scale=-1.0).then_inc(expd, 1)


                def gate(name, b):
                    def step(st):
                        head(st, size(st, layer, name))
                        act.wait_ge(chunk_done, st.up(st.n + 1))
                        act.wait_ge(evac, st.up(st.n - (st.idx > 0)))
                        act.activation(sig[st.n % 2][:, 0:T], psA[st.slot][:, 0:T], ACT.Sigmoid).then_inc(sigd, 1)
                        if name == "fn" and st.idx in (2, 3):
                            c = st.idx - 2
                            act.wait_ge(sc_step, 12 * layer + 6 * (c + 1))
                            act.activation(y_hi[:, 2 + c, 0:T], pc[:, c, 0:T], ACT.Copy).then_inc(sc_head, 1)
                        if name == "cf" and st.i is None and st.idx > 0:
                            merged_head(st.idx - 1)
                    return step

                def merged_head(o):
                    act.wait_ge(m_sum, 24 * layer + 16 + o + 1)
                    act.activation(mg_hi[:, o, 0:T], branch_sum(layer, o), ACT.Copy).then_inc(m_head, 1)

                walk(act, layer, "fn", gate("fn", 0), keep=AHEAD)
                walk(act, layer, "sc", gate("sc", 1), keep=AHEAD)
                m0 = n0 + START["at"]
                for idx in range(LEN["at"]):
                    st = Step(m0 + idx, idx)
                    head(st, size(st, layer, "at"))
                    if idx % 3 < 2:
                        o = idx // 3 * 2 + idx % 3
                        act.wait_ge(chunk_done, st.n + 1)
                        act.wait_ge(evac, m0 if o < 2 else m0 + o // 2 * 3)
                        act.activation(sig[o % 2][:, 0:T], psA[st.slot][:, 0:T], ACT.Sigmoid).then_inc(sigd, 1)
                    if idx == 2:
                        for c, sq in enumerate((sqb, sqa)):
                            act.wait_ge(ln_xc, 2 * layer + c + 1)
                            act.activation(sq[:, 0:T], acc[:, c, 0:T], ACT.Square).then_inc(ln_sq, 1)
                    if idx == 7:
                        act.wait_ge(ln_var, layer + 1)
                        act.activation(sqb[:, 0:T], psB[(m0 + 3) % 4][:, 0:T], ACT.Sqrt, bias=V("eps", 0),
                                       scale=float(D // CONF_W)).then_inc(ln_root, 1)
                    if idx == 9:
                        for c in range(2):
                            act.wait_ge(ln_n, 2 * layer + c + 1)
                            act.activation(acc[:, c, 0:T], acc[:, c, 0:T], ACT.Silu, bias=V("ln_b", 2 * layer + c),
                                           scale=V("ln_g", 2 * layer + c)).then_inc(ln_silu, 1)
                        for c in range(2):
                            act.wait_ge(ln_silu, 2 * layer + c + 1)
                            act.activation(yc_hi[:, c, 0:T], acc[:, c, 0:T], ACT.Copy).then_inc(ln_head, 1)
                for idx in range(LEN["cf"]):
                    gate("cf", 3)(Step(n0 + START["cf"] + idx, idx))
                merged_head(KD - 1)

                def squares(name, r):
                    def step(st):
                        head(st, size(st, layer, name))
                        if st.idx:
                            square(8 * r + st.idx - 1, st.idx - 1, T, st.idx == 1, (evac, st.n))
                        if st.idx == KD - 1:
                            whole = (evac, st.n + 1)
                            last_squares(r, [whole] if T == SEQ else [(x_half, r), whole])
                    return step
                for idx in range(LEN["out"]):
                    squares("out", 2 * layer + 1)(Step(n0 + START["out"] + idx, idx))
                norm(layer, 1)

                for f in range(2):
                    p0 = HALF_FF * (2 * layer + f)

                    def hidden_head(n, pair, b):
                        act.wait_ge(evac, n)
                        dst = hid_hi[:, bass.ds(pair, 1), 0:T].rearrange("p a t -> p (a t)")
                        act.activation(dst, sig[b][:, 0:T], ACT.Copy).then_inc(hid_head, 1)

                    def lift(st):
                        head(st, size(st, layer, f"up{f}"))
                        pair, b = st.idx // 2, (st.idx // 2) % 2
                        if st.idx % 2 == 0:
                            if st.i is not None or st.idx:
                                hidden_head(st.up(st.n), st.up(pair - 1, 2), 1 - b)
                            act.wait_ge(chunk_done, st.up(st.n + 1))
                            act.wait_ge(evac, st.up(st.n - 2))
                            act.activation(tmp[b][:, 0:T], psA[st.slot][:, 0:T], ACT.Identity,
                                           bias=Vd("ffn_b", st.up(p0 + pair, 2)),
                                           scale=Vd("ffn_w", st.up(3 * (p0 + pair) + 1, 6))).then_inc(cv, 1)
                        else:
                            act.wait_ge(evac, st.up(st.n))
                            act.activation(tmp[b][:, 0:T], tmp[b][:, 0:T], ACT.Silu).then_inc(silu, 1)
                    walk(act, layer, f"up{f}", lift, skip=1 if layer else LEN["up0"], keep=AHEAD)
                    hidden_head(n0 + START[f"dn{f}"], HALF_FF - 1, (HALF_FF - 1) % 2)
                    if f == 0:
                        walk(act, layer, "dn0", lambda st: head(st, size(st, layer, "dn0")), keep=AHEAD)
                    else:
                        for idx in range(LEN["dn1"]):
                            squares("dn1", 2 * layer + 2)(Step(n0 + START["dn1"] + idx, idx))
            norm_root(2 * DEPTH)

        @block.vector
        def _(dve):
            def rest(st, tiles):
                if st.i is None and st.n + AHEAD >= TOTAL:
                    return
                s = (st.n + AHEAD) % SLOTS
                r, _ = st.filled("w", AHEAD)
                dve.wait_ge(head_done, st.up(st.n + AHEAD + 1))
                dve.tensor_tensor(w_lo[:, s, 0:tiles * P], raw[:, r, 0:tiles * P],
                                  w_hi[:, s, 0:tiles * P].bitcast(F32), ALU.subtract).then_inc(rest_done, 1)

            def size(st, name):
                return SIZE[START[name]] if st.i is not None else SIZE[(st.n + AHEAD) % PER_LAYER]

            def ada_step(a):
                p, g, kk = PLACE[("ada", a)], a // 8, a % 8
                dve.wait_ge(raw_full[p % SLOTS], 16 * (p // SLOTS + 1))
                if kk == 0 and g == 2:
                    dve.wait_ge(reduced, 2)
                elif kk == 0:
                    dve.wait_ge(folded, POS[g] - 2)
                else:
                    dve.wait_ge(ada_acc, ADA_STEPS[a] - ada_vectors(a))
                for vv in range(ada_vectors(a)):
                    w, dst, c = raw[:, p % SLOTS, 0:KD * P], ada_sum[:, vv, :], csil[:, kk, vv:vv + 1]
                    if kk == 0:
                        op = dve.tensor_scalar(dst, w, c, None, ALU.mult)
                    else:
                        op = dve.scalar_tensor_tensor(dst, w, c, dst, ALU.mult, ALU.add)
                    op.then_inc(ada_acc, 1)
                if kk == KD - 1:
                    dve.wait_ge(ada_acc, ADA_STEPS[a])
                    dve.wait_ge(reduced, POS[g])
                    for vv in range(ada_vectors(a)):
                        op = dve.tensor_reduce(ada_part[:, vv, :], ada_sum[:, vv, :].rearrange("p (b k) -> p b k", k=32),
                                               AX.X, ALU.add, apply_transpose=True)
                    op.then_inc(folded, 1)

            def read_mod(g, bank):
                dve.wait_ge(reduced, POS[g] + 1)
                layer, c0 = g // 6, KD * (g % 6)
                b = VEC["b_ada"] + KD * g
                vs = ada_vectors(8 * g)
                ps = bank[:, 0:2 * KD].rearrange("p (c v) -> p v c" if g < 2 else "p (v c) -> p v c", v=2)
                for vv in range(vs):
                    op = dve.tensor_tensor(mod[:, layer, c0:c0 + KD, vv], ps[:, vv, :], vec[:, b:b + KD], ALU.add)
                op.then_inc(mod_done, 1)
                if g % 6 in (1, 4):
                    dve.wait_ge(mod_done, POS[g] + 1)
                    which = g % 6 // 3
                    gv = VEC["g_mix" if which == 0 else "g_ffn"] + KD * layer
                    for vv in range(2):
                        if vv < vs:
                            op = dve.scalar_tensor_tensor(gsc[:, which, vv, :], mod[:, layer, c0:c0 + KD, vv],
                                                          1.0, vec[:, gv:gv + KD], ALU.add, ALU.mult)
                    op.then_inc(gsc_done, 1)

            def ada_behind(st):
                if st.i is None:
                    if st.n + 1 in REDUCE:
                        read_mod(REDUCE[st.n + 1], psB[(st.n + 1) % SLOTS])
                    if st.n in ADA_AT:
                        ada_step(ADA_AT[st.n])

            def add_square(count, T):
                r, o = divmod(count, 8)
                if 0 < o < 7:
                    dve.wait_ge(sq_done, 7 * r + o + 1)
                    if o > 1:
                        dve.wait_ge(sq_sum, 6 * r + o - 1)
                    dve.tensor_tensor(sqa[:, 0:T], sqa[:, 0:T], sqb[:, 0:T], ALU.add).then_inc(sq_sum, 1)

            def inverse_root(r, s):
                dve.wait_ge(root, normed(r, s))
                dve.reciprocal(root_col[:, 2 * s:2 * s + 2], root_col[:, 2 * s:2 * s + 2]).then_inc(inv_col, 1)
                dve.wait_ge(inv_col, normed(r, s))
                for b in range(2 * s, 2 * s + 2):
                    op = dve.tensor_scalar(sqb[:, b * P:(b + 1) * P], M("ident"), root_col[:, b:b + 1], float(D),
                                           ALU.mult, ALU.mult)
                op.then_inc(inv, 1)

            def query(st):
                T = SEQ * streams(st.n // PER_LAYER)
                dve.wait_ge(chunk_done, st.n + 1)
                dve.tensor_copy(q[:, st.idx, 0:T], psA[st.slot][:, 0:T]).then_inc(evac, 1)

            def norm(layer, which):
                r = 2 * layer + which
                if r:
                    inverse_root(r, 0)
                dve.wait_ge(gsc_done, r + 1)
                for s in range(norm_streams(r)):
                    h0 = 16 * r + KD * s
                    cols = slice(s * SEQ, (s + 1) * SEQ)
                    dve.wait_ge(spread, normed(r, s))
                    for kk in range(KD + 1):
                        if r == 2 and s == 1 and kk in SPLIT_IN_NORM:
                            if kk:
                                query(Step(PER_LAYER + SPLIT_IN_NORM[kk] - 1, SPLIT_IN_NORM[kk] - 1))
                            rest(Step(PER_LAYER + SPLIT_IN_NORM[kk], SPLIT_IN_NORM[kk]), SIZE[AHEAD])
                        if kk < KD:
                            if kk >= 2:
                                dve.wait_ge(h_rest, h0 + kk - 1)
                            dve.scalar_tensor_tensor(tmp[kk % 2][:, cols], X[:, kk, cols],
                                                     gsc[:, which, s, kk:kk + 1], spread_bank[s][:, cols],
                                                     ALU.mult, ALU.mult).then_inc(ht, 1)
                        if kk == 1 and s == 0:
                            if r == 0:
                                read_mod(ORDER[1], psB[1 + ORDER[1]])
                            if norm_streams(r) > 1:
                                inverse_root(r, 1)
                        if kk >= 1:
                            c = kk - 1
                            dve.wait_ge(h_head, h0 + c + 1)
                            dve.scalar_tensor_tensor(h_lo[:, c, cols], tmp[c % 2][:, cols],
                                                     mod[:, layer, 24 * which + c, s:s + 1],
                                                     h_hi[:, c, cols].bitcast(F32), ALU.add, ALU.subtract)\
                                .then_inc(h_rest, 1)

            dve.wait_ge(vecs_in, 16)
            dve.tensor_scalar(nsink[:, :], vec[:, VEC["sink"]:VEC["sink"] + DEPTH * N_HEADS], -1.0, None, ALU.mult)\
                .then_inc(nsink_done, 1)
            for kk in range(KD):
                add_square(kk, NT)
            inverse_root(0, 0)
            read_mod(ORDER[0], psB[1 + ORDER[0]])
            for ahead in range(AHEAD):
                dve.wait_ge(ada_pe, first_free(2 * SLOTS + ahead))
                if ahead == AHEAD - 1:
                    g = ORDER[1]
                    dve.wait_ge(ada_pe, ADA_A)
                    dve.tensor_copy(ada_sum[0:2, g, 512:1024], psA[2 * g + 1][0:2, :]).then_inc(ada_row, 1)
                rest(Step(ahead - AHEAD, 0), 8)

            for layer in range(DEPTH):
                n0 = layer * PER_LAYER
                S = streams(layer)
                T = SEQ * S
                norm(layer, 0)
                dve.wait_ge(pads, 2 * (layer + 1))
                for idx in range(LEN["in"]):
                    st = Step(n0 + idx, idx)
                    if not (layer and idx in SPLIT_IN_NORM.values()):
                        rest(st, size(st, "in"))
                    ps = psA[st.slot]
                    if idx < 4:
                        if not (layer and idx + 1 in SPLIT_IN_NORM.values()):
                            query(st)
                            ada_behind(st)
                        continue
                    if idx == 16:
                        for j in range(2 * S):
                            s, c = divmod(j, 2)
                            dve.wait_ge(fn_head, 4 * layer + j + 1)
                            dve.tensor_tensor(y_lo[:, c, s * SEQ:(s + 1) * SEQ], psB[j][:, 0:SEQ],
                                              y_hi[:, c, s * SEQ:(s + 1) * SEQ].bitcast(F32), ALU.subtract)\
                                .then_inc(fn_rest, 1)
                    if idx in (14, 16):
                        continue
                    dve.wait_ge(chunk_done, st.n + 1)
                    if idx == 4:
                        dve.tensor_copy(k[:, :], ps[:, :]).then_inc(evac, 1)
                    elif idx == 5:
                        dve.tensor_copy(sig[0][:, :], ps[:, :]).then_inc(evac, 1)
                    elif idx < 8:
                        dve.tensor_copy(f_in(layer, idx - 6), ps[:, 0:T]).then_inc(evac, 1)
                    elif idx in (8, 10):
                        dve.tensor_copy(pc[:, (idx - 8) // 2, 0:T], ps[:, 0:T]).then_inc(evac, 1)
                    elif idx in (9, 11):
                        c = (idx - 9) // 2
                        dve.wait_ge(evac, st.n)
                        dve.tensor_tensor(cx[:, c, 0:S, 1:1 + SEQ], both(ps[:, 0:T], T), both(pc[:, c, 0:T], T),
                                          ALU.mult).then_inc(evac, 1)
                    elif idx in (12, 13):
                        dve.tensor_copy(pb(layer, idx - 12), ps[:, 0:T]).then_inc(evac, 1)
                    else:
                        c = (idx - 15) // 2
                        dve.wait_ge(sigd, 34 * layer + c + 1)
                        dve.tensor_tensor(glu[:, c, 0:S, PAD:PAD + SEQ], both(ps[:, 0:T], T),
                                          both(sig[c][:, 0:T], T), ALU.mult).then_inc(evac, 2)
                    if idx == 8:
                        dve.wait_ge(v_mm, layer + 1)
                        dve.tensor_copy(v[:, :, :].rearrange("p b n -> p (b n)"), psB[2][:, :]).then_inc(v_done, 1)
                    if 6 <= idx < 11:
                        j = idx - 6
                        dst = q[:, j, 0:SEQ] if j < 4 else k[:, 0:SEQ]
                        r = 15 * layer + 3 * j
                        dve.wait_ge(rot, 5 * layer + j + 1)
                        if j >= 2:
                            dve.wait_ge(rope, r - 3)
                        dve.tensor_tensor(tmp[j % 2][:, 0:SEQ], psB[1 + 2 * (j % 2)][:, 0:SEQ], M("sin", SEQ),
                                          ALU.mult).then_inc(rope, 1)
                        dve.tensor_tensor(dst, dst, M("cos", SEQ), ALU.mult).then_inc(rope, 1)
                        dve.wait_ge(rope, r + 2)
                        dve.tensor_tensor(dst, dst, tmp[j % 2][:, 0:SEQ], ALU.add).then_inc(rope, 1)
                    ada_behind(st)

                def conv_tap(j):
                    w = V("conf_w", TAPS * layer + j)
                    src, dst = glu[:, 0, 0:S, j:j + SEQ], both(acc[:, 0, 0:T], T)
                    if j == 0:
                        op = dve.tensor_scalar(dst, src, w, V("conf_b", 2 * layer), ALU.mult, ALU.add)
                    else:
                        dve.wait_ge(tap, TAPS_V * layer + j)
                        op = dve.scalar_tensor_tensor(dst, src, w, dst, ALU.mult, ALU.add)
                    op.then_inc(tap, 1)

                un, u0 = units(layer), U0[layer]
                for j in range(len(un) + 4):
                    if j < len(un):
                        s, qi, t, half = un[j]
                        width = (4 if s == 0 else 2) * P
                        h = layer * N_HEADS + t + 4 * half
                        dve.wait_ge(s_mm, u0 + j + 1)
                        dve.tensor_reduce(small[:, j % 3, 0:1], score_bank[j % 3][:, 0:width], AX.X, ALU.max)\
                            .then_inc(negm, 1)
                    if 1 <= j <= len(un):
                        b = (j - 1) % 3
                        dve.wait_ge(expd, 2 * (u0 + j))
                        dve.tensor_tensor(small[:, b, 4:5], small[:, b, 2:3], small[:, b, 3:4], ALU.add)\
                            .then_inc(den, 1)
                    if j < len(un):
                        dve.wait_ge(negm, 2 * (u0 + j) + 1)
                        dve.tensor_scalar(small[:, j % 3, 1:2], small[:, j % 3, 0:1], -HEAD ** -0.5,
                                          nsink[:, h:h + 1], ALU.mult, ALU.min).then_inc(negm, 1)
                    if 1 <= j <= len(un):
                        width = (4 if un[j - 1][0] == 0 else 2) * P
                        dve.wait_ge(den, 2 * (u0 + j - 1) + 1)
                        dve.reciprocal(small[:, b, 4:5], small[:, b, 4:5]).then_inc(den, 1)
                        dve.wait_ge(den, 2 * (u0 + j))
                        dve.tensor_scalar(prob[b][:, 0:width], prob[b][:, 0:width], small[:, b, 4:5], None,
                                          ALU.mult).then_inc(pn, 1)
                    if j >= 5 and j % 2 == 1:
                        pair = (j - 5) // 2
                        s, qi, t, _ = un[2 * pair]
                        c0 = SEQ * s + P * qi
                        dve.wait_ge(o_head, u0 // 2 + pair + 1)
                        dve.tensor_tensor(y_lo[:, 4 + t, c0:c0 + P], psB[pair % 2][:, 0:P],
                                          y_hi[:, 4 + t, c0:c0 + P].bitcast(F32), ALU.subtract).then_inc(o_rest, 1)

                def dyn_sum(st_o):
                    c0 = 0 if layer == 0 else SEQ
                    if isinstance(st_o, int):
                        return X[:, st_o, c0:c0 + T]
                    return X[:, bass.ds(st_o, 1), c0:c0 + T].rearrange("p a t -> p (a t)")

                def branch(name, b):
                    def step(st):
                        rest(st, size(st, name))
                        if name == "cf" and st.idx > 0:
                            merged_rest(st.idx - 1)
                        o = st.up(st.idx)
                        dve.wait_ge(sigd, st.up(34 * layer + 2 + 8 * b + st.idx + 1))
                        dve.wait_ge(chunk_done, st.up(st.n + 1))
                        ps, sg = psB[st.slot][:, 0:T], sig[st.n % 2][:, 0:T]
                        if b == 0:
                            dve.tensor_tensor(dyn_sum(o), ps, sg, ALU.mult).then_inc(evac, 1)
                        else:
                            g = 8 * (b - 1) + st.idx
                            if g >= 2:
                                dve.wait_ge(m_sum, st.up(24 * layer + g - (st.idx > 0)))
                            t = tmp[st.n % 2][:, 0:T]
                            dve.tensor_tensor(t, ps, sg, ALU.mult).then_inc(evac, 1)
                        if name in ("fn", "sc"):
                            conv_tap(8 * (name == "sc") + st.idx)
                        if name == "fn" and st.idx in (3, 4):
                            c = st.idx - 3
                            dve.wait_ge(sc_head, 2 * layer + c + 1)
                            dve.tensor_tensor(y_lo[:, 2 + c, 0:T], pc[:, c, 0:T],
                                              y_hi[:, 2 + c, 0:T].bitcast(F32), ALU.subtract).then_inc(sc_rest, 1)
                        if layer == 0:
                            ada_behind(st)
                    return step

                def merged_rest(o):
                    dve.wait_ge(m_head, 8 * layer + o + 1)
                    dve.tensor_tensor(mg_lo[:, o, 0:T], branch_sum(layer, o), mg_hi[:, o, 0:T].bitcast(F32),
                                      ALU.subtract).then_inc(m_rest, 1)

                walk(dve, layer, "fn", branch("fn", 0), keep=AHEAD)
                walk(dve, layer, "sc", branch("sc", 1), keep=AHEAD)
                m0 = n0 + START["at"]
                for idx in range(LEN["at"]):
                    st = Step(m0 + idx, idx)
                    rest(st, size(st, "at"))
                    if idx == 2:
                        dve.wait_ge(ln_mean, layer + 1)
                        for c in range(2):
                            dve.scalar_tensor_tensor(acc[:, c, 0:T], psB[m0 % 4][:, 0:T], -float(D // CONF_W),
                                                     acc[:, c, 0:T], ALU.mult, ALU.add).then_inc(ln_xc, 1)
                    if idx % 3 == 2:
                        for half, ps in enumerate((psA, psB)):
                            o = idx // 3 * 2 + half
                            if half == 0:
                                dve.wait_ge(sigd, 34 * layer + 2 + 16 + o + 2)
                                dve.wait_ge(chunk_done, st.n + 1)
                                dve.wait_ge(m_sum, 24 * layer + 8 + o)
                            t = tmp[half][:, 0:T]
                            op = dve.tensor_tensor(t, ps[st.slot][:, 0:T], sig[half][:, 0:T], ALU.mult)
                        op.then_inc(evac, 3)
                    if layer == 0:
                        ada_behind(st)
                    if idx == 8:
                        dve.wait_ge(ln_root, layer + 1)
                        dve.reciprocal(sqb[:, 0:T], sqb[:, 0:T]).then_inc(ln_inv, 1)
                        dve.wait_ge(ln_inv, layer + 1)
                        for c in range(2):
                            dve.tensor_tensor(acc[:, c, 0:T], acc[:, c, 0:T], sqb[:, 0:T], ALU.mult)\
                                .then_inc(ln_n, 1)
                    if idx == 10:
                        for c in range(2):
                            dve.wait_ge(ln_head, 2 * layer + c + 1)
                            dve.tensor_tensor(yc_lo[:, c, 0:T], acc[:, c, 0:T], yc_hi[:, c, 0:T].bitcast(F32),
                                              ALU.subtract).then_inc(ln_rest, 1)
                for idx in range(LEN["cf"]):
                    branch("cf", 3)(Step(n0 + START["cf"] + idx, idx))
                merged_rest(KD - 1)

                def residual(name, which, r, ada_col):
                    def step(st):
                        rest(st, size(st, name))
                        if r is not None and st.idx > 0:
                            add_square(8 * r + st.idx - 1, T)
                        by_stream = r is not None and st.idx == KD - 1 and S == 2
                        if by_stream:
                            dve.wait_ge(half_done, r)
                        else:
                            dve.wait_ge(chunk_done, st.up(st.n + 1))
                        o = st.up(st.idx)
                        for s in range(S):
                            bank = psA[st.slot]
                            if by_stream and s == 1:
                                op.then_inc(x_half, 1)
                                dve.wait_ge(chunk_done, st.n + 1)
                                bank = psB[1]
                            cols = slice(s * SEQ, (s + 1) * SEQ)
                            old = x_in if layer == 0 and name == "out" else X
                            if st.i is None:
                                dst, src = X[:, st.idx, cols], old[:, st.idx, cols]
                                g = mod[:, layer, ada_col + st.idx, s:s + 1]
                            else:
                                dst = X[:, bass.ds(o, 1), cols].rearrange("p a t -> p (a t)")
                                src = dst
                                g = mod[:, layer, bass.ds(o + ada_col, 1), s:s + 1].rearrange("p a b -> p (a b)")
                            op = dve.scalar_tensor_tensor(dst, bank[:, cols], g, src, ALU.mult, ALU.add)
                        op.then_inc(evac, 1)
                        if layer == 0:
                            ada_behind(st)
                    return step

                if layer == 0:
                    dve.wait_ge(x_again, 16)
                for idx in range(LEN["out"]):
                    residual("out", 1, 2 * layer + 1, 16)(Step(n0 + START["out"] + idx, idx))
                add_square(8 * (2 * layer + 1) + 7, T)
                norm(layer, 1)

                for f in range(2):
                    p0 = HALF_FF * (2 * layer + f)

                    def lift(st):
                        rest(st, size(st, f"up{f}"))
                        pair, b = st.idx // 2, (st.idx // 2) % 2
                        ps = psA[st.slot][:, 0:T]
                        dve.wait_ge(chunk_done, st.up(st.n + 1))
                        if st.idx % 2 == 0:
                            w = 3 * p0 + 3 * pair
                            c0 = 2 * p0 + 2 * pair
                            t3, p3 = both(tmp[b][:, 0:T], T), both(ps, T)
                            dve.wait_ge(cv, st.up(c0 + 1, 4))
                            dve.scalar_tensor_tensor(t3[:, :, 1:SEQ], p3[:, :, 0:SEQ - 1], Vd("ffn_w", st.up(w, 6)),
                                                     t3[:, :, 1:SEQ], ALU.mult, ALU.add).then_inc(cv, 1)
                            dve.wait_ge(cv, st.up(c0 + 2, 4))
                            dve.scalar_tensor_tensor(t3[:, :, 0:SEQ - 1], p3[:, :, 1:SEQ],
                                                     Vd("ffn_w", st.up(w + 2, 6)), t3[:, :, 0:SEQ - 1],
                                                     ALU.mult, ALU.add).then_inc(evac, 1)
                        else:
                            dve.wait_ge(silu, st.up(p0 + pair + 1, 2))
                            if st.i is not None or pair >= 2:
                                dve.wait_ge(hid_rest, st.up(p0 + pair - 1, 2))
                            dve.tensor_tensor(sig[b][:, 0:T], ps, tmp[b][:, 0:T], ALU.mult).then_inc(evac, 1)
                        if layer == 0:
                            ada_behind(st)
                    walk(dve, layer, f"up{f}", lift, skip=1 if layer else LEN["up0"], keep=AHEAD)
                    name = f"dn{f}"
                    if f == 0:
                        walk(dve, layer, name, residual(name, 1, None, 40), keep=AHEAD)
                    else:
                        for idx in range(LEN[name]):
                            residual(name, 1, 2 * layer + 2, 40)(Step(n0 + START[name] + idx, idx))
                        add_square(8 * (2 * layer + 2) + 7, T)
            inverse_root(2 * DEPTH, 0)
            dve.wait_ge(spread, normed(2 * DEPTH, 0))
            for kk in range(KD):
                dve.scalar_tensor_tensor(y_out[:, kk, :], X[:, kk, 0:SEQ], V("g_final", kk), spread_bank[0][:, 0:SEQ],
                                         ALU.mult, ALU.mult).then_inc(fin, 1)


def constants():
    import numpy as np
    m = np.zeros((P, NMAT), np.float64)

    def put(name, a, off=0):
        m[:a.shape[0], MAT[name] + off:MAT[name] + off + a.shape[1]] = a
    put("ident", np.eye(P))
    put("mean", np.full((P, P), 1.0 / D))
    put("fold", np.tile(np.eye(32), (4, 1)))
    r = np.zeros((P, P))
    for g in range(P // 32):
        for j in range(16):
            a, b = 32 * g + j, 32 * g + 16 + j
            r[b, a] = -1.0
            r[a, b] = 1.0
    put("rot", r)
    i = np.arange(P)
    put("mask0", np.where(i[None, :] <= i[:, None], 0.0, -1e30))
    put("mask1", np.where(i[None, :] >= i[:, None], 0.0, -1e30))
    c = np.arange(64)
    ang = 2 * np.pi * np.outer(c, c) / 64
    put("chan", np.kron(np.eye(2), np.cos(ang)))
    put("chan", np.kron(np.eye(2), np.sin(ang)), 128)
    n = np.arange(SEQ)
    ang = 2 * np.pi * (np.outer(n, n) % SEQ) / SEQ
    scale = 1.0 / np.sqrt(SEQ * 64)
    for h in range(2):
        put("pos", np.cos(ang)[h * P:(h + 1) * P] * scale, 512 * h)
        put("pos", -np.sin(ang)[h * P:(h + 1) * P] * scale, 512 * h + 256)
    m = m.astype(np.float32)
    inv = np.float32(10000.0) ** (-np.arange(16, dtype=np.float32) / np.float32(16))
    pos = np.stack([n // 64, n % 64]).astype(np.float32)
    a = np.zeros((64, SEQ), np.float32)
    for axis in range(2):
        for half in range(2):
            a[axis * 32 + half * 16:axis * 32 + half * 16 + 16] = pos[axis][None, :] * inv[:, None]
    m[:, MAT["cos"]:MAT["cos"] + SEQ] = np.tile(np.cos(a), (2, 1))
    m[:, MAT["sin"]:MAT["sin"] + SEQ] = np.tile(np.sin(a), (2, 1))
    return m


def kernel(**inputs):
    import numpy as np
    import concourse.bacc as bacc
    from concourse.bass_utils import run_bass_kernel_spmd as run

    a = {name: np.asarray(x) for name, x in inputs.items()}

    def tiles(w):
        kk, mm = w.shape
        return w.reshape(kk // P, P, mm // P, P).transpose(2, 0, 1, 3)

    def chunks(t):
        n, c = t.shape[:2]
        return np.ascontiguousarray(t.transpose(0, 2, 1, 3).reshape(n, P, c * P))

    def channels(x):
        return x.T.reshape(-1, P, x.shape[0]).transpose(1, 0, 2)

    arrays = {"mat": constants()}
    heads = np.concatenate([np.arange(HEAD) + HEAD * h for t in range(4) for h in (t, t + 4)])
    arrays["x"] = np.ascontiguousarray(np.concatenate([channels(a["x"][0]), channels(a["ctx"][0])], axis=2))
    vec = np.zeros((P, NVEC), np.float32)

    def put(name, cols, off=0):
        vec[:, VEC[name] + off:VEC[name] + off + cols.shape[1]] = cols
    put("cc", np.stack([a["c"][0].reshape(KD, P), a["c_ctx"].reshape(KD, P)], 2).transpose(1, 0, 2).reshape(P, -1))
    put("b_ada", a["b_ada"].reshape(-1, P).T)
    put("g_mix", a["g_mix"].reshape(-1, P).T)
    put("g_ffn", a["g_ffn"].reshape(-1, P).T)
    put("g_final", a["g_final"].reshape(-1, P).T)
    put("sink", np.broadcast_to(a["attn_sink"].reshape(1, -1), (P, DEPTH * N_HEADS)))
    put("conf_w", a["conf_dw_w"].reshape(DEPTH, CONF_K, 2, P).transpose(3, 0, 2, 1).reshape(P, -1))
    put("conf_b", a["conf_dw_b"].reshape(-1, P).T)
    put("ln_g", a["conf_ln_g"].reshape(-1, P).T)
    put("ln_b", a["conf_ln_b"].reshape(-1, P).T)
    put("sc_w", a["sc_w"].reshape(DEPTH, SC_K, 2, P).transpose(3, 0, 2, 1).reshape(P, -1))
    put("ffn_w", a["ffn_dw_w"].reshape(DEPTH, 3, 2 * HALF_FF, P).transpose(3, 0, 2, 1).reshape(P, -1))
    put("ffn_b", a["ffn_dw_b"].reshape(-1, P).T)
    vec[:, VEC["eps"]] = EPS
    vec[:, VEC["one"]] = 1.0
    arrays["vec"] = vec
    arrays["w_ada"] = np.ascontiguousarray(a["w_ada"].reshape(DEPTH, KD, P, 6, D).transpose(0, 3, 1, 2, 4)
                                           .reshape(-1, P, D))
    for layer in range(DEPTH):
        w = a["w_in"][layer]
        at = np.cumsum([0, Q_W, KV_W, KV_W, 2 * CONF_W, SC_W, SC_W, SC_W, FN_W])
        wq, wk, wv, wcf, wb, wc, wx, wf = (tiles(w[:, s:e]) for s, e in zip(at[:-1], at[1:]))
        wq = tiles(w[:, heads])
        gates = tiles(w[:, at[-1]:]).reshape(4, KD, KD, P, P)
        arrays[f"w_in{layer}"] = chunks(np.concatenate(
            [wq, wk, wv, wf, wc[0:1], wx[0:1], wc[1:2], wx[1:2], wb, wcf[2:3], wcf[0:1], wcf[3:4], wcf[1:2]]))
        br = [tiles(a["w_br_attn"][layer][heads]), tiles(a["w_br_conf"][layer]), tiles(a["w_br_sconv"][layer]),
              tiles(a["w_br_fourier"][layer])]
        for name, b in (("fn", 3), ("sc", 2), ("cf", 1)):
            arrays[f"w_{name}{layer}"] = chunks(np.concatenate([gates[b], br[b]], axis=1))
        at_chunks = []
        for o in range(0, KD, 2):
            at_chunks += [gates[0][o], gates[0][o + 1], np.concatenate([br[0][o], br[0][o + 1]])]
        arrays[f"w_at{layer}"] = chunks(np.stack(at_chunks))
        arrays[f"w_out{layer}"] = chunks(tiles(a["w_out"][layer]))
        up = tiles(a["w_up"][layer]).reshape(2, 2, HALF_FF, KD, P, P)
        down = tiles(a["w_down"][layer])
        for f in range(2):
            arrays[f"w_up{f}{layer}"] = chunks(up[:, f].transpose(1, 0, 2, 3, 4).reshape(2 * HALF_FF, KD, P, P))
            arrays[f"w_dn{f}{layer}"] = chunks(down[:, f * HALF_FF:(f + 1) * HALF_FF])

    nc = bacc.Bacc("TRN2", target_bir_lowering=False, num_devices=1)
    io = {name: nc.dram_tensor(name, x.shape, F32, kind="ExternalInput").ap() for name, x in arrays.items()}
    io["out"] = nc.dram_tensor("out", (P, KD, SEQ), F32, kind="ExternalOutput").ap()
    program(nc, io)
    r = run(nc, [arrays], core_ids=[0])
    return np.ascontiguousarray(r.results[0]["out"].transpose(2, 1, 0).reshape(1, SEQ, D))
```
